# Optimizing a Trainium2 kernel written in Bass

```python
import jax
import jax.numpy as jnp
from jax import lax
import numpy as np

D_MODEL = 2048
BATCH = 1
SEQ = 256
DEPTH = 1

GRID_W = 64
CTX_LEN = 256
RWKV_HEADS = 16
RWKV_HEAD_DIM = 64
RWKV_WIDTH = RWKV_HEADS * RWKV_HEAD_DIM
DECAY_LORA = 96
ICL_LORA = 96
GATE_LORA = 64
RWKV_GN_EPS = 64e-5
GLA_HEADS = 4
GLA_KEY_DIM = 128
GLA_VAL_DIM = 256
GLA_QK_WIDTH = GLA_HEADS * GLA_KEY_DIM
GLA_V_WIDTH = GLA_HEADS * GLA_VAL_DIM
GLA_GATE_LORA = 16
GLA_TAU = 16.0
GLA_CHUNK = 64
GLA_NORM_EPS = 1e-5
D_FF_RAW = -(-8 * D_MODEL // 3)
D_FF = -(-D_FF_RAW // 256) * 256
NORM_EPS = 1e-6
RWKV_SPLITS = (RWKV_WIDTH, RWKV_WIDTH, RWKV_WIDTH, DECAY_LORA, DECAY_LORA, ICL_LORA, ICL_LORA, GATE_LORA)
GLA_SPLITS = (GLA_QK_WIDTH, GLA_QK_WIDTH, GLA_V_WIDTH, GLA_V_WIDTH, GLA_GATE_LORA, GLA_GATE_LORA)
RWKV_IN = sum(RWKV_SPLITS)
MIX_IN = RWKV_IN + sum(GLA_SPLITS)
N_IN = MIX_IN + 2 * D_MODEL

kernel_name = 'hybrid_rwkv7_gla_gated_dit_block'

def split_cols(p, sizes):
    return jnp.split(p, [int(i) for i in np.cumsum(sizes)[:-1]], axis=-1)

def rms_norm(x, g):
    xf = x.astype(jnp.float32)
    y = xf * lax.rsqrt(jnp.mean(xf * xf, axis=-1, keepdims=True) + NORM_EPS)
    return (y * g).astype(x.dtype)

def modulate(h, shift, scale):
    return h * (1.0 + scale) + shift

def centred_shift_mix(p, mu):
    prev = jnp.pad(p[:, :-1], ((0, 0), (1, 0), (0, 0)))
    nxt = jnp.pad(p[:, 1:], ((0, 0), (0, 1), (0, 0)))
    return p + mu * (0.5 * (prev + nxt) - p)

def to_col_major(t):
    b, n, ch = t.shape
    rows = n // GRID_W
    return t.reshape(b, rows, GRID_W, ch).swapaxes(1, 2).reshape(b, n, ch)

def from_col_major(t):
    b, n, ch = t.shape
    rows = n // GRID_W
    return t.reshape(b, GRID_W, rows, ch).swapaxes(1, 2).reshape(b, n, ch)

def rwkv7_scan(r, w, k, v, kk, a, s0, reverse, want_out):
    xs = tuple(jnp.moveaxis(t, 1, 0) for t in (w, k, v, kk, a))
    if want_out:
        xs = xs + (jnp.moveaxis(r, 1, 0),)

    def step(s, inp):
        w_t, k_t, v_t, kk_t, a_t = inp[:5]
        sa = jnp.einsum('bhvk,bhk->bhv', s, kk_t)
        s = (s * w_t[:, :, None, :] - sa[..., None] * (kk_t * a_t)[:, :, None, :]
             + v_t[..., None] * k_t[:, :, None, :])
        if not want_out:
            return s, None
        return s, jnp.einsum('bhvk,bhk->bhv', s, inp[5])

    s, ys = lax.scan(step, s0, xs, reverse=reverse)
    return s, (jnp.moveaxis(ys, 0, 1) if want_out else None)

def rwkv7_mixer(p, lp, s0_f, s0_b, want_out):
    bsz, n, _ = p.shape
    r, k, v, wd_f, wd_b, ad_f, ad_b, gd = split_cols(p, RWKV_SPLITS)

    def heads(t):
        return t.reshape(bsz, n, RWKV_HEADS, RWKV_HEAD_DIM)

    kk = heads((k * lp['rwkv_k_k']).astype(jnp.float32))
    kk = kk / jnp.maximum(jnp.linalg.norm(kk, axis=-1, keepdims=True), 1e-12)
    rh, vh = heads(r), heads(v)
    y_sum, bonus, states = 0.0, 0.0, []
    for d, (wd, ad, s0) in enumerate(((wd_f, ad_f, s0_f), (wd_b, ad_b, s0_b))):
        w_log = -jax.nn.softplus(-(lp['rwkv_w0'][d] + jnp.tanh(wd) @ lp['rwkv_w2'][d])) - 0.5
        decay = jnp.exp(-jnp.exp(w_log.astype(jnp.float32)))
        a = jax.nn.sigmoid(lp['rwkv_a0'][d] + ad @ lp['rwkv_a2'][d])
        kd = heads(k * (1.0 + (a - 1.0) * lp['rwkv_k_a']))
        s, y = rwkv7_scan(rh, heads(decay), kd, vh, kk, heads(a), s0, d == 1, want_out)
        states.append(s)
        if want_out:
            y_sum = y_sum + y
            bonus = bonus + jnp.sum(rh * kd * lp['rwkv_r_k'], axis=-1, keepdims=True) * vh
    if not want_out:
        return None, states[0], states[1]
    y_sum = y_sum.astype(jnp.float32)
    mean = jnp.mean(y_sum, axis=-1, keepdims=True)
    var = jnp.var(y_sum, axis=-1, keepdims=True)
    gn = ((y_sum - mean) * lax.rsqrt(var + RWKV_GN_EPS)).reshape(bsz, n, RWKV_WIDTH)
    gn = gn * lp['rwkv_ln_g'] + lp['rwkv_ln_b']
    g = jax.nn.sigmoid(gd) @ lp['rwkv_g2']
    return (gn + bonus.reshape(bsz, n, RWKV_WIDTH)) * g, states[0], states[1]

def gla_chunked(q, k, v, log_a, s0, want_out):
    bsz, n, h, _ = k.shape
    dv = v.shape[-1]
    nc = n // GLA_CHUNK

    def to_chunks(t):
        return jnp.moveaxis(t.reshape(bsz, nc, GLA_CHUNK, h, t.shape[-1]), 1, 0).swapaxes(2, 3)

    in_chunk = jnp.tril(jnp.ones((GLA_CHUNK, GLA_CHUNK), dtype=bool))[:, :, None]
    xs = (to_chunks(k), to_chunks(v), to_chunks(log_a))
    if want_out:
        xs = xs + (to_chunks(q),)

    def step(s, inp):
        k_c, v_c, la_c = inp[:3]
        b = jnp.cumsum(la_c.astype(jnp.float32), axis=2)
        b_end = b[:, :, -1:, :]
        s_next = (jnp.exp(b_end)[:, :, 0, :, None] * s
                  + jnp.einsum('bhsd,bhsv->bhdv', k_c * jnp.exp(b_end - b), v_c))
        if not want_out:
            return s_next, None
        q_c = inp[3]
        o_inter = jnp.einsum('bhtd,bhdv->bhtv', q_c * jnp.exp(b), s)
        diff = jnp.where(in_chunk, b[:, :, :, None, :] - b[:, :, None, :, :], -jnp.inf)
        att = jnp.einsum('bhtd,bhsd,bhtsd->bhts', q_c, k_c, jnp.exp(diff))
        return s_next, o_inter + jnp.einsum('bhts,bhsv->bhtv', att, v_c)

    s, o = lax.scan(step, s0, xs)
    if want_out:
        o = jnp.moveaxis(o.swapaxes(2, 3), 0, 1).reshape(bsz, n, h, dv)
    return s, o

def gla_mixer(p, lp, s0_f, s0_b, want_out):
    bsz, n, _ = p.shape
    q, k, v, g, ad_f, ad_b = split_cols(p, GLA_SPLITS)

    def heads(t):
        return t.reshape(bsz, n, GLA_HEADS, -1)

    q = heads(q) * GLA_KEY_DIM ** -0.5
    k, v = heads(k), heads(v)
    la = [heads(jax.nn.log_sigmoid((ad @ lp['gla_alpha_up'][d] + lp['gla_alpha_b'][d]).astype(jnp.float32)) / GLA_TAU)
          for d, ad in enumerate((ad_f, ad_b))]

    def flip(t):
        return jnp.flip(t, axis=1)

    s_f, o_f = gla_chunked(q, k, v, la[0], s0_f, want_out)
    s_b, o_b = gla_chunked(flip(q), flip(k), flip(v), flip(la[1]), s0_b, want_out)
    if not want_out:
        return None, s_f, s_b
    o = (o_f + flip(o_b)).astype(jnp.float32)
    o = o * lax.rsqrt(jnp.mean(o * o, axis=-1, keepdims=True) + GLA_NORM_EPS)
    o = o.reshape(bsz, n, GLA_V_WIDTH) * lp['gla_norm_g']
    return o * jax.nn.silu(g), s_f, s_b

def merge_branches(p_gate, y_a, y_b, lp):
    g_a, g_b = jnp.split(p_gate, 2, axis=-1)
    m = jax.nn.sigmoid(g_a) * (y_a @ lp['w_rwkv_up']) + jax.nn.sigmoid(g_b) * (y_b @ lp['w_gla_up'])
    return m @ lp['w_out']

def swiglu(h, lp):
    return (jax.nn.silu(h @ lp['ffn_w_gate']) * (h @ lp['ffn_w_up'])) @ lp['ffn_w_down']

def trunk_layer(x, ctx, c, c_ctx, lp, last):
    bsz = x.shape[0]
    mod_x = jax.nn.silu(c) @ lp['ada_w'] + lp['ada_b']
    mod_c = jax.nn.silu(c_ctx) @ lp['ada_w'] + lp['ada_b']
    shx1, scx1, gx1, shx2, scx2, gx2 = [t[:, None, :] for t in jnp.split(mod_x, 6, axis=-1)]
    shc1, scc1, gc1, shc2, scc2, gc2 = jnp.split(mod_c, 6, axis=-1)

    hx = modulate(rms_norm(x, lp['norm_pre_mix']), shx1, scx1)
    hc = modulate(rms_norm(ctx, lp['norm_pre_mix']), shc1, scc1)
    px = hx @ lp['w_in']
    pc = hc @ (lp['w_in'][:, :MIX_IN] if last else lp['w_in'])

    zero_r = jnp.zeros((bsz, RWKV_HEADS, RWKV_HEAD_DIM, RWKV_HEAD_DIM), jnp.float32)
    zero_g = jnp.zeros((bsz, GLA_HEADS, GLA_KEY_DIM, GLA_VAL_DIM), jnp.float32)

    yc_a, sr_f, sr_b = rwkv7_mixer(centred_shift_mix(pc[..., :RWKV_IN], lp['shift_mu']), lp, zero_r, zero_r, not last)
    yx_a, _, _ = rwkv7_mixer(centred_shift_mix(px[..., :RWKV_IN], lp['shift_mu']), lp, sr_f, sr_b, True)

    yc_b, sg_f, sg_b = gla_mixer(pc[..., RWKV_IN:MIX_IN], lp, zero_g, zero_g, not last)
    yx_b, _, _ = gla_mixer(to_col_major(px[..., RWKV_IN:MIX_IN]), lp, sg_f, sg_b, True)
    yx_b = from_col_major(yx_b)

    x = x + gx1 * rms_norm(merge_branches(px[..., MIX_IN:], yx_a, yx_b, lp), lp['norm_post_mix'])
    hx = modulate(rms_norm(x, lp['norm_pre_ffn']), shx2, scx2)
    x = x + gx2 * rms_norm(swiglu(hx, lp), lp['norm_post_ffn'])

    if not last:
        ctx = ctx + gc1 * rms_norm(merge_branches(pc[..., MIX_IN:], yc_a, yc_b, lp), lp['norm_post_mix'])
        hc = modulate(rms_norm(ctx, lp['norm_pre_ffn']), shc2, scc2)
        ctx = ctx + gc2 * rms_norm(swiglu(hc, lp), lp['norm_post_ffn'])
    return x, ctx

def setup_inputs(seed: int = 0) -> dict:
    key = jax.random.key(seed)
    ks = jax.random.split(key, 31)
    L, D, W = DEPTH, D_MODEL, RWKV_WIDTH

    def nrm(i, shape, std):
        return std * jax.random.normal(ks[i], shape, jnp.float32)

    def uni(i, shape, lo, hi):
        return jax.random.uniform(ks[i], shape, jnp.float32, lo, hi)

    return {
        'x': nrm(0, (BATCH, SEQ, D), 1.0),
        'c': nrm(1, (BATCH, D), 1.0),
        'ctx': nrm(2, (BATCH, CTX_LEN, D), 1.0),
        'c_ctx': nrm(3, (D,), 1.0),
        'ada_w': nrm(4, (L, D, 6 * D), 0.5 * D ** -0.5),
        'ada_b': nrm(5, (L, 6 * D), 0.02),
        'norm_pre_mix': 1.0 + nrm(6, (L, D), 0.05),
        'norm_post_mix': 1.0 + nrm(7, (L, D), 0.05),
        'norm_pre_ffn': 1.0 + nrm(8, (L, D), 0.05),
        'norm_post_ffn': 1.0 + nrm(9, (L, D), 0.05),
        'w_in': nrm(10, (L, D, N_IN), D ** -0.5),
        'shift_mu': uni(11, (L, RWKV_IN), 0.0, 1.0),
        'rwkv_w0': uni(12, (L, 2, W), -6.0, -1.0),
        'rwkv_w2': nrm(13, (L, 2, DECAY_LORA, W), 0.5 * DECAY_LORA ** -0.5),
        'rwkv_a0': nrm(14, (L, 2, W), 0.1),
        'rwkv_a2': nrm(15, (L, 2, ICL_LORA, W), ICL_LORA ** -0.5),
        'rwkv_g2': nrm(16, (L, GATE_LORA, W), GATE_LORA ** -0.5),
        'rwkv_k_k': 0.85 + nrm(17, (L, W), 0.05),
        'rwkv_k_a': 1.0 + nrm(18, (L, W), 0.05),
        'rwkv_r_k': nrm(19, (L, RWKV_HEADS, RWKV_HEAD_DIM), 0.1),
        'rwkv_ln_g': 1.0 + nrm(20, (L, W), 0.1),
        'rwkv_ln_b': nrm(21, (L, W), 0.02),
        'w_rwkv_up': nrm(22, (L, W, D), W ** -0.5),
        'gla_alpha_up': nrm(23, (L, 2, GLA_GATE_LORA, GLA_QK_WIDTH), 0.5 * GLA_GATE_LORA ** -0.5),
        'gla_alpha_b': uni(24, (L, 2, GLA_QK_WIDTH), 0.0, 4.0),
        'gla_norm_g': 1.0 + nrm(25, (L, GLA_V_WIDTH), 0.1),
        'w_gla_up': nrm(26, (L, GLA_V_WIDTH, D), GLA_V_WIDTH ** -0.5),
        'w_out': nrm(27, (L, D, D), D ** -0.5),
        'ffn_w_gate': nrm(28, (L, D, D_FF), D ** -0.5),
        'ffn_w_up': nrm(29, (L, D, D_FF), D ** -0.5),
        'ffn_w_down': nrm(30, (L, D_FF, D), D_FF ** -0.5),
    }

def reference(x, c, ctx, c_ctx, ada_w, ada_b, norm_pre_mix, norm_post_mix, norm_pre_ffn, norm_post_ffn,
              w_in, shift_mu, rwkv_w0, rwkv_w2, rwkv_a0, rwkv_a2, rwkv_g2, rwkv_k_k, rwkv_k_a, rwkv_r_k,
              rwkv_ln_g, rwkv_ln_b, w_rwkv_up, gla_alpha_up, gla_alpha_b, gla_norm_g, w_gla_up, w_out,
              ffn_w_gate, ffn_w_up, ffn_w_down):
    for i in range(DEPTH):
        lp = {
            'ada_w': ada_w[i], 'ada_b': ada_b[i],
            'norm_pre_mix': norm_pre_mix[i], 'norm_post_mix': norm_post_mix[i],
            'norm_pre_ffn': norm_pre_ffn[i], 'norm_post_ffn': norm_post_ffn[i],
            'w_in': w_in[i], 'shift_mu': shift_mu[i],
            'rwkv_w0': rwkv_w0[i], 'rwkv_w2': rwkv_w2[i], 'rwkv_a0': rwkv_a0[i], 'rwkv_a2': rwkv_a2[i],
            'rwkv_g2': rwkv_g2[i], 'rwkv_k_k': rwkv_k_k[i], 'rwkv_k_a': rwkv_k_a[i], 'rwkv_r_k': rwkv_r_k[i],
            'rwkv_ln_g': rwkv_ln_g[i], 'rwkv_ln_b': rwkv_ln_b[i], 'w_rwkv_up': w_rwkv_up[i],
            'gla_alpha_up': gla_alpha_up[i], 'gla_alpha_b': gla_alpha_b[i], 'gla_norm_g': gla_norm_g[i],
            'w_gla_up': w_gla_up[i], 'w_out': w_out[i],
            'ffn_w_gate': ffn_w_gate[i], 'ffn_w_up': ffn_w_up[i], 'ffn_w_down': ffn_w_down[i],
        }
        x, ctx = trunk_layer(x, ctx, c, c_ctx, lp, i == DEPTH - 1)
    return x


_drawn_inputs = setup_inputs


def setup_inputs(seed=0):
    import zlib

    import numpy as np

    out = dict(_drawn_inputs(seed))
    spreads = {}
    factors = {'norm_post_mix': 3.478,
     'norm_pre_ffn': 2.846,
     'norm_post_ffn': 3.782,
     'rwkv_w2': 6.865,
     'rwkv_a0': 7.985,
     'rwkv_k_k': 3.161,
     'rwkv_k_a': 2.995,
     'rwkv_ln_g': 3.288,
     'rwkv_ln_b': 8.0,
     'gla_alpha_up': 3.468}
    for name, (base, spread) in spreads.items():
        noise = np.random.default_rng([zlib.crc32(name.encode()), seed]).standard_normal(out[name].shape)
        drawn = base * np.exp(spread * noise) if base else spread * noise
        out[name] = jnp.asarray(drawn.astype(out[name].dtype))
    for name, factor in factors.items():
        out[name] = (out[name] * factor).astype(out[name].dtype)
    return out
```

```python
import math
from contextlib import ExitStack

import concourse.bass as bass
from concourse import mybir

D = 2048
SEQ = 256
CTX = 256
GRID_W = 64
GRID_H = SEQ // GRID_W
RH, RD = 16, 64
RW = RH * RD
LORA = 96
GLORA = 64
GH, GK, GV = 4, 128, 256
GQW, GVW = GH * GK, GH * GV
GLR = 16
FF = 5632
P = 128
KT = D // P
TOK = CTX + SEQ
RWKV_IN = 3 * RW + 4 * LORA + GLORA
MIX_IN = RWKV_IN + 2 * GQW + 2 * GVW + 2 * GLR
PAIRS = RW // P
C = 64
NCH = TOK // C
NORM_EPS = 1e-6
GN_EPS = 64e-5
GLA_EPS = 1e-5
GLA_TAU = 16.0
DECAY_TOP = math.exp(-0.5)
REF = DECAY_TOP * C / 2

f32 = mybir.dt.float32
f32r = mybir.dt.float32r
ALU = mybir.AluOpType
ACT = mybir.ActivationFunctionType

PARAM_ROWS = [("norm_pre_mix", KT), ("norm_post_mix", KT), ("norm_pre_ffn", KT), ("norm_post_ffn", KT),
              ("ada_b", 6 * KT), ("c", KT), ("c_ctx", KT), ("mu", 3 * PAIRS), ("mu_lora", 5),
              ("rwkv_w0", 2 * PAIRS), ("rwkv_a0", 2 * PAIRS), ("rwkv_k_k", PAIRS), ("rwkv_k_a", PAIRS),
              ("rwkv_r_k", PAIRS), ("rwkv_ln_g", PAIRS), ("rwkv_ln_b", PAIRS), ("gla_alpha_b", 2 * GH),
              ("gla_norm_g", 2 * GH)]
COL, _n = {}, 0
for _name, _rows in PARAM_ROWS:
    COL[_name] = _n
    _n += _rows
PROWS = -(-_n // P)

T_R, T_K, T_V, T_GQ, T_GK, T_GV, T_GG, T_GATE = 0, 8, 16, 24, 28, 32, 40, 48
T_LORA = 80
N_PX = 86
LORA_COLS = [3 * RW + LORA * n for n in range(5)] + [RWKV_IN + 2 * GQW + 2 * GVW]

RAW = 4
TILE = 2048
KH = 8


def b32(ap):
    return ap.bitcast(f32)


def hybrid_block(nc, A, out, stop=99, first=0):
    top = ExitStack()

    def dram(name, shape):
        return nc.dram_tensor(name, shape, f32, kind="Internal").ap()

    live = []

    def sem(name):
        live.append(nc.alloc_semaphore(name=name))
        return live[-1]

    def end_phase():
        nums = sorted(s.num for s in live)
        with nc.Block() as block:
            @block.sync
            def _(sp):
                at = 0
                while at < len(nums):
                    n = at
                    while n + 1 < len(nums) and nums[n + 1] == nums[n] + 1:
                        n += 1
                    sp.sem_clear(range(nums[at], nums[n] + 1))
                    at = n + 1
        for s in live:
            nc.release_semaphore(s)
        live.clear()

    px = dram("px_scratch", (N_PX, P, TOK))
    xfm_d = dram("xfm_scratch", (P, KT, SEQ))
    shared_d = dram("rwkv_kk_v_scratch", (P, 2 * PAIRS, TOK))
    r_d = dram("rwkv_r_scratch", (P, PAIRS, SEQ))
    dir_d = dram("rwkv_dir_scratch", (2, P, 3 * PAIRS, TOK))
    y_d = dram("rwkv_y_scratch", (P, PAIRS, SEQ))
    yb_d = dram("gla_y_scratch", (P, GVW // P, SEQ))
    x1_d = dram("x1_scratch", (P, KT, SEQ))
    yo_d = dram("ffn_y_scratch", (P, KT, SEQ))
    post_d = dram("rwkv_post_scratch", (P, 2 * PAIRS, SEQ))

    def alloc(stack, name, shape, dt=f32):
        return stack.enter_context(nc.sbuf_tensor(name, shape, dt))

    def psum(stack, name, cols):
        cols = -(-cols // 512) * 512
        return stack.enter_context(nc.psum_tensor(name, [P, cols], f32))

    with top:
        ident = alloc(top, "ident", [P, P])
        ones = alloc(top, "ones", [P, P])
        head_ones = alloc(top, "head_ones", [P, P])
        prm = alloc(top, "prm", [P, PROWS * P])
        modv = alloc(top, "modv", [P, 6 * KT, 2])
        one_minus_mu = alloc(top, "one_minus_mu", [P, 29])
        half_mu = alloc(top, "half_mu", [P, 29])
        one_minus_ka = alloc(top, "one_minus_ka", [P, PAIRS])

        def col(name, n=0, w=1):
            return prm[:, COL[name] + n:COL[name] + n + w]

        class Ring:
            def __init__(self, stack, tag, raw=RAW, split=RAW, width=TILE, parts=(None, None)):
                self.R, self.S = raw, split
                self.raw = alloc(stack, f"{tag}_w_raw", [P, raw, width])
                self.hi, self.lo = [given if given is not None else
                                    alloc(stack, f"{tag}_w_{n}", [P, split, width], f32r)
                                    for n, given in zip(("hi", "lo"), parts)]
                self.landed = [sem(f"{tag}_w_landed{n}") for n in range(raw)]
                self.hi_done = sem(f"{tag}_w_hi_done")
                self.lo_even = sem(f"{tag}_w_lo_even_done")
                self.lo_odd = sem(f"{tag}_w_lo_odd_done")
                self.used = sem(f"{tag}_w_used")

            def load(self, eng, src, m, t, shape):
                s = m % self.R
                if not (isinstance(t, int) and t < self.R):
                    lo = self.lo_odd if m % 2 else self.lo_even
                    eng.wait_ge(lo, halves(t, 1 - self.R // 2))
                w = shape[0] * shape[1]
                eng.dma_start(self.raw[:, s, 0:w].rearrange("p (k n) -> p k n", k=shape[0]), src)\
                   .then_inc(self.landed[s], 16)

            def split_hi(self, act, m, t, w=TILE):
                s = m % self.R
                act.wait_ge(self.landed[s], landings(t))
                if not (isinstance(t, int) and t < self.S):
                    act.wait_ge(self.used, t - self.S + 1)
                act.activation(self.hi[:, m % self.S, 0:w], self.raw[:, s, 0:w], ACT.Copy)\
                   .then_inc(self.hi_done, 1)

            def split_lo(self, eng, m, t, w=TILE):
                s = m % self.R
                eng.wait_ge(self.hi_done, t + 1)
                eng.tensor_tensor(self.lo[:, m % self.S, 0:w], self.raw[:, s, 0:w],
                                  b32(self.hi[:, m % self.S, 0:w]), ALU.subtract)\
                   .then_inc(self.lo_odd if m % 2 else self.lo_even, 1)

            def wait_split(self, pe, m, t):
                pe.wait_ge(self.lo_odd if m % 2 else self.lo_even, halves(t, 1))

        class Tile:
            def __init__(self, i, per, const):
                self.i, self.per, self.const = i, per, const

            def __sub__(self, n):
                return self.i * self.per + (self.const - n)

            def __add__(self, n):
                return self.i * self.per + (self.const + n)

        def halves(t, n):
            return t // 2 + n if isinstance(t, int) else t.i * (t.per // 2) + (t.const // 2 + n)

        def landings(t):
            return 16 * (t // RAW + 1) if isinstance(t, int) else t.i * (16 * t.per // RAW) + 16 * (t.const // RAW + 1)

        def tile_no(i, per, const):
            return i * per + const if isinstance(i, int) else Tile(i, per, const)

        def bodies(eng, n, body, peel):
            first = 1 if peel else 0
            if peel:
                body(0)
            if n - first == 1:
                body(first)
            elif n > first:
                with eng.Fori(first, n) as i:
                    body(i)

        def mm3(pe, o, wh, wl, xh, xl, first, last):
            pe.matmul(o, wh, xh, start=first, stop=False)
            pe.matmul(o, wh, xl, start=False, stop=False)
            return pe.matmul(o, wl, xh, start=False, stop=last)

        with ExitStack() as ph_h:
            h_hi = alloc(ph_h, "h_hi", [P, KT, TOK], f32r)
            h_lo = alloc(ph_h, "h_lo", [P, KT, TOK], f32r)
            if first <= 0:
                phase_inputs(nc, A, locals())
                end_phase()
            if first <= 1 and stop >= 1:
                phase_w_in(nc, A, locals())
                end_phase()
        if stop >= 2:
            for ph in (phase_gla, phase_rwkv_pre, phase_rwkv_scan, phase_tail)[max(first - 2, 0):stop - 1]:
                ph(nc, A, out, locals())
                end_phase()


def phase_inputs(nc, A, env):
    alloc, psum, sem, Ring, col = (env[k] for k in ("alloc", "psum", "sem", "Ring", "col"))
    ident, ones, head_ones, prm, modv = (env[k] for k in ("ident", "ones", "head_ones", "prm", "modv"))
    h_hi, h_lo, xfm_d = env["h_hi"], env["h_lo"], env["xfm_d"]
    one_minus_mu, half_mu, one_minus_ka = env["one_minus_mu"], env["half_mu"], env["one_minus_ka"]
    tile_no, bodies = env["tile_no"], env["bodies"]

    vectors = {n: A[n].rearrange("a (r p) -> (a r) p", p=P) for n in
               ("norm_pre_mix", "norm_post_mix", "norm_pre_ffn", "norm_post_ffn", "ada_b", "c",
                "rwkv_k_k", "rwkv_k_a", "rwkv_ln_g", "rwkv_ln_b", "gla_norm_g")}
    vectors["c_ctx"] = A["c_ctx"].rearrange("(r p) -> r p", p=P)
    vectors["mu"] = A["shift_mu"][:, 0:3 * RW].rearrange("a (r p) -> (a r) p", p=P)
    for n in ("rwkv_w0", "rwkv_a0", "gla_alpha_b"):
        vectors[n] = A[n].rearrange("a d (r p) -> (a d r) p", p=P)
    vectors["rwkv_r_k"] = A["rwkv_r_k"].rearrange("a (r h) k -> (a r) (h k)", h=2)
    pieces = []
    for name, rows in PARAM_ROWS:
        if name == "mu_lora":
            for n in range(5):
                w = LORA if n < 4 else GLORA
                q = COL[name] + n
                pieces.append((q // P, q % P, 1, w, A["shift_mu"][:, LORA_COLS[n]:LORA_COLS[n] + w]))
            continue
        q, at = COL[name], 0
        while at < rows:
            take = min(rows - at, P - (q + at) % P)
            pieces.append(((q + at) // P, (q + at) % P, take, P, vectors[name][at:at + take, :]))
            at += take

    s_const = sem("i_constants_made")
    s_prow = sem("i_param_rows_landed")
    s_prmT = sem("i_params_transposed")
    s_prm = sem("i_params_ready")
    s_xt = [sem(f"i_tokens_landed{n}") for n in range(2)]
    s_xT = sem("i_tokens_transposed")
    s_fm = sem("i_tokens_evacuated")
    s_sq = sem("i_squares_ready")
    s_ss = sem("i_square_sums_added")
    s_ssall = sem("i_square_sums_ready")
    s_std = sem("i_std_ready")
    s_nrm = sem("i_normalised")
    s_xst = sem("i_x_stored")
    s_sig = sem("i_c_sigmoid")
    s_sc = sem("i_c_silu")
    s_chi = sem("i_c_hi")
    s_clo = sem("i_c_split")
    s_rowc = sem("i_ada_row_copied")
    s_modp = sem("i_ada_columns_made")
    s_modc = sem("i_ada_columns_copied")
    s_mod = sem("i_modulation_ready")
    s_v = sem("i_vector_step")
    s_h = sem("i_h_ready")
    s_hh = sem("i_h_hi_ready")
    s_hl = sem("i_h_lo_ready")
    ada = A["ada_w"].rearrange("a (k p) n -> p (a k) n", p=P)
    CW = 512
    NB = 6 * D // CW // 2

    with ExitStack() as st:
        ring = Ring(st, "i", parts=[h[:].rearrange("p k t -> p (k t)").rearrange("p (s n) -> p s n", s=RAW)
                                    for h in (h_hi, h_lo)])
        prow = alloc(st, "prow", [P, PROWS, P])
        xt = alloc(st, "xt", [P, 2, D])
        fm = alloc(st, "fm", [P, KT, TOK])
        c_split = alloc(st, "c_split", [P, KT, P], f32r)
        sigc = alloc(st, "sigc", [P, 2 * KT])
        siluc = alloc(st, "siluc", [P, 2, KT])
        sel = alloc(st, "sel", [4, 2])
        sq = alloc(st, "sq", [P, 2, TOK])
        rstd = alloc(st, "rstd", [P, TOK])
        hbuf = alloc(st, "hbuf", [P, 2, TOK])
        rows = alloc(st, "ada_rows", [4, 2, CW])
        gain = alloc(st, "gain", [P, KT, 2])
        p_row = [psum(st, f"p_row{n}", CW) for n in range(2)]
        p_col = psum(st, "p_col", 512)
        p_xT = [psum(st, f"p_xT{n}", TOK) for n in range(2)]
        p_ss = psum(st, "p_ss", TOK)
        tokens = [A["ctx"][0, 0:P, :], A["ctx"][0, P:2 * P, :], A["x"][0, 0:P, :], A["x"][0, P:2 * P, :]]

        with nc.Block() as block:

            @block.gpsimd
            def _(pool):
                made = [0]

                def make(ins):
                    made[0] += 1
                    ins.then_inc(s_const, 1)
                    pool.wait_ge(s_const, made[0])
                make(pool.memset(prow[:], 0.0))
                make(pool.memset(ident[:], 0.0))
                make(pool.affine_select(out=ident[:], in_=ident[:], compare_op=ALU.not_equal, fill=1.0, base=0,
                                        pattern=[[-1, P]], channel_multiplier=1))
                make(pool.memset(ones[:], 1.0))
                make(pool.memset(head_ones[:], 0.0))
                for b in (0, 64):
                    make(pool.memset(head_ones[b:b + 64, b:b + 64], 1.0))
                make(pool.memset(b32(c_split[:]), 0.0))
                make(pool.memset(sel[:], 0.0))
                for base in (0, -2):
                    make(pool.affine_select(out=sel[:], in_=sel[:], compare_op=ALU.not_equal, fill=1.0, base=base,
                                            pattern=[[-1, 2]], channel_multiplier=1))

                def body(i):
                    for m in range(1, 8, 2):
                        ring.split_lo(pool, m, tile_no(i, 8, m))
                bodies(pool, NB, body, False)

            @block.sync
            def _(sp):
                for n in range(2):
                    sp.dma_start(xt[:, n, :], tokens[n]).then_inc(s_xt[n], 16)
                sp.wait_ge(s_const, 1)
                for tile, row, n, w, src in pieces:
                    sp.dma_start(prow[row:row + n, tile, 0:w], src).then_inc(s_prow, 16)

                def body(i):
                    for m in range(8):
                        src = ada[:, 4 * (m % 4):4 * (m % 4) + 4, bass.ds((i * 2 + m // 4) * CW, CW)]
                        ring.load(sp, src, m, tile_no(i, 8, m), (4, CW))
                        if isinstance(i, int) and i == 0 and m == 3:
                            for n in range(2, 4):
                                sp.wait_ge(s_xT, 4 * (n - 1))
                                sp.dma_start(xt[:, n % 2, :], tokens[n]).then_inc(s_xt[n % 2], 16)
                bodies(sp, NB, body, True)
                sp.wait_ge(s_fm, 4 * 4)
                sp.dma_start(xfm_d, fm[:, :, CTX:]).then_inc(s_xst, 16)
                sp.wait_ge(s_xst, 16)

            @block.tensor
            def _(pe):
                pe.wait_ge(s_const, 11)
                for n in range(4):
                    pe.wait_ge(s_xt[n % 2], 16 * (n // 2 + 1))
                    for g in range(4):
                        b = 4 * n + g
                        if b >= 2:
                            pe.wait_ge(s_fm, b - 1)
                        for f in range(4):
                            last = pe.transpose(p_xT[b % 2][:, f * P:(f + 1) * P],
                                                xt[:, n % 2, (4 * g + f) * P:(4 * g + f + 1) * P], ident[:])
                        last.then_inc(s_xT, 1)
                    if n == 1:
                        pe.wait_ge(s_prow, 16 * len(pieces))
                        for r in range(PROWS):
                            last = pe.transpose(p_col[:, r * P:(r + 1) * P], prow[:, r, :], ident[:])
                        last.then_inc(s_prmT, 1)
                for k in range(KT):
                    pe.wait_ge(s_sq, k + 1)
                    last = pe.matmul(p_ss[:], ones[:], sq[:, k % 2, :], start=k == 0, stop=k == KT - 1)
                    last.then_inc(s_ss, 1)
                pe.wait_ge(s_clo, 1)

                def columns(r, h):
                    pe.wait_ge(s_rowc, r + 1)
                    if isinstance(r, int) and r == 0:
                        pe.wait_ge(s_prm, 1)
                    else:
                        pe.wait_ge(s_modc, r)
                    for f in range(4):
                        last = pe.matmul(p_col[:, 2 * f:2 * f + 2], rows[:, h, f * P:(f + 1) * P], sel[:],
                                         start=True, stop=True)
                    last.then_inc(s_modp, 1)

                def body(i):
                    for h in range(2):
                        for q in range(4):
                            m = 4 * h + q
                            if q == 2 and not (isinstance(i, int) and i == 0 and h == 0):
                                columns(i * 2 + (h - 1), 1 - h)
                            ring.wait_split(pe, m, tile_no(i, 8, m))
                            for part in (ring.hi, ring.lo):
                                for k in range(4):
                                    last = pe.matmul(p_row[h][:], c_split[:, 4 * q + k, :],
                                                     part[:, m % ring.S, k * CW:(k + 1) * CW],
                                                     start=q == 0 and k == 0 and part is ring.hi,
                                                     stop=q == 3 and k == 3 and part is ring.lo)
                            last.then_inc(ring.used, 1)
                bodies(pe, NB, body, True)
                columns(2 * NB - 1, 1)

            @block.scalar
            def _(act):
                act.wait_ge(s_prm, 1)
                act.activation(sigc[:], prm[:, COL["c"]:COL["c"] + 2 * KT], ACT.Sigmoid).then_inc(s_sig, 1)
                act.wait_ge(s_sc, 1)
                act.activation(c_split[:, :, 0:2].rearrange("p k v -> p v k"), siluc[:], ACT.Copy)\
                   .then_inc(s_chi, 1)
                for m in range(2):
                    ring.split_hi(act, m, m)
                act.wait_ge(s_fm, 16)
                for k in range(KT):
                    if k >= 2:
                        act.wait_ge(s_ss, k - 1)
                    act.activation(sq[:, k % 2, :], fm[:, k, :], ACT.Square).then_inc(s_sq, 1)
                act.wait_ge(s_ssall, 1)
                act.activation(rstd[:], sq[:, 0, :], ACT.Sqrt).then_inc(s_std, 1)

                def body(i):
                    for m in range(8):
                        if isinstance(i, int) and i == 0 and m < 2:
                            continue
                        ring.split_hi(act, m, tile_no(i, 8, m))
                bodies(act, NB, body, True)
                for k in range(KT):
                    act.wait_ge(s_h, k + 1)
                    act.activation(h_hi[:, k, :], hbuf[:, k % 2, :], ACT.Copy).then_inc(s_hh, 1)

            @block.vector
            def _(dve):
                step = [0]

                def done(ins):
                    step[0] += 1
                    ins.then_inc(s_v, 1)
                    dve.wait_ge(s_v, step[0])

                def evac(b):
                    dve.wait_ge(s_xT, b + 1)
                    dve.tensor_copy(fm[:, 4 * (b % 4):4 * (b % 4) + 4, (b // 4) * P:(b // 4 + 1) * P],
                                    p_xT[b % 2][:].rearrange("p (f t) -> p f t", f=4)).then_inc(s_fm, 1)
                for b in range(8):
                    evac(b)
                dve.wait_ge(s_prmT, 1)
                dve.tensor_copy(prm[:], p_col[:, 0:PROWS * P]).then_inc(s_prm, 1)
                dve.wait_ge(s_prm, 1)
                mu = prm[:, COL["mu"]:COL["mu"] + 29]
                dve.tensor_scalar(one_minus_mu[:], mu, -1.0, 1.0, ALU.mult, ALU.add)
                dve.tensor_scalar(half_mu[:], mu, 0.5, None, ALU.mult)
                dve.tensor_scalar(one_minus_ka[:], col("rwkv_k_a", 0, PAIRS), -1.0, 1.0, ALU.mult, ALU.add)
                dve.wait_ge(s_sig, 1)
                dve.tensor_tensor(siluc[:].rearrange("p v k -> p (v k)"), prm[:, COL["c"]:COL["c"] + 2 * KT],
                                  sigc[:], ALU.mult).then_inc(s_sc, 1)
                dve.wait_ge(s_chi, 1)
                dve.tensor_tensor(c_split[:, :, 2:4].rearrange("p k v -> p v k"), siluc[:],
                                  b32(c_split[:, :, 0:2]).rearrange("p k v -> p v k"), ALU.subtract)\
                   .then_inc(s_clo, 1)
                for b in range(8, 16):
                    evac(b)
                dve.wait_ge(s_ss, KT)
                dve.tensor_scalar(sq[:, 0, :], p_ss[:], 1.0 / D, NORM_EPS, ALU.mult, ALU.add).then_inc(s_ssall, 1)
                dve.wait_ge(s_std, 1)
                done(dve.reciprocal(rstd[:], rstd[:]))
                dve.tensor_tensor(fm[:, :, 0:CTX], fm[:, :, 0:CTX],
                                  rstd[:, 0:CTX].unsqueeze(1).broadcast_to([P, KT, CTX]), ALU.mult)\
                   .then_inc(s_nrm, 1)

                def row(r, h, used, at):
                    dve.wait_ge(ring.used, used)
                    dve.tensor_copy(rows[:, h, :], p_row[h][0:4, :]).then_inc(s_rowc, 1)
                    dve.wait_ge(s_modp, r + 1)
                    dve.tensor_copy(modv[:, bass.ds(at, 4), :],
                                    p_col[:, 0:8].rearrange("p (f v) -> p f v", v=2)).then_inc(s_modc, 1)

                def body(i):
                    for h in range(2):
                        for m in range(4 * h, 4 * h + 4, 2):
                            ring.split_lo(dve, m, tile_no(i, 8, m))
                        if not (isinstance(i, int) and i == 0 and h == 0):
                            row(i * 2 + (h - 1), 1 - h, i * 8 + 4 * h, i * 8 + 4 * (h - 1))
                bodies(dve, NB, body, True)
                row(2 * NB - 1, 1, 8 * NB, 8 * NB - 4)
                dve.wait_ge(s_modc, 2 * NB)
                done(dve.tensor_tensor(modv[:], modv[:], col("ada_b", 0, 6 * KT).unsqueeze(2)
                                       .broadcast_to([P, 6 * KT, 2]), ALU.add))
                done(dve.tensor_scalar(gain[:], modv[:, KT:2 * KT, :], 1.0, None, ALU.add))
                done(dve.tensor_tensor(gain[:], gain[:], col("norm_pre_mix", 0, KT).unsqueeze(2)
                                       .broadcast_to([P, KT, 2]), ALU.mult))
                dve.wait_ge(s_xst, 16)
                done(dve.tensor_tensor(fm[:, :, CTX:], fm[:, :, CTX:],
                                       rstd[:, CTX:].unsqueeze(1).broadcast_to([P, KT, SEQ]), ALU.mult))
                for k in range(KT):
                    if k >= 2:
                        dve.wait_ge(s_hh, k - 1)
                    for v, lo in ((1, 0), (0, CTX)):
                        last = dve.tensor_scalar(hbuf[:, k % 2, lo:lo + CTX], fm[:, k, lo:lo + CTX],
                                                 gain[:, k, v:v + 1], modv[:, k, v:v + 1], ALU.mult, ALU.add)
                    last.then_inc(s_h, 1)
                    dve.wait_ge(s_hh, k + 1)
                    dve.tensor_tensor(h_lo[:, k, :], hbuf[:, k % 2, :], b32(h_hi[:, k, :]), ALU.subtract)\
                       .then_inc(s_hl, 1)


W_IN_SEGMENTS = [(0, 4, True, T_R), (RW, 8, False, T_K), (RWKV_IN, 2, True, T_GQ),
                 (RWKV_IN + GQW, 6, False, T_GK), (RWKV_IN + 2 * GQW + GVW, 4, True, T_GG),
                 (MIX_IN, 16, True, T_GATE)]


def phase_w_in(nc, A, env):
    alloc, psum, sem, Ring = (env[k] for k in ("alloc", "psum", "sem", "Ring"))
    h_hi, h_lo, px = env["h_hi"], env["h_lo"], env["px"]
    tile_no, bodies, mm3 = env["tile_no"], env["bodies"], env["mm3"]
    s_evac = sem("w_in_group_copied")
    s_out = [sem(f"w_in_group_stored{g}") for g in range(2)]
    w = A["w_in"].rearrange("a (k p) n -> p (a k) n", p=P)
    n_bodies = sum(s[1] for s in W_IN_SEGMENTS) // 2
    with ExitStack() as st:
        ring = Ring(st, "p")
        stage = alloc(st, "stage", [P, 2, 2, TOK])
        pp = [psum(st, f"p_in{g}", 2 * TOK) for g in range(2)]

        def segments(eng, body):
            before = 0
            for seg in W_IN_SEGMENTS:
                n = seg[1] // 2
                bodies(eng, max(n - 1, 1), lambda i: body(seg, i, before), True)
                if n > 1:
                    body(seg, n - 1, before)
                before += n

        def start(i, before):
            return isinstance(i, int) and i + before == 0

        def toks(seg):
            return slice(CTX, TOK) if seg[2] else slice(0, TOK)

        with nc.Block() as block:

            @block.sync
            def _(sp):
                def body(seg, i, before):
                    for m in range(4):
                        src = w[:, KH * (m % 2):KH * (m % 2) + KH, bass.ds(i * 512 + (seg[0] + 256 * (m // 2)), 256)]
                        ring.load(sp, src, m, tile_no(i, 4, m + 4 * before), (KH, 256))
                segments(sp, body)
                for n in range(6):
                    t = 4 * n_bodies + n
                    ring.load(sp, w[:, :, LORA_COLS[n]:LORA_COLS[n] + LORA], t, t, (KT, LORA))

            @block.scalar
            def _(act):
                def store_lora(n):
                    act.wait_ge(s_evac, 2 * n_bodies + n + 1)
                    act.dma_start(px[T_LORA + n, 0:LORA, :], stage[0:LORA, n % 2, 0, :]).then_inc(s_out[n % 2], 16)

                def store(seg, i, before, g, back=0):
                    act.wait_ge(s_evac, i * 2 + (2 * (before - back) + g + 1))
                    act.dma_start(px[bass.ds(i * 4 + (seg[3] + 2 * g - 4 * back), 2), :, toks(seg)]
                                  .rearrange("f p t -> p f t"), stage[:, g, :, toks(seg)]).then_inc(s_out[g], 16)

                def body(seg, i, before):
                    for m in range(4):
                        ring.split_hi(act, m, tile_no(i, 4, m + 4 * before))
                        if m == 1 and not (isinstance(i, int) and i == 0):
                            store(seg, i, before, 1, 1)
                    store(seg, i, before, 0)
                    if isinstance(i, int) and i == seg[1] // 2 - 1:
                        store(seg, i, before, 1)
                segments(act, body)
                for n in range(6):
                    t = 4 * n_bodies + n
                    ring.split_hi(act, t, t, KT * LORA)
                    if n:
                        store_lora(n - 1)
                store_lora(5)
                for g in range(2):
                    act.wait_ge(s_out[g], 16 * (n_bodies + 3))

            @block.gpsimd
            def _(pool):
                def body(seg, i, before):
                    for m in (1, 3):
                        ring.split_lo(pool, m, tile_no(i, 4, m + 4 * before))
                segments(pool, body)
                for n in (1, 3, 5):
                    t = 4 * n_bodies + n
                    ring.split_lo(pool, t, t, KT * LORA)

            @block.vector
            def _(dve):
                def copy(seg, i, before, g, back=0):
                    b = before - back
                    dve.wait_ge(ring.used, i * 4 + (4 * b + 2 * g + 2))
                    if not start(i, b):
                        dve.wait_ge(s_out[g], i * 16 + 16 * b)
                    dve.tensor_copy(stage[:, g, :, toks(seg)], pp[g][:].rearrange("p (f t) -> p f t", f=2)
                                    [:, :, toks(seg)]).then_inc(s_evac, 1)

                def body(seg, i, before):
                    ring.split_lo(dve, 0, tile_no(i, 4, 4 * before))
                    if not (isinstance(i, int) and i == 0):
                        copy(seg, i, before, 1, 1)
                    ring.split_lo(dve, 2, tile_no(i, 4, 2 + 4 * before))
                    copy(seg, i, before, 0)
                    if isinstance(i, int) and i == seg[1] // 2 - 1:
                        copy(seg, i, before, 1)
                segments(dve, body)
                for n in range(6):
                    t = 4 * n_bodies + n
                    if n % 2 == 0:
                        ring.split_lo(dve, t, t, KT * LORA)
                    dve.wait_ge(ring.used, t + 1)
                    dve.wait_ge(s_out[n % 2], 16 * (n_bodies + n // 2))
                    dve.tensor_copy(stage[0:LORA, n % 2, 0, :], pp[n % 2][0:LORA, 0:TOK]).then_inc(s_evac, 1)

            @block.tensor
            def _(pe):
                def body(seg, i, before):
                    ts = toks(seg)
                    for g in range(2):
                        if not start(i, before):
                            pe.wait_ge(s_evac, i * 2 + (2 * before + g - 1))
                        for q in range(2):
                            m = 2 * g + q
                            ring.wait_split(pe, m, tile_no(i, 4, m + 4 * before))
                            s = m % ring.S
                            for f in range(2):
                                o = pp[g][:, f * TOK + ts.start:(f + 1) * TOK]
                                for k in range(KH):
                                    at = slice(k * 256 + f * P, k * 256 + (f + 1) * P)
                                    kk = KH * q + k
                                    last = mm3(pe, o, ring.hi[:, s, at], ring.lo[:, s, at], h_hi[:, kk, ts],
                                               h_lo[:, kk, ts], kk == 0, kk == KT - 1)
                            last.then_inc(ring.used, 1)
                segments(pe, body)
                for n in range(6):
                    t = 4 * n_bodies + n
                    pe.wait_ge(s_evac, 2 * n_bodies + n - 1)
                    ring.wait_split(pe, t, t)
                    for k in range(KT):
                        at = slice(k * LORA, (k + 1) * LORA)
                        last = mm3(pe, pp[n % 2][0:LORA, 0:TOK], ring.hi[:, t % ring.S, at],
                                   ring.lo[:, t % ring.S, at], h_hi[:, k, :], h_lo[:, k, :], k == 0, k == KT - 1)
                    last.then_inc(ring.used, 1)


def phase_rwkv_pre(nc, A, out, env):
    alloc, psum, sem, col, px = (env[k] for k in ("alloc", "psum", "sem", "col", "px"))
    shared_d, r_d, dir_d, post_d = (env[k] for k in ("shared_d", "r_d", "dir_d", "post_d"))
    head_ones, one_minus_mu, half_mu, one_minus_ka = (env[k] for k in
                                                      ("head_ones", "one_minus_mu", "half_mu", "one_minus_ka"))
    s_zero = sem("r_edges_zero")
    s_w = sem("r_lora_weights_landed")
    s_lx = sem("r_lora_inputs_landed")
    s_in = [sem(f"r_pair_landed{n}") for n in range(2)]
    s_nb = sem("r_lora_neighbours_added")
    s_mid = sem("r_lora_middle_scaled")
    s_lmix = sem("r_lora_shifted")
    s_lact = sem("r_lora_activated")
    s_nk, s_mk, s_mix = sem("r_neighbours_added"), sem("r_middle_scaled"), sem("r_shifted")
    s_nr = sem("r_r_neighbours_added")
    s_kx, s_sq, s_ss, s_mx, s_nrm = (sem(f"r_{n}") for n in
                                     ("k_scaled", "k_squared", "k_square_sums", "norm_floored", "norm_ready"))
    s_inv = sem("r_norm_inverted")
    s_kk = sem("r_kk_ready")
    s_z, s_sg = sem("r_lora_products"), sem("r_sigmoids")
    s_lw, s_u, s_nak, s_kd, s_ks = (sem(f"r_{n}") for n in
                                    ("log_decay_ready", "k_factor_ready", "rate_ready", "kd_ready", "kd_summed"))
    s_rk, s_bp, s_post, s_v = (sem(f"r_{n}") for n in
                               ("bonus_terms", "bonus_and_gate_products", "bonus_and_gate_ready", "vector_step"))
    s_st = [sem(f"r_pair_stored{n}") for n in range(2)]
    N_ST = 5

    with ExitStack() as st:
        w2 = alloc(st, "w2", [LORA, 2, RW])
        a2 = alloc(st, "a2", [LORA, 2, RW])
        g2 = alloc(st, "g2", [GLORA, RW])
        lpad = alloc(st, "lora_pad", [LORA, 5, 2, SEQ + 2])
        lnb = alloc(st, "lora_nb", [LORA, 5, 2, SEQ])
        lmid = alloc(st, "lora_mid", [LORA, 5, 2, SEQ])
        lx = alloc(st, "lora_x", [LORA, 5, TOK])
        pad = alloc(st, "pad", [P, 2, 2, 2, SEQ + 2])
        rpad = alloc(st, "rpad", [P, 2, SEQ + 2])
        nb = alloc(st, "nb", [P, 2, 2, 2, SEQ])
        mid = alloc(st, "mid", [P, 2, 2, 2, SEQ])
        rnb = alloc(st, "rnb", [P, 2, SEQ])
        rmid = alloc(st, "rmid", [P, 2, SEQ])
        kmix = alloc(st, "kmix", [P, 2, TOK])
        kx = alloc(st, "kx", [P, 2, TOK])
        ksq = alloc(st, "ksq", [P, 2, TOK])
        nrm = alloc(st, "nrm", [P, 2, TOK])
        sh = alloc(st, "sh", [P, 2, 2, TOK])
        rr = alloc(st, "rr", [P, 2, SEQ])
        sg = alloc(st, "sg", [P, 2, 2, 2, TOK])
        dr = alloc(st, "dr", [P, 2, 2, 3, TOK])
        u = alloc(st, "u", [P, 2, 2, TOK])
        ks = alloc(st, "ks", [P, 2, SEQ])
        post = alloc(st, "post", [P, 2, 2, SEQ])
        pz = [psum(st, f"pz{n}", TOK) for n in range(4)]
        pss = psum(st, "pss", TOK)
        pbonus = psum(st, "pbonus", SEQ)
        pgate = psum(st, "pgate", SEQ)

        with nc.Block() as block:

            @block.sync
            def _(sp):
                sp.dma_start(w2[:], A["rwkv_w2"][0].rearrange("d k n -> k d n")).then_inc(s_w, 16)
                sp.dma_start(a2[:], A["rwkv_a2"][0].rearrange("d k n -> k d n")).then_inc(s_w, 16)
                sp.dma_start(g2[:], A["rwkv_g2"][0]).then_inc(s_w, 16)
                for n in range(5):
                    sp.dma_start(lpad[:, n, :, 1:SEQ + 1], px[T_LORA + n, 0:LORA, :]
                                 .rearrange("p (s t) -> p s t", s=2)).then_inc(s_lx, 16)

                def load(j):
                    if j >= 2:
                        sp.wait_ge(s_mk, j - 1)
                        sp.wait_ge(s_nk, j - 1)
                        sp.wait_ge(s_nr, j - 1)
                    for n, t in enumerate((T_K, T_V)):
                        sp.dma_start(pad[:, j % 2, n, :, 1:SEQ + 1], px[t + j].rearrange("p (s t) -> p s t", s=2))\
                          .then_inc(s_in[j % 2], 16)
                    sp.dma_start(rpad[:, j % 2, 1:SEQ + 1], px[T_R + j, :, CTX:]).then_inc(s_in[j % 2], 16)

                def store(j):
                    b = j % 2
                    sp.wait_ge(s_kk, j + 1)
                    sp.wait_ge(s_mix, 3 * (j + 1))
                    sp.dma_start(shared_d.rearrange("p (a j) t -> p a j t", a=2)[:, :, j, :], sh[:, b])\
                      .then_inc(s_st[b], 16)
                    sp.dma_start(r_d[:, j, :], rr[:, b, :]).then_inc(s_st[b], 16)
                    sp.wait_ge(s_nak, 2 * (j + 1))
                    sp.wait_ge(s_kd, 2 * (j + 1))
                    sp.wait_ge(s_lw, 2 * (j + 1))
                    for d in range(2):
                        sp.dma_start(dir_d[d].rearrange("p (a j) t -> p a j t", a=3)[:, :, j, :], dr[:, b, d])\
                          .then_inc(s_st[b], 16)
                    sp.wait_ge(s_post, 2 * (j + 1))
                    sp.dma_start(post_d.rearrange("p (a j) t -> p a j t", a=2)[:, :, j, :], post[:, b])\
                      .then_inc(s_st[b], 16)
                load(0)
                load(1)
                for j in range(PAIRS):
                    store(j)
                    if j + 2 < PAIRS:
                        load(j + 2)
                for b in range(2):
                    sp.wait_ge(s_st[b], 16 * N_ST * PAIRS // 2)

            @block.gpsimd
            def _(pool):
                pool.wait_ge(s_zero, 2)
                pool.wait_ge(s_lx, 80)
                pool.tensor_tensor(lnb[:], lpad[:, :, :, 0:SEQ], lpad[:, :, :, 2:SEQ + 2], ALU.add).then_inc(s_nb, 1)

                def neighbours(j):
                    b = j % 2
                    pool.wait_ge(s_in[b], 48 * (j // 2 + 1))
                    if j >= 2:
                        pool.wait_ge(s_mix, 3 * (j - 1))
                    for n in range(2):
                        last = pool.tensor_tensor(nb[:, b, n], pad[:, b, n, :, 0:SEQ], pad[:, b, n, :, 2:SEQ + 2],
                                                  ALU.add)
                    last.then_inc(s_nk, 1)
                pool.wait_ge(s_nb, 1)
                neighbours(0)
                for j in range(PAIRS):
                    b = j % 2
                    if j + 1 < PAIRS:
                        neighbours(j + 1)
                    if j >= 2:
                        pool.wait_ge(s_st[b], 16 * N_ST * (j // 2))
                    for d in range(2):
                        pool.wait_ge(s_sg, 4 * j + 2 * d + 1)
                        pool.tensor_scalar(dr[:, b, d, 0, :], sg[:, b, 0, d, :], -DECAY_TOP, None, ALU.mult)\
                            .then_inc(s_lw, 1)
                        pool.wait_ge(s_sg, 4 * j + 2 * d + 2)
                        if j >= 2:
                            pool.wait_ge(s_kd, 2 * (j - 1))
                        pool.tensor_scalar(u[:, b, d, :], sg[:, b, 1, d, :], col("rwkv_k_a", j), one_minus_ka[:, j:j + 1],
                                           ALU.mult, ALU.add).then_inc(s_u, 1)

            @block.scalar
            def _(act):
                act.wait_ge(s_lx, 80)
                for n in range(5):
                    act.activation(lmid[:, n], lpad[:, n, :, 1:SEQ + 1], ACT.Copy,
                                   scale=one_minus_mu[0:LORA, 24 + n:25 + n]).then_inc(s_mid, 1)
                act.wait_ge(s_lmix, 5)
                act.activation(lx[:, 0:2, :], lx[:, 0:2, :], ACT.Tanh).then_inc(s_lact, 1)
                act.activation(lx[0:GLORA, 4, :], lx[0:GLORA, 4, :], ACT.Sigmoid).then_inc(s_lact, 1)

                def middle(j):
                    b = j % 2
                    act.wait_ge(s_in[b], 48 * (j // 2 + 1))
                    if j >= 2:
                        act.wait_ge(s_mix, 3 * (j - 1))
                    for n, m in enumerate((PAIRS + j, 2 * PAIRS + j)):
                        act.activation(mid[:, b, n], pad[:, b, n, :, 1:SEQ + 1], ACT.Copy,
                                       scale=one_minus_mu[:, m:m + 1])
                    act.activation(rmid[:, b, :], rpad[:, b, 1:SEQ + 1], ACT.Copy, scale=one_minus_mu[:, j:j + 1])\
                       .then_inc(s_mk, 1)
                middle(0)
                for j in range(PAIRS):
                    b = j % 2
                    act.wait_ge(s_kx, j + 1)
                    if j >= 2:
                        act.wait_ge(s_ss, j - 1)
                    act.activation(ksq[:, b, :], kx[:, b, :], ACT.Square).then_inc(s_sq, 1)
                    if j >= 2:
                        act.wait_ge(s_lw, 2 * (j - 1))
                        act.wait_ge(s_u, 2 * (j - 1))
                        act.wait_ge(s_nak, 2 * (j - 1))
                    for d in range(2):
                        for w, name in enumerate(("rwkv_w0", "rwkv_a0")):
                            act.wait_ge(s_z, 4 * j + 2 * d + w + 1)
                            act.activation(sg[:, b, w, d, :], pz[2 * w + d][:], ACT.Sigmoid,
                                           bias=col(name, d * PAIRS + j)).then_inc(s_sg, 1)
                    act.wait_ge(s_mx, j + 1)
                    act.activation(nrm[:, b, :], nrm[:, b, :], ACT.Sqrt).then_inc(s_nrm, 1)
                    act.wait_ge(s_bp, j + 1)
                    if j >= 2:
                        act.wait_ge(s_st[b], 16 * N_ST * (j // 2))
                    act.activation(post[:, b, 1, :], pgate[:, 0:SEQ], ACT.Copy).then_inc(s_post, 1)
                    if j + 1 < PAIRS:
                        middle(j + 1)

            @block.tensor
            def _(pe):
                pe.wait_ge(s_w, 48)
                pe.wait_ge(s_lact, 2)
                for j in range(PAIRS):
                    b = j % 2
                    at = slice(j * P, (j + 1) * P)
                    for d in range(2):
                        for w, wt in enumerate((w2, a2)):
                            if j:
                                pe.wait_ge(s_sg, 4 * (j - 1) + 2 * d + w + 1)
                            pe.matmul(pz[2 * w + d][:], wt[:, d, at], lx[:, 2 * w + d, :], start=True, stop=True)\
                              .then_inc(s_z, 1)
                    pe.wait_ge(s_sq, j + 1)
                    if j:
                        pe.wait_ge(s_mx, j)
                    pe.matmul(pss[:], head_ones[:], ksq[:, b, :], start=True, stop=True).then_inc(s_ss, 1)
                    pe.wait_ge(s_rk, j + 1)
                    if j:
                        pe.wait_ge(s_post, 2 * j)
                    pe.matmul(pbonus[:, 0:SEQ], head_ones[:], ks[:, b, :], start=True, stop=True)
                    pe.matmul(pgate[:, 0:SEQ], g2[:, at], lx[0:GLORA, 4, CTX:], start=True, stop=True).then_inc(s_bp, 1)

            @block.vector
            def _(dve):
                step = [0]

                def done(ins):
                    step[0] += 1
                    ins.then_inc(s_v, 1)
                    dve.wait_ge(s_v, step[0])

                for n in range(2):
                    dve.memset(lpad[:, :, :, n * (SEQ + 1):n * (SEQ + 1) + 1], 0.0)
                    dve.memset(pad[:, :, :, :, n * (SEQ + 1):n * (SEQ + 1) + 1], 0.0)
                    dve.memset(rpad[:, :, n * (SEQ + 1):n * (SEQ + 1) + 1], 0.0).then_inc(s_zero, 1)
                dve.wait_ge(s_zero, 2)
                dve.wait_ge(s_nb, 1)
                for n in range(5):
                    dve.wait_ge(s_mid, n + 1)
                    dve.scalar_tensor_tensor(out=lx[:, n, :], in0=lnb[:, n].rearrange("p s t -> p (s t)"),
                                             scalar=half_mu[0:LORA, 24 + n:25 + n],
                                             in1=lmid[:, n].rearrange("p s t -> p (s t)"),
                                             op0=ALU.mult, op1=ALU.add).then_inc(s_lmix, 1)
                for j in range(PAIRS):
                    b = j % 2
                    dve.wait_ge(s_nk, j + 1)
                    dve.tensor_tensor(rnb[:, b, :], rpad[:, b, 0:SEQ], rpad[:, b, 2:SEQ + 2], ALU.add).then_inc(s_nr, 1)
                    dve.wait_ge(s_mk, j + 1)
                    if j >= 2:
                        dve.wait_ge(s_st[b], 16 * N_ST * (j // 2))
                    for n, (o, m) in enumerate(((kmix[:, b, :], PAIRS + j), (sh[:, b, 1, :], 2 * PAIRS + j))):
                        dve.scalar_tensor_tensor(out=o, in0=nb[:, b, n].rearrange("p s t -> p (s t)"),
                                                 scalar=half_mu[:, m:m + 1],
                                                 in1=mid[:, b, n].rearrange("p s t -> p (s t)"),
                                                 op0=ALU.mult, op1=ALU.add).then_inc(s_mix, 1)
                    dve.wait_ge(s_nr, j + 1)
                    dve.scalar_tensor_tensor(out=rr[:, b, :], in0=rnb[:, b, :], scalar=half_mu[:, j:j + 1],
                                             in1=rmid[:, b, :], op0=ALU.mult, op1=ALU.add).then_inc(s_mix, 1)
                    dve.wait_ge(s_mix, 3 * j + 1)
                    dve.tensor_scalar(kx[:, b, :], kmix[:, b, :], col("rwkv_k_k", j), None, ALU.mult).then_inc(s_kx, 1)
                    dve.wait_ge(s_ss, j + 1)
                    dve.tensor_scalar(nrm[:, b, :], pss[:], 1e-24, None, ALU.max).then_inc(s_mx, 1)
                    for d in range(2):
                        dve.wait_ge(s_u, 2 * j + d + 1)
                        dve.tensor_tensor(dr[:, b, d, 2, :], u[:, b, d, :], kmix[:, b, :], ALU.mult).then_inc(s_kd, 1)
                    dve.wait_ge(s_kd, 2 * (j + 1))
                    dve.wait_ge(s_mix, 3 * (j + 1))
                    if j >= 2:
                        dve.wait_ge(s_bp, j - 1)
                    dve.tensor_tensor(ks[:, b, :], dr[:, b, 0, 2, CTX:], dr[:, b, 1, 2, CTX:], ALU.add).then_inc(s_ks, 1)
                    dve.wait_ge(s_ks, j + 1)
                    dve.scalar_tensor_tensor(out=ks[:, b, :], in0=ks[:, b, :], scalar=col("rwkv_r_k", j),
                                             in1=rr[:, b, :], op0=ALU.mult, op1=ALU.mult).then_inc(s_rk, 1)
                    dve.wait_ge(s_nrm, j + 1)
                    dve.reciprocal(nrm[:, b, :], nrm[:, b, :]).then_inc(s_inv, 1)
                    dve.wait_ge(s_inv, j + 1)
                    dve.tensor_tensor(sh[:, b, 0, :], kx[:, b, :], nrm[:, b, :], ALU.mult).then_inc(s_kk, 1)
                    dve.wait_ge(s_kk, j + 1)
                    for d in range(2):
                        dve.scalar_tensor_tensor(out=dr[:, b, d, 1, :], in0=sg[:, b, 1, d, :], scalar=-1.0,
                                                 in1=sh[:, b, 0, :], op0=ALU.mult, op1=ALU.mult).then_inc(s_nak, 1)
                    dve.wait_ge(s_bp, j + 1)
                    dve.tensor_tensor(post[:, b, 0, :], pbonus[:, 0:SEQ], sh[:, b, 1, CTX:], ALU.mult).then_inc(s_post, 1)


def phase_rwkv_scan(nc, A, out, env):
    alloc, psum, sem = (env[k] for k in ("alloc", "psum", "sem"))
    shared_d, r_d, dir_d, y_d = (env[k] for k in ("shared_d", "r_d", "dir_d", "y_d"))
    U8 = PAIRS
    LV = 5
    names = {}

    def sm(name, d):
        if (name, d) not in names:
            names[name, d] = sem(f"s_{name}_{'fb'[d]}")
        return names[name, d]

    with ExitStack() as st:
        masks = alloc(st, "masks", [P, 2, 2, C])
        y_sum = alloc(st, "y_sum", [P, U8, SEQ])
        masks_bd = alloc(st, "masks_bd", [P, 2, 8, 2, C])
        eye = env["ident"]

        def pair_of(name, shape, dt=f32):
            return [alloc(st, f"{name}_{x}", [P] + shape, dt) for x in "fb"]

        kkv = pair_of("kkv", [2, U8, C])
        rc = pair_of("rc", [U8, C])
        ldr = pair_of("ldr", [3, U8, C])
        b = pair_of("b", [U8, C])
        bm = pair_of("bm", [U8, C])
        es = pair_of("es", [U8, C])
        q12 = pair_of("q12", [U8, 2, C])
        q1_bd = pair_of("q1_bd", [U8, 2, C])
        s1_bd = pair_of("s1_bd", [U8, 2, C])
        s2_bd = pair_of("s2_bd", [U8, 2, C])
        w_bd = pair_of("w_bd", [U8, 2, C])
        t1_bd = pair_of("t1_bd", [U8, 2, C])
        n_bd = [pair_of(f"n_bd{n}", [U8, 2, C]) for n in range(2)]
        t2_bd = pair_of("t2_bd", [U8, 2, C])
        r1 = pair_of("r1", [U8, C])
        r2 = pair_of("r2", [U8, C])
        x_bd = pair_of("x_bd", [U8, 2, C])
        xt_bd = pair_of("xt_bd", [U8, 2, C])
        rhs = pair_of("rhs", [U8, C])
        vt = pair_of("vt", [U8, C])
        vt_bd = pair_of("vt_bd", [U8, P])
        s1t_bd = pair_of("s1t_bd", [U8, P])
        s2t_bd = pair_of("s2t_bd", [U8, P])
        u = pair_of("u", [U8, C])
        S = pair_of("S", [U8, C])
        s_bd = pair_of("s_bd", [U8, 2, C])
        e_end = pair_of("e_end", [U8])
        keep = alloc(st, "keep", [P, U8 * C])
        refs = alloc(st, "refs", [P, 2])
        pa = [psum(st, f"pa{d}", 2 * U8 * C) for d in range(2)]
        pb = [psum(st, f"pb{d}", 2 * U8 * C) for d in range(2)]
        W = U8 * C

        def halves(bd, h):
            return bd[64 * h:64 * h + 64, :, h, :]

        def flat(t):
            return t[:].rearrange("p u c -> p (u c)")

        def mask(n, d):
            return masks[:, d, n, :].unsqueeze(1).broadcast_to([P, U8, C])

        def mask_bd(n, d):
            return masks_bd[:, d, n].unsqueeze(1).broadcast_to([P, U8, 2, C])

        def twice(t):
            return t.unsqueeze(2).broadcast_to([P, U8, 2, C])

        def mask_half(n, d, h):
            return masks[64 * h:64 * h + 64, d, n, :].unsqueeze(1).broadcast_to([64, U8, C])
        STRICT, INCL = range(2)
        HEADS, LEVEL0_T, LEVEL0 = 5, 6, 7
        EYE_BD = eye[:].unsqueeze(1).broadcast_to([P, U8, P])

        def wide(t):
            return t[:].rearrange("p u h c -> p u (h c)")

        def level_banks(d, l):
            return (pa[d], pb[d]) if l % 2 else (pb[d], pa[d])

        def bank(p, n):
            return p[:, n * W:(n + 1) * W].rearrange("p (u c) -> p u c", u=U8)

        def both(p):
            return p[:].rearrange("p (u c) -> p u c", u=U8)

        def whole(c, n):
            return isinstance(c, int) and c == n

        def later(c):
            return not whole(c, 0)

        def later_x(c, x):
            return x and not whole(c, 4)

        def needs_bd(c, x):
            return whole(c, 3) or (x and not whole(c, 7))

        def half(step, d, last, c, lev):
            def go(name, at, *which):
                if at and name in step:
                    step[name](*at, *which)
            go("prepare", c, d)
            for l, after_a, after_b in ((1, "rhs", "u"), (2, "state", "output"), (3, "scores1", "scores2"),
                                        (4, "tokens", "flip1"), (5, "flip2", None)):
                if l == 3:
                    go("prepare2", c, d)
                go("grow_a", lev, 1 - d, l)
                go(after_a, last if l < 3 else c, d)
                go("grow_b", lev, 1 - d, l)
                go(after_b, last if l < 3 else c, d)

        def run(step):
            def body(c, before, x, bx):
                last = None if before is None else (before, bx)
                half(step, 0, last, (c, x), last)
                half(step, 1, last, (c, x), (c, x))
            eng = step["engine"]
            body(0, None, False, False)
            body(1, 0, False, False)
            with eng.Fori(2, 4) as i:
                body(i, i - 1, False, False)
            body(4, 3, True, False)
            body(5, 4, True, True)
            with eng.Fori(6, 8) as i:
                body(i, i - 1, True, True)
            half(step, 0, (7, True), None, (7, True))
            half(step, 1, (7, True), None, None)

        with nc.Block() as block:

            @block.sync
            def _(sp):
                sp.dma_start(masks[:], A["scan_masks"]).then_inc(sm("masks", 0), 16)
                sp.dma_start(masks_bd[:], A["scan_masks_bd"]).then_inc(sm("masks", 0), 16)

                def body(c, x):
                    for d in range(2):
                        at = c * C if d == 0 else (c * -C) + (11 if x else 3) * C
                        if x:
                            rat = (c * C) - 4 * C if d == 0 else (c * -C) + 7 * C
                        if later(c):
                            for n, count in (("v_bd", c * 2), ("s1_bd", c * 2), ("q1", c), ("s2_bd", c), ("bm", c)):
                                sp.wait_ge(sm(n, d), count)
                        sp.dma_start(kkv[d][:].rearrange("p a u t -> p (a u) t"), shared_d[:, :, bass.ds(at, C)])\
                          .then_inc(sm("in", d), 16)
                        sp.dma_start(ldr[d][:].rearrange("p a u t -> p (a u) t"), dir_d[d, :, :, bass.ds(at, C)])\
                          .then_inc(sm("in", d), 16)
                        if x:
                            if later_x(c, x):
                                sp.wait_ge(sm("q2", d), c - 4)
                            sp.dma_start(rc[d][:], r_d[:, :, bass.ds(rat, C)]).then_inc(sm("rin", d), 16)
                body(0, False)
                with sp.Fori(1, 4) as i:
                    body(i, False)
                body(4, True)
                with sp.Fori(5, 8) as i:
                    body(i, True)
                sp.wait_ge(sm("ysum", 0), 8)
                sp.dma_start(y_d, y_sum[:]).then_inc(sm("stored", 0), 16)
                sp.wait_ge(sm("stored", 0), 16)

            @block.vector
            def _(dve):
                dve.memset(keep[:], 1.0).then_inc(sm("init", 0), 1)
                dve.wait_ge(sm("init", 0), 1)
                dve.memset(keep[:].rearrange("p (u c) -> p u c", u=U8)[:, :, 0:1], 0.0).then_inc(sm("init", 0), 1)
                for n, v in ((0, REF), (1, -REF)):
                    dve.memset(refs[:, n:n + 1], v)
                for d in range(2):
                    for t in (q1_bd, s1_bd, s2_bd, w_bd, n_bd[0], n_bd[1], t1_bd, t2_bd, s_bd, S):
                        dve.memset(t[d][:], 0.0).then_inc(sm("init", 1), 1)
                dve.memset(y_sum[:], 0.0).then_inc(sm("init", 0), 1)
                dve.wait_ge(sm("init", 0), 3)

                def prepare(c, x, d):
                    rev = slice(None, None, -1 if d else 1)
                    dve.wait_ge(sm("in", d), c * 32 + 32)
                    if later(c):
                        dve.wait_ge(sm("e2", d), c)
                    dve.tensor_tensor_scan(out=flat(b[d])[:, rev], data0=keep[:],
                                           data1=ldr[d][:, 0].rearrange("p u c -> p (u c)")[:, rev], initial=0.0,
                                           op0=ALU.mult, op1=ALU.add).then_inc(sm("b", d), 1)
                    dve.wait_ge(sm("b", d), c + 1)
                    dve.tensor_tensor(bm[d][:], b[d][:], ldr[d][:, 0], ALU.subtract).then_inc(sm("bm", d), 1)
                    dve.wait_ge(sm("es", d), c + 1)
                    if later(c):
                        dve.wait_ge(sm("t2r2", d), c)
                        dve.wait_ge(sm("q1_bd", d), c * 2)
                    dve.tensor_tensor(ldr[d][:, 1], ldr[d][:, 1], es[d][:], ALU.mult).then_inc(sm("s1", d), 1)
                    dve.wait_ge(sm("e1", d), c + 1)
                    dve.tensor_tensor(q12[d][:, :, 0, :], kkv[d][:, 0], bm[d][:], ALU.mult).then_inc(sm("q1", d), 1)

                def prepare2(c, x, d):
                    if x:
                        if later_x(c, x):
                            dve.wait_ge(sm("y", d), c - 4)
                        dve.wait_ge(sm("rin", d), c * 16 - 48)
                        dve.wait_ge(sm("e2", d), c + 1)
                        dve.tensor_tensor(q12[d][:, :, 1, :], rc[d][:], b[d][:], ALU.mult).then_inc(sm("q2", d), 1)

                def scores1(c, x, d):
                    p1 = pa[d][:].rearrange("p (u q c) -> p u q c", u=U8, q=2)
                    if whole(c, 0):
                        dve.wait_ge(sm("masks", 0), 32)
                    dve.wait_ge(sm("t1r1", d), c + 1)
                    if later(c):
                        dve.wait_ge(sm("n_bd", d), c * LV)
                    for h in range(2):
                        dve.tensor_tensor(halves(t1_bd[d], h), p1[64 * h:64 * h + 64, :, 0, :],
                                          mask_half(STRICT, d, h), ALU.mult).then_inc(sm("t1", d), 1)
                    if x:
                        dve.tensor_tensor(r1[d][:], p1[:, :, 1, :], mask(INCL, d), ALU.mult).then_inc(sm("r1", d), 1)

                def scores2(c, x, d):
                    p2 = pb[d][:].rearrange("p (u q c) -> p u q c", u=U8, q=2)
                    dve.wait_ge(sm("t2r2", d), c + 1)
                    for h in range(2):
                        dve.tensor_tensor(halves(t2_bd[d], h), p2[64 * h:64 * h + 64, :, 0, :],
                                          mask_half(STRICT, d, h), ALU.mult).then_inc(sm("t2", d), 1)
                    if x:
                        dve.tensor_tensor(r2[d][:], p2[:, :, 1, :], mask(INCL, d), ALU.mult).then_inc(sm("r2", d), 1)

                def flip1(c, x, d):
                    dve.wait_ge(sm("ntr", d), c + 1)
                    dve.tensor_tensor(wide(x_bd[d]), both(pb[d]), mask_bd(LEVEL0, d).rearrange("p u h c -> p u (h c)"),
                                      ALU.mult).then_inc(sm("xm", d), 1)
                    dve.wait_ge(sm("xm", d), c + 1)
                    dve.tensor_tensor(wide(x_bd[d]), wide(x_bd[d]), EYE_BD, ALU.add).then_inc(sm("x", d), 1)
                    dve.wait_ge(sm("xtm", d), c + 1)
                    dve.tensor_tensor(wide(xt_bd[d]), wide(xt_bd[d]), EYE_BD, ALU.add).then_inc(sm("xt", d), 1)

                def grow_a(c, x, d, l):
                    if l > 1:
                        dve.wait_ge(sm("xtr", d), c * (LV - 1) + (l - 1))
                        dve.tensor_copy(wide(xt_bd[d]), both(level_banks(d, l - 1)[0])).then_inc(sm("xtc", d), 1)

                def grow_b(c, x, d, l):
                    p_xt, p_x = level_banks(d, l)
                    if l < LV:
                        dve.wait_ge(sm("dx", d), c * (LV - 1) + l)
                        dve.tensor_tensor(wide(x_bd[d]), wide(x_bd[d]), both(p_x), ALU.add).then_inc(sm("x", d), 1)
                    else:
                        dve.wait_ge(sm("dxt", d), c + 1)
                        dve.tensor_tensor(wide(xt_bd[d]), wide(xt_bd[d]), both(p_xt), ALU.add)\
                            .then_inc(sm("inverse", d), 1)

                def state(c, x, d):
                    if whole(c, 7):
                        return
                    dve.wait_ge(sm("st", d), c + 1)
                    dve.tensor_tensor(S[d][:], S[d][:], bank(pa[d], 1), ALU.add).then_inc(sm("sadd", d), 1)
                    dve.wait_ge(sm("sadd", d), c + 1)
                    dve.wait_ge(sm("e_end", d), c + 1)
                    dve.tensor_tensor(S[d][:], S[d][:], e_end[d][:].unsqueeze(2).broadcast_to([P, U8, C]), ALU.mult)\
                       .then_inc(sm("S", d), 1)

                def output(c, x, d):
                    if x:
                        yat = y_sum[:, :, bass.ds((c * C) - 4 * C if d == 0 else (c * -C) + 7 * C, C)]
                        dve.wait_ge(sm("y", d), c - 3)
                        if d or later_x(c, x):
                            dve.wait_ge(sm("ysum", 0), c * 2 - 8 + d)
                        dve.tensor_tensor(yat, yat, bank(pb[d], 0), ALU.add).then_inc(sm("ysum", 0), 1)
                    if needs_bd(c, x):
                        dve.wait_ge(sm("S", d), c + 1)
                        for h in range(2):
                            dve.tensor_copy(halves(s_bd[d], h), S[d][64 * h:64 * h + 64]).then_inc(sm("s_bd", d), 1)
                run(dict(engine=dve, prepare=prepare, prepare2=prepare2, scores1=scores1, scores2=scores2,
                         flip1=flip1, grow_a=grow_a, grow_b=grow_b,
                         state=state, output=output))

            @block.scalar
            def _(act):
                act.wait_ge(sm("init", 1), 20)

                def prepare(c, x, d):
                    act.wait_ge(sm("b", d), c + 1)
                    if later(c):
                        act.wait_ge(sm("s1", d), c)
                        act.wait_ge(sm("s2_bd", d), c)
                    act.activation(es[d][:], b[d][:], ACT.Exp, bias=refs[:, 1:2], scale=-1.0).then_inc(sm("es", d), 1)
                    act.wait_ge(sm("bm", d), c + 1)
                    act.activation(bm[d][:], bm[d][:], ACT.Exp, bias=refs[:, 0:1]).then_inc(sm("e1", d), 1)
                    act.wait_ge(sm("s1", d), c + 1)
                    if later(c):
                        act.wait_ge(sm("s1tr", d), c)
                    for h in range(2):
                        act.activation(halves(s1_bd[d], h), ldr[d][64 * h:64 * h + 64, 1], ACT.Copy)\
                           .then_inc(sm("s1_bd", d), 1)

                def prepare2(c, x, d):
                    last = 0 if d else C - 1
                    if later(c):
                        act.wait_ge(sm("S", d), c)
                    act.activation(e_end[d][:].unsqueeze(2), b[d][:, :, last:last + 1], ACT.Exp)\
                       .then_inc(sm("e_end", d), 1)
                    act.wait_ge(sm("es", d), c + 1)
                    act.wait_ge(sm("e_end", d), c + 1)
                    act.activation(b[d][:], b[d][:], ACT.Exp, bias=refs[:, 0:1]).then_inc(sm("e2", d), 1)
                    act.wait_ge(sm("q1", d), c + 1)
                    if later(c):
                        act.wait_ge(sm("rhs", d), c)
                    for h in range(2):
                        act.activation(halves(q1_bd[d], h), q12[d][64 * h:64 * h + 64, :, 0, :], ACT.Copy)\
                           .then_inc(sm("q1_bd", d), 1)
                    if later_x(c, x):
                        act.wait_ge(sm("y", d), c - 4)
                    for h in range(2):
                        act.activation(halves(w_bd[d], h), kkv[d][64 * h:64 * h + 64, 1], ACT.Copy)\
                           .then_inc(sm("v_bd", d), 1)

                def tokens(c, x, d):
                    act.wait_ge(sm("vtr", d), c + 1)
                    act.activation(vt_bd[d][:], both(pa[d]), ACT.Copy).then_inc(sm("vt_bd", d), 1)
                    for h in range(2):
                        act.activation(vt[d][64 * h:64 * h + 64], both(pa[d])[64 * h:64 * h + 64, :, 64 * h:64 * h + 64],
                                       ACT.Copy).then_inc(sm("vt", d), 1)

                def flip1(c, x, d):
                    act.wait_ge(sm("s1tr", d), c + 1)
                    act.activation(s1t_bd[d][:], both(pa[d]), ACT.Copy).then_inc(sm("s1t", d), 1)

                def flip2(c, x, d):
                    act.wait_ge(sm("s2tr", d), c + 1)
                    act.activation(s2t_bd[d][:], both(pb[d]), ACT.Copy).then_inc(sm("s2t", d), 1)

                def grow_a(c, x, d, l):
                    act.wait_ge(sm("nx", d), c * LV + l)
                    act.activation(wide(w_bd[d]), both(level_banks(d, l)[0]), ACT.Copy).then_inc(sm("y_bd", d), 1)

                def rhs_copy(c, x, d):
                    act.wait_ge(sm("rhs", d), c + 1)
                    act.activation(rhs[d][:], bank(pb[d], 1), ACT.Copy).then_inc(sm("rhsc", d), 1)

                def u_step(c, x, d):
                    act.wait_ge(sm("u", d), c + 1)
                    act.activation(u[d][:], bank(pa[d], 0), ACT.Copy).then_inc(sm("uc", d), 1)
                    if x:
                        for h in range(2):
                            act.activation(halves(w_bd[d], h), bank(pa[d], 0)[64 * h:64 * h + 64], ACT.Copy)\
                               .then_inc(sm("u_bd", d), 1)
                run(dict(engine=act, prepare=prepare, prepare2=prepare2, tokens=tokens, flip1=flip1,
                         flip2=flip2, grow_a=grow_a,                         rhs=rhs_copy, u=u_step))

            @block.gpsimd
            def _(pool):
                pool.wait_ge(sm("init", 1), 20)
                pool.wait_ge(sm("masks", 0), 32)

                def prepare(c, x, d):
                    pool.wait_ge(sm("es", d), c + 1)
                    pool.tensor_tensor(ldr[d][:, 2], ldr[d][:, 2], es[d][:], ALU.mult).then_inc(sm("s2", d), 1)
                    pool.wait_ge(sm("s2", d), c + 1)
                    if later(c):
                        pool.wait_ge(sm("s2tr", d), c)
                    pool.tensor_tensor(s2_bd[d][:], twice(ldr[d][:, 2]), mask_bd(HEADS, d), ALU.mult).then_inc(sm("s2_bd", d), 1)

                def block_of(c, d, l):
                    pool.tensor_tensor(n_bd[l % 2][d][:], t1_bd[d][:], mask_bd(l - 1, d), ALU.mult)\
                        .then_inc(sm("n_bd", d), 1)

                def tokens(c, x, d):
                    pool.wait_ge(sm("t1", d), c * 2 + 2)
                    if later(c):
                        pool.wait_ge(sm("u", d), c)
                    pool.tensor_tensor(xt_bd[d][:], t1_bd[d][:], mask_bd(LEVEL0_T, d), ALU.mult)\
                        .then_inc(sm("xtm", d), 1)
                    if later(c):
                        pool.wait_ge(sm("nx", d), c * LV)
                    for l in (1, 2):
                        block_of(c, d, l)

                def grow_a(c, x, d, l):
                    if l + 2 <= LV:
                        pool.wait_ge(sm("nx", d), c * LV + l)
                        block_of(c, d, l + 2)
                run(dict(engine=pool, prepare=prepare, tokens=tokens, grow_a=grow_a))

            @block.tensor
            def _(pe):
                pe.wait_ge(sm("init", 1), 20)

                def unit(t, d, j):
                    return t[d][:, j].rearrange("p h c -> p (h c)")

                def scores1(c, x, d):
                    n = 2 if x else 1
                    pe.wait_ge(sm("s1_bd", d), c * 2 + 2)
                    pe.wait_ge(sm("q1", d), c + 1)
                    if x:
                        pe.wait_ge(sm("q2", d), c - 3)
                    if later(c):
                        pe.wait_ge(sm("sadd", d), c)
                        pe.wait_ge(sm("uc", d), c)
                    if later_x(c, x):
                        pe.wait_ge(sm("u_bd", d), c * 2 - 8)
                    for j in range(U8):
                        last = pe.matmul(pa[d][:, j * P:j * P + n * C], unit(s1_bd, d, j),
                                         q12[d][:, j, 0:n, :].rearrange("p q c -> p (q c)"), start=True, stop=True)
                    last.then_inc(sm("t1r1", d), 1)

                def scores2(c, x, d):
                    n = 2 if x else 1
                    pe.wait_ge(sm("s2_bd", d), c + 1)
                    if later(c):
                        pe.wait_ge(sm("rhsc", d), c)
                    if later_x(c, x):
                        pe.wait_ge(sm("ysum", 0), c * 2 - 9 + d)
                    for j in range(U8):
                        last = pe.matmul(pb[d][:, j * P:j * P + n * C], unit(s2_bd, d, j),
                                         q12[d][:, j, 0:n, :].rearrange("p q c -> p (q c)"), start=True, stop=True)
                    last.then_inc(sm("t2r2", d), 1)

                def tokens(c, x, d):
                    pe.wait_ge(sm("v_bd", d), c * 2 + 2)
                    pe.wait_ge(sm("t1", d), c * 2 + 2)
                    if x:
                        pe.wait_ge(sm("r1", d), c - 3)
                    for j in range(U8):
                        last = pe.transpose(pa[d][:, j * P:(j + 1) * P], unit(w_bd, d, j), env["ident"][:])
                    last.then_inc(sm("vtr", d), 1)
                    pe.wait_ge(sm("t2", d), c * 2 + 2)
                    if x:
                        pe.wait_ge(sm("r2", d), c - 3)
                    for j in range(U8):
                        last = pe.transpose(pb[d][:, j * P:(j + 1) * P], unit(t1_bd, d, j), eye[:])
                    last.then_inc(sm("ntr", d), 1)

                def flip1(c, x, d):
                    pe.wait_ge(sm("vt_bd", d), c + 1)
                    pe.wait_ge(sm("vt", d), c * 2 + 2)
                    for j in range(U8):
                        last = pe.transpose(pa[d][:, j * P:(j + 1) * P], unit(s1_bd, d, j), env["ident"][:])
                    last.then_inc(sm("s1tr", d), 1)

                def flip2(c, x, d):
                    pe.wait_ge(sm("xm", d), c + 1)
                    for j in range(U8):
                        last = pe.transpose(pb[d][:, j * P:(j + 1) * P], unit(s2_bd, d, j), env["ident"][:])
                    last.then_inc(sm("s2tr", d), 1)

                def grow_a(c, x, d, l):
                    pe.wait_ge(sm("x", d), c * LV + l)
                    if l > 1:
                        for j in range(U8):
                            last = pe.transpose(level_banks(d, l - 1)[0][:, j * P:(j + 1) * P], unit(x_bd, d, j), eye[:])
                        last.then_inc(sm("xtr", d), 1)
                    pe.wait_ge(sm("n_bd", d), c * LV + l)
                    if l == 1:
                        pe.wait_ge(sm("s1t", d), c + 1)
                        pe.wait_ge(sm("s2t", d), c + 1)
                    for j in range(U8):
                        last = pe.matmul(level_banks(d, l)[0][:, j * P:(j + 1) * P], unit(n_bd[l % 2], d, j),
                                         unit(x_bd, d, j), start=True, stop=True)
                    last.then_inc(sm("nx", d), 1)

                def grow_b(c, x, d, l):
                    p_xt, p_x = level_banks(d, l)
                    if l == 1:
                        pe.wait_ge(sm("xt", d), c + 1)
                    else:
                        pe.wait_ge(sm("xtc", d), c * (LV - 1) + (l - 1))
                    pe.wait_ge(sm("y_bd", d), c * LV + l)
                    if l < LV:
                        for j in range(U8):
                            last = pe.matmul(p_x[:, j * P:(j + 1) * P], unit(xt_bd, d, j), unit(w_bd, d, j),
                                             start=True, stop=True)
                        last.then_inc(sm("dx", d), 1)
                    else:
                        for j in range(U8):
                            last = pe.matmul(p_xt[:, j * P:(j + 1) * P], unit(w_bd, d, j), unit(xt_bd, d, j),
                                             start=True, stop=True)
                        last.then_inc(sm("dxt", d), 1)

                def rhs_sum(c, x, d):
                    pe.wait_ge(sm("q1_bd", d), c * 2 + 2)
                    if later(c):
                        pe.wait_ge(sm("S", d), c)
                    for j in range(U8):
                        o = pb[d][:, W + j * C:W + (j + 1) * C]
                        pe.matmul(o, unit(q1_bd, d, j), S[d][:, j, :], start=True, stop=False)
                        last = pe.matmul(o, unit(t2_bd, d, j), vt[d][:, j, :], start=False, stop=True)
                    last.then_inc(sm("rhs", d), 1)

                def u_step(c, x, d):
                    pe.wait_ge(sm("inverse", d), c + 1)
                    pe.wait_ge(sm("rhsc", d), c + 1)
                    for j in range(U8):
                        last = pe.matmul(pa[d][:, j * C:(j + 1) * C], unit(xt_bd, d, j), rhs[d][:, j, :],
                                         start=True, stop=True)
                    last.then_inc(sm("u", d), 1)

                def state(c, x, d):
                    if whole(c, 7):
                        return
                    pe.wait_ge(sm("uc", d), c + 1)
                    for j in range(U8):
                        o = pa[d][:, W + j * C:W + (j + 1) * C]
                        pe.matmul(o, s2t_bd[d][:, j, :], vt[d][:, j, :], start=True, stop=False)
                        last = pe.matmul(o, s1t_bd[d][:, j, :], u[d][:, j, :], start=False, stop=True)
                    last.then_inc(sm("st", d), 1)

                def output(c, x, d):
                    if not x:
                        return
                    pe.wait_ge(sm("uc", d), c + 1)
                    pe.wait_ge(sm("u_bd", d), c * 2 - 6)
                    pe.wait_ge(sm("s_bd", d), c * 2 - 6)
                    for j in range(U8):
                        o = pb[d][:, j * C:(j + 1) * C]
                        pe.matmul(o, unit(s_bd, d, j), q12[d][:, j, 1, :], start=True, stop=False)
                        pe.matmul(o, vt_bd[d][:, j, :], r2[d][:, j, :], start=False, stop=False)
                        last = pe.matmul(o, unit(w_bd, d, j), r1[d][:, j, :], start=False, stop=True)
                    last.then_inc(sm("y", d), 1)
                run(dict(engine=pe, scores1=scores1, scores2=scores2, tokens=tokens, flip1=flip1, flip2=flip2, grow_a=grow_a, grow_b=grow_b, rhs=rhs_sum,
                         u=u_step, state=state, output=output))


def phase_gla(nc, A, out, env):
    alloc, psum, sem, col, px = (env[k] for k in ("alloc", "psum", "sem", "col", "px"))
    ident, ones, yb_d = (env[k] for k in ("ident", "ones", "yb_d"))
    BT = SEQ // P
    LEVELS = 8
    VT = GVW // P
    ORDER = [(l, d) for l in range(LEVELS) for d in range(2)]
    (s_w, s_lx, s_q, s_k, s_v, s_g, s_zero, s_z, s_zc, s_abs, s_exp, s_ln, s_la, s_b, s_qp, s_kp, s_vp, s_vt, s_vtc,
     s_be, s_bx, s_kc, s_kt, s_ktc, s_S, s_Sc, s_qb, s_qbm, s_diff, s_e, s_Q, s_K, s_att, s_sel, s_sel2, s_o, s_oc,
     s_osq, s_oss, s_std, s_sqrt, s_rec, s_sig, s_silu, s_yb1, s_yb, s_st, s_v2, s_mask) = \
        [sem(f"g_{n}") for n in
         ("weights_landed", "lora_landed", "q_landed", "k_landed", "v_landed", "g_landed", "zeroed", "gate_products",
          "gates_copied", "abs", "exp", "ln", "log_decay", "cumulative", "q_ready", "k_ready", "v_permuted",
          "v_transposed", "v_tokens_ready", "to_end", "to_end_exp", "k_decayed", "k_transposed", "k_tokens_ready",
          "state_done", "state_ready", "from_start_exp", "q_decayed", "level_diff", "level_exp", "level_q", "level_k",
          "level_products", "level_selected", "cross_copied", "o_done", "o_copied", "o_squared", "o_square_sums",
          "o_meaned", "o_std", "o_rstd", "g_sigmoid", "g_silu", "y_scaled", "y_ready", "y_stored", "vector_step",
          "masks_landed")]

    def raster(t):
        return t.rearrange("p f (c r) -> p f r c", r=GRID_H)

    def colmajor(t):
        return t.rearrange("p f (r c) -> p f c r", c=GRID_W)

    with ExitStack() as st:
        up = alloc(st, "up", [2 * GLR, 2, GQW])
        lx = alloc(st, "g_lx", [2 * GLR, TOK])
        qr = alloc(st, "qr", [P, GH, SEQ])
        kr = alloc(st, "kr", [P, GH, TOK])
        vr = alloc(st, "vr", [P, VT, TOK])
        gr = alloc(st, "gr", [P, VT, SEQ])
        q = alloc(st, "q", [P, GH, SEQ])
        q_twice = alloc(st, "q_twice", [P, GH, SEQ])
        k = alloc(st, "k", [P, GH, SEQ])
        vp = alloc(st, "vp", [P, VT, SEQ])
        vt = alloc(st, "g_vt", [P, 2 * BT, GVW])
        zb = [alloc(st, f"zb{d}", [P, GH, TOK]) for d in range(2)]
        ez = alloc(st, "ez", [P, GH, TOK])
        keep = alloc(st, "g_keep", [P, GH, TOK])
        B = [alloc(st, f"B{d}", [P, GH, TOK]) for d in range(2)]
        kc = alloc(st, "kc", [P, GH, CTX])
        kct = alloc(st, "kct", [P, GH, BT, P])
        S = [alloc(st, f"g_S{d}", [P, GH, GV]) for d in range(2)]
        qb = [alloc(st, f"qb{d}", [P, GH, SEQ]) for d in range(2)]
        E = alloc(st, "E", [P, 2, GH, SEQ])
        Q = alloc(st, "Q", [P, 2, GH, SEQ])
        K = alloc(st, "K", [P, 2, GH, SEQ])
        att = ez[:].rearrange("p h (s t n) -> p h s t n", s=BT, t=BT)
        gm = alloc(st, "gm", [P, 2, 7, P])
        one = alloc(st, "one", [P, 1])
        o, osq, rec, sg = vr[:, :, 0:SEQ], vr[:, :, SEQ:], kr[:, :, 0:SEQ], gr
        pl = [psum(st, f"pl{n}", 512) for n in range(4)]
        po = [psum(st, f"po{n}", 512) for n in range(4)]

        with nc.Block() as block:

            @block.sync
            def _(sp):
                sp.wait_ge(s_zero, 1)
                for d in range(2):
                    sp.dma_start(up[GLR * d:GLR * d + GLR, d, :], A["gla_alpha_up"][0, d]).then_inc(s_w, 16)
                sp.dma_start(lx[:], px[T_LORA + 5, 0:2 * GLR, :]).then_inc(s_lx, 16)
                sp.dma_start(gm[:], A["gla_masks"]).then_inc(s_mask, 16)

                def rows(t0, n, lo):
                    return px[t0:t0 + n, :, lo:].rearrange("f p t -> p f t")
                sp.dma_start(kr[:], rows(T_GK, GH, 0)).then_inc(s_k, 16)
                sp.dma_start(vr[:], rows(T_GV, VT, 0)).then_inc(s_v, 16)
                sp.dma_start(qr[:], rows(T_GQ, GH, CTX)).then_inc(s_q, 16)
                sp.dma_start(gr[:], rows(T_GG, VT, CTX)).then_inc(s_g, 16)
                sp.wait_ge(s_yb, VT)
                sp.dma_start(yb_d, vp[:]).then_inc(s_st, 16)
                sp.wait_ge(s_st, 16)

            @block.gpsimd
            def _(pool):
                pool.wait_ge(s_k, 16)
                pool.tensor_copy(k[:].rearrange("p f (c r) -> p f c r", r=GRID_H), colmajor(kr[:, :, CTX:])).then_inc(s_kp, 1)
                pool.wait_ge(s_v, 16)
                pool.tensor_copy(vp[:].rearrange("p f (c r) -> p f c r", r=GRID_H), colmajor(vr[:, :, CTX:])).then_inc(s_vp, 1)
                for n, (l, d) in enumerate(ORDER):
                    pool.wait_ge(s_e, n + 1)
                    if n >= 2:
                        pool.wait_ge(s_att, n - 1)
                    pool.tensor_tensor(K[:, n % 2], k[:], E[:, n % 2], ALU.mult).then_inc(s_K, 1)

            @block.scalar
            def _(act):
                act.wait_ge(s_q, 16)
                for f in range(GH):
                    act.activation(q[:, f].rearrange("p (c r) -> p c r", r=GRID_H),
                                   qr[:, f].rearrange("p (r c) -> p c r", c=GRID_W), ACT.Copy, scale=float(GK) ** -0.5)
                    act.activation(q_twice[:, f].rearrange("p (c r) -> p c r", r=GRID_H),
                                   qr[:, f].rearrange("p (r c) -> p c r", c=GRID_W), ACT.Copy,
                                   scale=2 * float(GK) ** -0.5).then_inc(s_qp, 1)
                for n in range(2 * GH):
                    d, h = n // GH, n % GH
                    act.wait_ge(s_z, n + 1)
                    bias = col("gla_alpha_b", n)
                    act.activation(zb[d][:, h, 0:CTX], pl[n % 4][:, 0:CTX], ACT.Identity, bias=bias)
                    act.activation(zb[d][:, h, CTX:].rearrange("p (c r) -> p c r", r=GRID_H),
                                   pl[n % 4][:, CTX:].rearrange("p (r c) -> p c r", c=GRID_W), ACT.Identity,
                                   bias=bias).then_inc(s_zc, 1)
                act.wait_ge(s_v2, 3)
                for d in range(2):
                    act.wait_ge(s_zc, GH * (d + 1))
                    if d:
                        act.wait_ge(s_la, 1)
                    act.activation(ez[:], zb[d][:], ACT.Abs).then_inc(s_abs, 1)
                    act.wait_ge(s_abs, d + 1)
                    act.activation(ez[:], ez[:], ACT.Exp, scale=-1.0).then_inc(s_exp, 1)
                    act.wait_ge(s_exp, d + 1)
                    act.activation(ez[:], ez[:], ACT.Ln, bias=one[:]).then_inc(s_ln, 1)
                for n in range(2 * VT * BT // 4):
                    act.wait_ge(s_vt, n + 1)
                    blk, f = n // 2, 4 * (n % 2)
                    act.activation(vt[:, blk, f * P:(f + 4) * P], pl[n % 4][:], ACT.Copy).then_inc(s_vtc, 1)
                for d in range(2):
                    act.wait_ge(s_be, d + 1)
                    act.activation(kc[:], kc[:], ACT.Exp, scale=1 / GLA_TAU).then_inc(s_bx, 1)
                    act.activation(qb[d][:], B[d][:, :, CTX:], ACT.Exp, scale=1 / GLA_TAU).then_inc(s_qb, 1)
                    for n in range(2):
                        act.wait_ge(s_kt, 2 * d + n + 1)
                        act.activation(kct[:, 2 * n:2 * n + 2].rearrange("p f b s -> p (f b s)"), pl[n][:], ACT.Copy)\
                           .then_inc(s_ktc, 1)
                    for n in range(2):
                        act.wait_ge(s_S, 2 * d + n + 1)
                        act.activation(S[d][:, 2 * n:2 * n + 2, :].rearrange("p f v -> p (f v)"), pl[2 + n][:], ACT.Copy)\
                           .then_inc(s_Sc, 1)
                for n, (l, d) in enumerate(ORDER):
                    act.wait_ge(s_diff, n + 1)
                    act.activation(E[:, n % 2], E[:, n % 2], ACT.Exp, scale=1 / GLA_TAU).then_inc(s_e, 1)
                    if l == LEVELS - 1:
                        act.wait_ge(s_att, n + 1)
                        src, dst = (0, 1) if d == 0 else (1, 0)
                        act.activation(att[:, :, src, dst, :], pl[2 * (n % 2)][:].rearrange("p (h t) -> p h t", h=GH),
                                       ACT.Copy).then_inc(s_sel2, 1)
                for n in range(VT // 2):
                    act.wait_ge(s_o, n + 1)
                    act.activation(o[:, 2 * n:2 * n + 2, :], po[n][:].rearrange("p (f t) -> p f t", f=2), ACT.Copy)\
                       .then_inc(s_oc, 1)
                    act.wait_ge(s_oc, n + 1)
                    act.activation(osq[:, 2 * n:2 * n + 2, :], o[:, 2 * n:2 * n + 2, :], ACT.Square).then_inc(s_osq, 1)
                act.wait_ge(s_std, GH)
                act.activation(rec, rec, ACT.Sqrt).then_inc(s_sqrt, 1)
                act.wait_ge(s_g, 16)
                act.activation(vp[:], gr[:], ACT.Sigmoid).then_inc(s_sig, 1)

            @block.vector
            def _(dve):
                step = [0]

                def done(ins):
                    step[0] += 1
                    ins.then_inc(s_v2, 1)
                    dve.wait_ge(s_v2, step[0])
                dve.memset(up[:], 0.0).then_inc(s_zero, 1)
                done(dve.memset(keep[:], 1.0))
                done(dve.memset(keep[:].rearrange("p h (s t) -> p (h s) t", s=2)[:, :, 0:1], 0.0))
                done(dve.memset(one[:], 1.0))
                for d in range(2):
                    dve.wait_ge(s_ln, d + 1)
                    dve.scalar_tensor_tensor(out=zb[d][:].rearrange("p h t -> p (h t)"),
                                             in0=zb[d][:].rearrange("p h t -> p (h t)"), scalar=0.0,
                                             in1=ez[:].rearrange("p h t -> p (h t)"), op0=ALU.min, op1=ALU.subtract)\
                       .then_inc(s_la, 1)
                    dve.wait_ge(s_la, d + 1)
                    rev = slice(None, None, -1 if d else 1)
                    dve.tensor_tensor_scan(out=B[d][:].rearrange("p h t -> p (h t)")[:, rev],
                                           data0=keep[:].rearrange("p h t -> p (h t)"),
                                           data1=zb[d][:].rearrange("p h t -> p (h t)")[:, rev], initial=0.0,
                                           op0=ALU.mult, op1=ALU.add).then_inc(s_b, 1)
                for d in range(2):
                    end = 0 if d else CTX - 1
                    dve.wait_ge(s_b, d + 1)
                    if d:
                        dve.wait_ge(s_kt, 2)
                    dve.tensor_tensor(kc[:], B[d][:, :, end:end + 1].broadcast_to([P, GH, CTX]), B[d][:, :, 0:CTX],
                                      ALU.subtract).then_inc(s_be, 1)
                    dve.wait_ge(s_bx, d + 1)
                    dve.wait_ge(s_k, 16)
                    dve.tensor_tensor(kc[:], kc[:], kr[:, :, 0:CTX], ALU.mult).then_inc(s_kc, 1)
                    dve.wait_ge(s_qb, d + 1)
                    dve.wait_ge(s_qp, GH)
                    dve.tensor_tensor(qb[d][:], qb[d][:], q[:], ALU.mult).then_inc(s_qbm, 1)

                def diff(n):
                    l, d = ORDER[n]
                    m = 1 << l
                    if n >= 2:
                        dve.wait_ge(s_K, n - 1)
                        dve.wait_ge(s_Q, n - 1)
                    x = B[d][:, :, CTX:].rearrange("p h (n two m) -> p h n two m", two=2, m=m)
                    e = E[:, n % 2].rearrange("p h (n two m) -> p h n two m", two=2, m=m)
                    earlier, later = (1, 0) if d else (0, 1)
                    ref = x[:, :, :, 1, 0:1] if d else x[:, :, :, 0, m - 1:m]
                    ref = ref.broadcast_to([P, GH, SEQ // (2 * m), m])
                    dve.tensor_tensor(e[:, :, :, later, :], x[:, :, :, later, :], ref, ALU.subtract)
                    dve.tensor_tensor(e[:, :, :, earlier, :], ref, x[:, :, :, earlier, :], ALU.subtract).then_inc(s_diff, 1)

                def select(n, mask):
                    dve.wait_ge(s_att, n + 1)
                    if n:
                        dve.wait_ge(s_sel, 2 * min(n, 2 * (LEVELS - 1)))
                    for blk in range(BT):
                        dve.copy_predicated(att[:, :, blk, blk, :], mask, pl[2 * (n % 2) + blk][:]
                                            .rearrange("p (h t) -> p h t", h=GH)).then_inc(s_sel, 1)
                dve.memset(ez[:], 0.0).then_inc(s_zero, 1)
                diff(0)
                dve.wait_ge(s_mask, 16)
                dve.wait_ge(s_zero, 2)
                for n, (l, d) in enumerate(ORDER):
                    if n + 1 < len(ORDER):
                        diff(n + 1)
                    dve.wait_ge(s_e, n + 1)
                    if n >= 2:
                        dve.wait_ge(s_att, n - 1)
                    dve.tensor_tensor(Q[:, n % 2], q[:], E[:, n % 2], ALU.mult).then_inc(s_Q, 1)
                    if n >= 1 and n - 1 < 2 * (LEVELS - 1):
                        pl_, pd = ORDER[n - 1]
                        select(n - 1, gm[:, pd, pl_, :].bitcast(mybir.dt.uint32).unsqueeze(1).broadcast_to([P, GH, P]))
                select(len(ORDER), ident[:].bitcast(mybir.dt.uint32).unsqueeze(1).broadcast_to([P, GH, P]))
                for h in range(GH):
                    dve.wait_ge(s_oss, h + 1)
                    dve.tensor_scalar(rec[:, h, :], pl[h][:, 0:SEQ], 1.0 / GV, GLA_EPS, ALU.mult, ALU.add).then_inc(s_std, 1)
                dve.wait_ge(s_sqrt, 1)
                dve.reciprocal(rec, rec).then_inc(s_rec, 1)
                dve.wait_ge(s_sig, 1)
                dve.tensor_tensor(gr[:], gr[:], vp[:], ALU.mult).then_inc(s_silu, 1)
                dve.wait_ge(s_rec, 1)
                for f in range(VT):
                    dve.scalar_tensor_tensor(out=o[:, f, :], in0=o[:, f, :], scalar=col("gla_norm_g", f),
                                             in1=rec[:, f // 2, :], op0=ALU.mult, op1=ALU.mult).then_inc(s_yb1, 1)
                dve.wait_ge(s_silu, 1)
                for f in range(VT):
                    dve.wait_ge(s_yb1, f + 1)
                    dve.tensor_tensor(vp[:, f, :].rearrange("p (r c) -> p r c", c=GRID_W),
                                      o[:, f, :].rearrange("p (c r) -> p r c", r=GRID_H),
                                      gr[:, f, :].rearrange("p (r c) -> p r c", c=GRID_W), ALU.mult).then_inc(s_yb, 1)

            @block.tensor
            def _(pe):
                pe.wait_ge(s_w, 32)
                pe.wait_ge(s_lx, 16)
                for n in range(2 * GH):
                    if n >= 4:
                        pe.wait_ge(s_zc, n - 3)
                    pe.matmul(pl[n % 4][:], up[:, n // GH, (n % GH) * P:(n % GH + 1) * P], lx[:], start=True, stop=True)\
                      .then_inc(s_z, 1)
                pe.wait_ge(s_v, 16)
                for n in range(2 * VT * BT // 4):
                    pe.wait_ge(s_zc, 2 * GH)
                    if n >= 4:
                        pe.wait_ge(s_vtc, n - 3)
                    if n == 4:
                        pe.wait_ge(s_vp, 1)
                    blk, f0 = n // 2, 4 * (n % 2)
                    for f in range(4):
                        src = vr[:, f0 + f, blk * P:(blk + 1) * P] if blk < BT else vp[:, f0 + f, (blk - BT) * P:(blk - BT + 1) * P]
                        last = pe.transpose(pl[n % 4][:, f * P:(f + 1) * P], src, ident[:])
                    last.then_inc(s_vt, 1)
                pe.wait_ge(s_vtc, 2 * VT * BT // 4)
                for d in range(2):
                    pe.wait_ge(s_kc, d + 1)
                    if d:
                        pe.wait_ge(s_ktc, 2)
                    for n in range(2):
                        for i in range(4):
                            h, b = 2 * n + i // 2, i % 2
                            last = pe.transpose(pl[n][:, i * P:(i + 1) * P], kc[:, h, b * P:(b + 1) * P], ident[:])
                        last.then_inc(s_kt, 1)
                    pe.wait_ge(s_ktc, 2 * d + 2)
                    if d:
                        pe.wait_ge(s_Sc, 2)
                    for n in range(2):
                        for i in range(2):
                            h = 2 * n + i
                            for b in range(BT):
                                last = pe.matmul(pl[2 + n][:, i * GV:(i + 1) * GV], kct[:, h, b, :],
                                                 vt[:, b, h * GV:(h + 1) * GV], start=b == 0, stop=b == BT - 1)
                        last.then_inc(s_S, 1)
                pe.wait_ge(s_Sc, 4)

                def level(n, kk, qq, cross):
                    if n >= 2:
                        pe.wait_ge(s_sel, 2 * min(n - 1, 2 * (LEVELS - 1)))
                    if n >= 2 * (LEVELS - 1) + 2:
                        pe.wait_ge(s_sel2, 1)
                    blocks = ([(0, 1), (1, 0)][cross[1]],) if cross else ((0, 0), (1, 1))
                    for i, (sb, tb) in enumerate(blocks):
                        for h in range(GH):
                            last = pe.matmul(pl[2 * (n % 2) + i][:, h * P:(h + 1) * P], kk[:, h, sb * P:(sb + 1) * P],
                                             qq[:, h, tb * P:(tb + 1) * P], start=True, stop=True)
                    last.then_inc(s_att, 1)
                for n, (l, d) in enumerate(ORDER):
                    pe.wait_ge(s_Q, n + 1)
                    pe.wait_ge(s_K, n + 1)
                    level(n, K[:, n % 2], Q[:, n % 2], (True, d) if l == LEVELS - 1 else None)
                pe.wait_ge(s_qp, GH)
                level(len(ORDER), k[:], q_twice[:], None)
                pe.wait_ge(s_sel, 2 * (2 * (LEVELS - 1) + 1))
                pe.wait_ge(s_sel2, 2)
                pe.wait_ge(s_qbm, 2)
                for f in range(VT):
                    h, at = f // 2, slice(f * P, (f + 1) * P)
                    dst = po[f // 2][:, (f % 2) * SEQ:(f % 2 + 1) * SEQ]
                    for b in range(BT):
                        pe.matmul(dst, vt[:, BT + b, at], att[:, h, b].rearrange("p b t -> p (b t)"),
                                  start=b == 0, stop=False)
                    for d in range(2):
                        last = pe.matmul(dst, S[d][:, h, (f % 2) * P:(f % 2 + 1) * P], qb[d][:, h, :],
                                         start=False, stop=d == 1)
                    if f % 2:
                        last.then_inc(s_o, 1)
                for h in range(GH):
                    pe.wait_ge(s_osq, h + 1)
                    for f in range(2):
                        last = pe.matmul(pl[h][:, 0:SEQ], ones[:], osq[:, 2 * h + f, :], start=f == 0, stop=f == 1)
                    last.then_inc(s_oss, 1)


def phase_branches(nc, A, out, env, ya, yb):
    alloc, psum, sem, col = (env[k] for k in ("alloc", "psum", "sem", "col"))
    y_d, yb_d, post_d, head_ones = (env[k] for k in ("y_d", "yb_d", "post_d", "head_ones"))
    s_in, s_mean, s_cen, s_sq, s_var, s_ve, s_sqrt, s_rec, s_gn, s_aff, s_b, s_y, s_hi, s_lo, s_bin, s_pin = \
        [sem(f"b_{n}") for n in ("y_landed", "means", "centred", "squared", "variances", "variances_copied", "std",
                                 "rstd", "normed", "affine", "bonus_added", "y_ready", "hi", "lo", "gla_landed",
                                 "post_landed")]
    with ExitStack() as st:
        y = alloc(st, "b_y", [P, PAIRS, SEQ])
        sq = alloc(st, "b_sq", [P, PAIRS, SEQ])
        v = alloc(st, "b_var", [P, PAIRS, SEQ])
        post = alloc(st, "b_post", [P, 2 * PAIRS, SEQ])
        g = alloc(st, "b_gla", [P, PAIRS, SEQ])
        pm = [psum(st, f"pm{n}", 512) for n in range(4)]
        pv = [psum(st, f"pv{n}", 512) for n in range(4)]

        def two(t, n):
            return t[:, 2 * n:2 * n + 2, :].rearrange("p f t -> p (f t)")

        with nc.Block() as block:

            @block.sync
            def _(sp):
                sp.dma_start(y[:], y_d).then_inc(s_in, 16)
                sp.dma_start(g[:], yb_d).then_inc(s_bin, 16)
                sp.dma_start(post[:], post_d).then_inc(s_pin, 16)

            @block.tensor
            def _(pe):
                pe.wait_ge(s_in, 16)
                for n in range(4):
                    pe.matmul(pm[n][:], head_ones[:], two(y, n), start=True, stop=True).then_inc(s_mean, 1)
                for n in range(4):
                    pe.wait_ge(s_sq, n + 1)
                    pe.matmul(pv[n][:], head_ones[:], two(sq, n), start=True, stop=True).then_inc(s_var, 1)

            @block.scalar
            def _(act):
                act.wait_ge(s_bin, 16)
                act.activation(yb[0][:], g[:], ACT.Copy).then_inc(s_hi, 1)
                for n in range(4):
                    act.wait_ge(s_cen, n + 1)
                    act.activation(two(sq, n), two(y, n), ACT.Square).then_inc(s_sq, 1)
                act.wait_ge(s_ve, 4)
                act.activation(v[:], v[:], ACT.Sqrt).then_inc(s_sqrt, 1)
                act.wait_ge(s_y, 1)
                act.activation(ya[0][:], y[:], ACT.Copy).then_inc(s_hi, 1)

            @block.vector
            def _(dve):
                for n in range(4):
                    dve.wait_ge(s_mean, n + 1)
                    dve.scalar_tensor_tensor(out=two(y, n), in0=pm[n][:], scalar=-1.0 / RD, in1=two(y, n),
                                             op0=ALU.mult, op1=ALU.add).then_inc(s_cen, 1)
                for n in range(4):
                    dve.wait_ge(s_var, n + 1)
                    dve.tensor_scalar(two(v, n), pv[n][:], 1.0 / RD, GN_EPS, ALU.mult, ALU.add).then_inc(s_ve, 1)
                dve.wait_ge(s_hi, 1)
                dve.tensor_tensor(yb[1][:], g[:], b32(yb[0][:]), ALU.subtract).then_inc(s_lo, 1)
                dve.wait_ge(s_sqrt, 1)
                dve.reciprocal(v[:], v[:]).then_inc(s_rec, 1)
                dve.wait_ge(s_rec, 1)
                dve.tensor_tensor(y[:], y[:], v[:], ALU.mult).then_inc(s_gn, 1)
                dve.wait_ge(s_gn, 1)
                for f in range(PAIRS):
                    dve.tensor_scalar(y[:, f, :], y[:, f, :], col("rwkv_ln_g", f), col("rwkv_ln_b", f), ALU.mult,
                                      ALU.add).then_inc(s_aff, 1)
                dve.wait_ge(s_pin, 16)
                dve.wait_ge(s_aff, PAIRS)
                dve.tensor_tensor(y[:], y[:], post[:, 0:PAIRS, :], ALU.add).then_inc(s_b, 1)
                dve.wait_ge(s_b, 1)
                dve.tensor_tensor(y[:], y[:], post[:, PAIRS:, :], ALU.mult).then_inc(s_y, 1)
                dve.wait_ge(s_hi, 2)
                dve.tensor_tensor(ya[1][:], y[:], b32(ya[0][:]), ALU.subtract).then_inc(s_lo, 1)


def weights(t, n=0):
    return t[0, :, :].rearrange("(k p) n -> p k n", p=P)


def two_banks(p):
    return p[:].rearrange("p (f t) -> p f t", f=2)[:, :, 0:SEQ]


def phase_merge(nc, A, out, env, ya, yb, m, slots):
    alloc, psum, sem, Ring, px = (env[k] for k in ("alloc", "psum", "sem", "Ring", "px"))
    tile_no, bodies, mm3 = env["tile_no"], env["bodies"], env["mm3"]
    s_g = [sem(f"m_gates_landed{g}") for g in range(2)]
    s_sig, s_m1, s_m, s_hi, s_lo = (sem(f"m_{n}") for n in ("sigmoid", "gated", "merged", "hi", "lo"))
    wa, wb = weights(A["w_rwkv_up"]), weights(A["w_gla_up"])
    NB = D // 512
    with ExitStack() as st:
        ring = Ring(st, "m", parts=(slots, None))
        gates = alloc(st, "m_gates", [P, 2, 2, 2, SEQ])
        gated = alloc(st, "m_gated", [P, 2, 2, 2, SEQ])
        stage = alloc(st, "m_stage", [P, 2, 2, SEQ])
        pp = [[psum(st, f"pm_{g}{b}", 1024) for b in range(2)] for g in range(2)]

        with nc.Block() as block:

            @block.sync
            def _(sp):
                def body(i):
                    for g in range(2):
                        if not (isinstance(i, int) and i == 0):
                            sp.wait_ge(s_m1, i * 4 + (2 * g - 2))
                        for b in range(2):
                            sp.dma_start(gates[:, g, b], px[bass.ds(i * 4 + (T_GATE + KT * b + 2 * g), 2), :, CTX:]
                                         .rearrange("f p t -> p f t")).then_inc(s_g[g], 16)
                        for b, w in enumerate((wa, wb)):
                            ring.load(sp, w[:, :, bass.ds(i * 512 + 256 * g, 256)], 2 * g + b,
                                      tile_no(i, 4, 2 * g + b), (KH, 256))
                bodies(sp, NB, body, True)

            @block.scalar
            def _(act):
                def body(i):
                    for g in range(2):
                        for b in range(2):
                            ring.split_hi(act, 2 * g + b, tile_no(i, 4, 2 * g + b))
                        act.wait_ge(s_g[g], i * 32 + 32)
                        act.activation(gates[:, g], gates[:, g], ACT.Sigmoid).then_inc(s_sig, 1)
                        if not (isinstance(i, int) and i == 0 and g == 0):
                            hi(i * 2 + g, i * 4 + (2 * g - 2), 1 - g)

                def hi(count, at, g):
                    act.wait_ge(s_m, count)
                    act.activation(m[0][:, bass.ds(at, 2), :], stage[:, g], ACT.Copy).then_inc(s_hi, 1)
                bodies(act, NB, body, True)
                hi(2 * NB, 4 * NB - 2, 1)

            @block.gpsimd
            def _(pool):
                def body(i):
                    for n in (1, 3):
                        ring.split_lo(pool, n, tile_no(i, 4, n))
                bodies(pool, NB, body, False)

            @block.vector
            def _(dve):
                def finish(used, n, at, g):
                    dve.wait_ge(ring.used, used)
                    dve.wait_ge(s_sig, n + 1)
                    for b in range(2):
                        dve.tensor_tensor(gated[:, g, b], two_banks(pp[g][b]), gates[:, g, b], ALU.mult)\
                           .then_inc(s_m1, 1)
                    dve.wait_ge(s_m1, n * 2 + 2)
                    dve.tensor_tensor(stage[:, g], gated[:, g, 0], gated[:, g, 1], ALU.add).then_inc(s_m, 1)
                    dve.wait_ge(s_hi, n + 1)
                    dve.tensor_tensor(m[1][:, bass.ds(at, 2), :], stage[:, g], b32(m[0][:, bass.ds(at, 2), :]),
                                      ALU.subtract).then_inc(s_lo, 1)

                def body(i):
                    for g in range(2):
                        ring.split_lo(dve, 2 * g, tile_no(i, 4, 2 * g))
                        if not (isinstance(i, int) and i == 0 and g == 0):
                            finish(i * 4 + (2 * g), i * 2 + (g - 1), i * 4 + (2 * g - 2), 1 - g)
                bodies(dve, NB, body, True)
                finish(4 * NB, 2 * NB - 1, 4 * NB - 2, 1)

            @block.tensor
            def _(pe):
                def body(i):
                    for g in range(2):
                        if not (isinstance(i, int) and i == 0):
                            pe.wait_ge(s_m1, i * 4 + (2 * g - 2))
                        for b, x in enumerate((ya, yb)):
                            n = 2 * g + b
                            ring.wait_split(pe, n, tile_no(i, 4, n))
                            for f in range(2):
                                for k in range(KH):
                                    at = slice(k * 256 + f * P, k * 256 + (f + 1) * P)
                                    last = mm3(pe, pp[g][b][:, 512 * f:512 * f + SEQ], ring.hi[:, n % ring.S, at],
                                               ring.lo[:, n % ring.S, at], x[0][:, k, :], x[1][:, k, :], k == 0,
                                               k == KH - 1)
                            last.then_inc(ring.used, 1)
                bodies(pe, NB, body, True)


class Norm:

    def __init__(self, st, env, tag, sq=None):
        alloc, psum, sem = (env[k] for k in ("alloc", "psum", "sem"))
        self.ones = env["ones"]
        self.sq = sq if sq is not None else alloc(st, f"{tag}_sq", [P, KT // 2, 2 * SEQ])
        self.rstd = alloc(st, f"{tag}_rstd", [P, SEQ])
        self.ps = psum(st, f"{tag}_ps", 512)
        self.s_sq, self.s_ss, self.s_ms, self.s_std, self.s_rstd = \
            [sem(f"{tag}_{n}") for n in ("squared", "square_sums", "mean", "std", "rstd")]

    def act(self, act, x):
        act.activation(self.sq[:].rearrange("p k t -> p (k t)"), x.rearrange("p k t -> p (k t)"), ACT.Square)\
           .then_inc(self.s_sq, 1)
        act.wait_ge(self.s_ms, 1)
        act.activation(self.rstd[:], self.rstd[:], ACT.Sqrt).then_inc(self.s_std, 1)

    def pe(self, pe):
        pe.wait_ge(self.s_sq, 1)
        for k in range(KT):
            last = pe.matmul(self.ps[:, 0:SEQ], self.ones[:], self.sq[:, k // 2, (k % 2) * SEQ:(k % 2 + 1) * SEQ],
                             start=k == 0, stop=k == KT - 1)
        last.then_inc(self.s_ss, 1)

    def dve(self, dve):
        dve.wait_ge(self.s_ss, 1)
        dve.tensor_scalar(self.rstd[:], self.ps[:, 0:SEQ], 1.0 / D, NORM_EPS, ALU.mult, ALU.add).then_inc(self.s_ms, 1)
        dve.wait_ge(self.s_std, 1)
        dve.reciprocal(self.rstd[:], self.rstd[:]).then_inc(self.s_rstd, 1)
        dve.wait_ge(self.s_rstd, 1)

    def row(self, n=KT):
        return self.rstd[:].unsqueeze(1).broadcast_to([P, n, SEQ])


def phase_w_out(nc, A, out, env, m, h2, slots):
    alloc, psum, sem, Ring, col = (env[k] for k in ("alloc", "psum", "sem", "Ring", "col"))
    tile_no, bodies, mm3, modv, xfm_d, x1_d = (env[k] for k in ("tile_no", "bodies", "mm3", "modv", "xfm_d", "x1_d"))
    s_x, s_evac, s_v, s_x1, s_h, s_hi, s_lo, s_st = (sem(f"o_{n}") for n in (
        "x_landed", "copied", "vector_step", "x1_ready", "h_ready", "h_hi", "h_lo", "x1_stored"))
    w = weights(A["w_out"])
    NB = D // 512
    with ExitStack() as st:
        ring = Ring(st, "o", parts=(slots, None))
        x = alloc(st, "o_x", [P, KT, SEQ])
        mo = alloc(st, "mo", [P, KT, SEQ])
        gain = alloc(st, "o_gain", [P, KT])
        n1 = Norm(st, env, "on1", sq=ring.raw[:, 0:2].rearrange("p s n -> p (s n)")
                  .rearrange("p (k t) -> p k t", t=2 * SEQ))
        n2 = Norm(st, env, "on2", sq=n1.sq)
        pp = [psum(st, f"po_{g}", 1024) for g in range(2)]

        with nc.Block() as block:

            @block.sync
            def _(sp):
                sp.dma_start(x[:], xfm_d).then_inc(s_x, 16)

                def body(i):
                    for n in range(4):
                        ring.load(sp, w[:, KH * (n % 2):KH * (n % 2 + 1), bass.ds(i * 512 + 256 * (n // 2), 256)], n,
                                  tile_no(i, 4, n), (KH, 256))
                bodies(sp, NB, body, True)
                sp.wait_ge(s_x1, 1)
                sp.dma_start(x1_d, x[:]).then_inc(s_st, 16)
                sp.wait_ge(s_st, 16)

            @block.scalar
            def _(act):
                def body(i):
                    for n in range(4):
                        ring.split_hi(act, n, tile_no(i, 4, n))
                bodies(act, NB, body, True)
                act.wait_ge(s_evac, 2 * NB)
                n1.act(act, mo[:])
                act.wait_ge(s_x1, 1)
                n2.act(act, x[:])
                act.wait_ge(s_h, KT)
                act.activation(h2[0], mo[:], ACT.Copy).then_inc(s_hi, 1)

            @block.gpsimd
            def _(pool):
                def body(i):
                    for n in (1, 3):
                        ring.split_lo(pool, n, tile_no(i, 4, n))
                bodies(pool, NB, body, False)

            @block.vector
            def _(dve):
                step = [0]

                def done(ins):
                    step[0] += 1
                    ins.then_inc(s_v, 1)
                    dve.wait_ge(s_v, step[0])

                def copy(used, at, g):
                    dve.wait_ge(ring.used, used)
                    dve.tensor_copy(mo[:, bass.ds(at, 2), :], two_banks(pp[g])).then_inc(s_evac, 1)

                def body(i):
                    for g in range(2):
                        ring.split_lo(dve, 2 * g, tile_no(i, 4, 2 * g))
                        if not (isinstance(i, int) and i == 0 and g == 0):
                            copy(i * 4 + 2 * g, i * 4 + (2 * g - 2), 1 - g)
                bodies(dve, NB, body, True)
                copy(4 * NB, 4 * NB - 2, 1)
                done(dve.tensor_tensor(gain[:], modv[:, 2 * KT:3 * KT, 0], col("norm_post_mix", 0, KT), ALU.mult))
                n1.dve(dve)
                dve.wait_ge(s_evac, 2 * NB)
                dve.wait_ge(s_x, 16)
                for k in range(KT):
                    last = dve.scalar_tensor_tensor(out=mo[:, k, :], in0=mo[:, k, :], scalar=gain[:, k:k + 1],
                                                    in1=n1.rstd[:], op0=ALU.mult, op1=ALU.mult)
                done(last)
                dve.tensor_tensor(x[:], x[:], mo[:], ALU.add).then_inc(s_x1, 1)
                done(dve.tensor_scalar(gain[:], modv[:, 4 * KT:5 * KT, 0], 1.0, None, ALU.add))
                done(dve.tensor_tensor(gain[:], gain[:], col("norm_pre_ffn", 0, KT), ALU.mult))
                dve.wait_ge(s_x1, 1)
                n2.dve(dve)
                done(dve.tensor_tensor(mo[:], x[:], n2.row(), ALU.mult))
                for k in range(KT):
                    dve.tensor_scalar(mo[:, k, :], mo[:, k, :], gain[:, k:k + 1], modv[:, 3 * KT + k, 0:1], ALU.mult,
                                      ALU.add).then_inc(s_h, 1)
                dve.wait_ge(s_hi, 1)
                dve.tensor_tensor(h2[1], mo[:], b32(h2[0]), ALU.subtract).then_inc(s_lo, 1)

            @block.tensor
            def _(pe):
                def body(i):
                    for g in range(2):
                        if not (isinstance(i, int) and i == 0):
                            pe.wait_ge(s_evac, i * 2 + (g - 1))
                        for q in range(2):
                            n = 2 * g + q
                            ring.wait_split(pe, n, tile_no(i, 4, n))
                            for f in range(2):
                                for k in range(KH):
                                    at = slice(k * 256 + f * P, k * 256 + (f + 1) * P)
                                    kk = KH * q + k
                                    last = mm3(pe, pp[g][:, 512 * f:512 * f + SEQ], ring.hi[:, n % ring.S, at],
                                               ring.lo[:, n % ring.S, at], m[0][:, kk, :], m[1][:, kk, :], kk == 0,
                                               kk == KT - 1)
                            last.then_inc(ring.used, 1)
                bodies(pe, NB, body, True)
                n1.pe(pe)
                n2.pe(pe)


def phase_ffn_up(nc, A, out, env, h2, hid):
    alloc, psum, sem, Ring = (env[k] for k in ("alloc", "psum", "sem", "Ring"))
    tile_no, bodies, mm3 = env["tile_no"], env["bodies"], env["mm3"]
    s_sig, s_a, s_b, s_hi, s_lo = (sem(f"f_{n}") for n in ("sigmoid", "silu", "hidden", "hi", "lo"))
    wg, wu = weights(A["ffn_w_gate"]), weights(A["ffn_w_up"])
    NB = FF // 512
    with ExitStack() as st:
        ring = Ring(st, "f", split=2)
        sig = alloc(st, "f_sig", [P, 2, SEQ])
        stage = alloc(st, "f_stage", [P, 2, SEQ])
        pp = [[psum(st, f"pf_{g}{b}", 1024) for b in range(2)] for g in range(2)]

        with nc.Block() as block:

            @block.sync
            def _(sp):
                def body(i):
                    for n in range(8):
                        w = (wg, wu)[n // 2 % 2]
                        ring.load(sp, w[:, KH * (n % 2):KH * (n % 2 + 1), bass.ds(i * 512 + 256 * (n // 4), 256)], n,
                                  tile_no(i, 8, n), (KH, 256))
                bodies(sp, NB, body, True)

            @block.scalar
            def _(act):
                def gate(n, g):
                    act.wait_ge(ring.used, n * 4 + 2)
                    if not isinstance(n, int) or n:
                        act.wait_ge(s_a, n)
                    act.activation(sig[:], two_banks(pp[g][0]), ACT.Sigmoid).then_inc(s_sig, 1)

                def hi(n, at):
                    act.wait_ge(s_b, n + 1)
                    act.activation(hid[0][:, bass.ds(at, 2), :], stage[:], ACT.Copy).then_inc(s_hi, 1)

                def body(i):
                    for g in range(2):
                        first = isinstance(i, int) and i == 0 and g == 0
                        for n in range(4 * g, 4 * g + 4):
                            ring.split_hi(act, n, tile_no(i, 8, n))
                            if n % 4 == 1 and not first:
                                hi(i * 2 + (g - 1), i * 4 + (2 * g - 2))
                        gate(i * 2 + g, g)
                bodies(act, NB, body, True)
                hi(2 * NB - 1, 4 * NB - 2)

            @block.vector
            def _(dve):
                def finish(n, at, g):
                    dve.wait_ge(s_sig, n + 1)
                    if not isinstance(n, int) or n:
                        dve.wait_ge(s_lo, n)
                    dve.tensor_tensor(stage[:], two_banks(pp[g][0]), sig[:], ALU.mult).then_inc(s_a, 1)
                    dve.wait_ge(s_a, n + 1)
                    dve.wait_ge(ring.used, n * 4 + 4)
                    dve.tensor_tensor(stage[:], stage[:], two_banks(pp[g][1]), ALU.mult).then_inc(s_b, 1)

                def low(n, at):
                    dve.wait_ge(s_hi, n + 1)
                    dve.tensor_tensor(hid[1][:, bass.ds(at, 2), :], stage[:], b32(hid[0][:, bass.ds(at, 2), :]),
                                      ALU.subtract).then_inc(s_lo, 1)

                def body(i):
                    for g in range(2):
                        first = isinstance(i, int) and i == 0 and g == 0
                        for n in range(4 * g, 4 * g + 4):
                            ring.split_lo(dve, n, tile_no(i, 8, n))
                            if n % 4 == 0 and not first:
                                finish(i * 2 + (g - 1), i * 4 + (2 * g - 2), 1 - g)
                            if n % 4 == 2 and not first:
                                low(i * 2 + (g - 1), i * 4 + (2 * g - 2))
                bodies(dve, NB, body, True)
                finish(2 * NB - 1, 4 * NB - 2, 1)
                low(2 * NB - 1, 4 * NB - 2)

            @block.tensor
            def _(pe):
                def body(i):
                    for g in range(2):
                        if not (isinstance(i, int) and i == 0):
                            pe.wait_ge(s_b, i * 2 + (g - 1))
                        for b in range(2):
                            for q in range(2):
                                n = 4 * g + 2 * b + q
                                ring.wait_split(pe, n, tile_no(i, 8, n))
                                for f in range(2):
                                    for k in range(KH):
                                        at = slice(k * 256 + f * P, k * 256 + (f + 1) * P)
                                        kk = KH * q + k
                                        last = mm3(pe, pp[g][b][:, 512 * f:512 * f + SEQ], ring.hi[:, n % ring.S, at],
                                                   ring.lo[:, n % ring.S, at], h2[0][:, kk, :], h2[1][:, kk, :],
                                                   kk == 0, kk == KT - 1)
                                last.then_inc(ring.used, 1)
                bodies(pe, NB, body, True)


def phase_ffn_down(nc, A, out, env, hid, slots):
    alloc, psum, sem, Ring = (env[k] for k in ("alloc", "psum", "sem", "Ring"))
    mm3, yo_d = env["mm3"], env["yo_d"]
    s_evac, s_st = sem("d_copied"), sem("d_stored")
    w = weights(A["ffn_w_down"])
    KQ, CW = 4, 512
    PER = FF // P // KQ
    N = D // CW * PER
    with ExitStack() as st:
        ring = Ring(st, "d", parts=(slots, None))
        yo = alloc(st, "yo", [P, KT, SEQ])
        pp = [[psum(st, f"pd_{g}{f}", 512) for f in range(4)] for g in range(2)]

        with nc.Block() as block:

            @block.sync
            def _(sp):
                for t in range(N):
                    g, q = t // PER, t % PER
                    ring.load(sp, w[:, KQ * q:KQ * q + KQ, g * CW:(g + 1) * CW], t, t, (KQ, CW))
                sp.wait_ge(s_evac, D // CW)
                sp.dma_start(yo_d, yo[:]).then_inc(s_st, 16)
                sp.wait_ge(s_st, 16)

            @block.scalar
            def _(act):
                for t in range(N):
                    ring.split_hi(act, t, t)

            @block.vector
            def _(dve):
                def copy(g):
                    dve.wait_ge(ring.used, PER * (g + 1))
                    for f in range(4):
                        last = dve.tensor_copy(yo[:, 4 * g + f, :], pp[g % 2][f][:, 0:SEQ])
                    last.then_inc(s_evac, 1)
                copied = 0
                for t in range(N):
                    ring.split_lo(dve, t, t)
                    if t > PER * (copied + 1):
                        copy(copied)
                        copied += 1
                copy(copied)

            @block.tensor
            def _(pe):
                for t in range(N):
                    g, q = t // PER, t % PER
                    if q == 0 and g >= 2:
                        pe.wait_ge(s_evac, g - 1)
                    ring.wait_split(pe, t, t)
                    for f in range(4):
                        for k in range(KQ):
                            at = slice(k * CW + f * P, k * CW + (f + 1) * P)
                            kk = KQ * q + k
                            last = mm3(pe, pp[g % 2][f][:, 0:SEQ], ring.hi[:, t % ring.S, at],
                                       ring.lo[:, t % ring.S, at], hid[0][:, kk, :], hid[1][:, kk, :], kk == 0,
                                       kk == FF // P - 1)
                    last.then_inc(ring.used, 1)


def phase_final(nc, A, out, env):
    alloc, psum, sem, col = (env[k] for k in ("alloc", "psum", "sem", "col"))
    modv, x1_d, yo_d, ident = (env[k] for k in ("modv", "x1_d", "yo_d", "ident"))
    s_x, s_v, s_x2, s_t, s_tc, s_st, s_y = (sem(f"e_{n}") for n in (
        "x1_landed", "vector_step", "x2_ready", "transposed", "tokens_copied", "stored", "y_landed"))
    with ExitStack() as st:
        yo = alloc(st, "e_yo", [P, KT, SEQ])
        x = alloc(st, "e_x", [P, KT, SEQ])
        gain = alloc(st, "e_gain", [P, KT])
        tok = alloc(st, "tok", [P, 2, D])
        n3 = Norm(st, env, "en")
        pt = [psum(st, f"pt{n}", 512) for n in range(2)]

        with nc.Block() as block:

            @block.sync
            def _(sp):
                sp.dma_start(yo[:], yo_d).then_inc(s_y, 16)
                sp.dma_start(x[:], x1_d).then_inc(s_x, 16)
                for b in range(2):
                    sp.wait_ge(s_tc, 4 * b + 4)
                    sp.dma_start(out[0, b * P:(b + 1) * P, :], tok[:, b, :]).then_inc(s_st, 16)
                sp.wait_ge(s_st, 32)

            @block.scalar
            def _(act):
                act.wait_ge(s_y, 16)
                n3.act(act, yo[:])
                for n in range(0, 8, 2):
                    act.wait_ge(s_t, n + 1)
                    act.activation(tok[:, n // 4, (n % 4) * 512:(n % 4 + 1) * 512], pt[n % 2][:], ACT.Copy)\
                       .then_inc(s_tc, 1)
                    act.wait_ge(s_t, n + 2)
                    act.activation(tok[:, n // 4, (n % 4 + 1) * 512:(n % 4 + 2) * 512], pt[(n + 1) % 2][:], ACT.Copy)\
                       .then_inc(s_tc, 1)

            @block.vector
            def _(dve):
                step = [0]

                def done(ins):
                    step[0] += 1
                    ins.then_inc(s_v, 1)
                    dve.wait_ge(s_v, step[0])
                done(dve.tensor_tensor(gain[:], modv[:, 5 * KT:6 * KT, 0], col("norm_post_ffn", 0, KT), ALU.mult))
                n3.dve(dve)
                dve.wait_ge(s_y, 16)
                for k in range(KT):
                    last = dve.scalar_tensor_tensor(out=yo[:, k, :], in0=yo[:, k, :], scalar=gain[:, k:k + 1],
                                                    in1=n3.rstd[:], op0=ALU.mult, op1=ALU.mult)
                done(last)
                dve.wait_ge(s_x, 16)
                dve.tensor_tensor(x[:], x[:], yo[:], ALU.add).then_inc(s_x2, 1)

            @block.tensor
            def _(pe):
                n3.pe(pe)
                pe.wait_ge(s_x2, 1)
                for n in range(8):
                    if n >= 2:
                        pe.wait_ge(s_tc, n - 1)
                    for f in range(4):
                        last = pe.transpose(pt[n % 2][:, f * P:(f + 1) * P],
                                            x[:, 4 * (n % 4) + f, (n // 4) * P:(n // 4 + 1) * P], ident[:])
                    last.then_inc(s_t, 1)


def phase_tail(nc, A, out, env):
    alloc, end_phase = env["alloc"], env["end_phase"]

    def parts(stack, name, k):
        return [alloc(stack, f"{name}_{n}", [P, k, SEQ], f32r) for n in ("hi", "lo")]
    with ExitStack() as st_h2:
        h2_pair = alloc(st_h2, "h2", [P, 2, KT, SEQ], f32r)
        h2 = [h2_pair[:, 0], h2_pair[:, 1]]
        slots = h2_pair[:].rearrange("p a k t -> p (a k t)").rearrange("p (s n) -> p s n", s=RAW)
        with ExitStack() as st_m:
            m = parts(st_m, "m", KT)
            with ExitStack() as st_y:
                ya, yb = parts(st_y, "ya", PAIRS), parts(st_y, "yb", PAIRS)
                phase_branches(nc, A, out, env, ya, yb)
                end_phase()
                phase_merge(nc, A, out, env, ya, yb, m, slots)
                end_phase()
            phase_w_out(nc, A, out, env, m, h2, slots)
            end_phase()
        with ExitStack() as st_f:
            hid = parts(st_f, "hid", FF // P)
            phase_ffn_up(nc, A, out, env, h2, hid)
            end_phase()
            phase_ffn_down(nc, A, out, env, hid, slots)
            end_phase()
    phase_final(nc, A, out, env)


def scan_masks():
    import numpy as np
    i, t = np.arange(P)[:, None] % C, np.arange(C)[None, :]
    m = np.zeros((P, 2, 9, C), np.float32)

    def joins(src, dst, l, back):
        src_half, dst_half = (1, 0) if back else (0, 1)
        return (src >> l + 1 == dst >> l + 1) & (src >> l & 1 == src_half) & (dst >> l & 1 == dst_half)
    for d in range(2):
        m[:, d, 0] = i > t if d else i < t
        m[:, d, 1] = i >= t if d else i <= t
        for l in range(6):
            m[:, d, 2 + l] = joins(i, t, l, d)
        m[:, d, 8] = joins(t, i, 0, d)
    bd = np.zeros((P, 2, 8, 2, C), np.float32)
    for h in range(2):
        rows = slice(64 * h, 64 * h + 64)
        bd[rows, :, 0:5, h] = m[rows, :, 3:8]
        bd[rows, :, 5, h] = 1.0
        bd[rows, :, 6, h] = m[rows, :, 2]
        bd[rows, :, 7, h] = m[rows, :, 8]
    return {"scan_masks": np.ascontiguousarray(m[:, :, 0:2]), "scan_masks_bd": bd}


def gla_masks():
    import numpy as np
    s, t = np.arange(P)[:, None], np.arange(P)[None, :]
    m = np.zeros((P, 2, 7, P), np.float32)
    for d in range(2):
        for l in range(7):
            m[:, d, l] = (s >> l + 1 == t >> l + 1) & (s >> l & 1 == d) & (t >> l & 1 == 1 - d)
    return m


def consts():
    return {**scan_masks(), "gla_masks": gla_masks()}


_INS = ["x", "c", "ctx", "c_ctx", "ada_w", "ada_b", "norm_pre_mix", "norm_post_mix", "norm_pre_ffn", "norm_post_ffn",
        "w_in", "shift_mu", "rwkv_w0", "rwkv_w2", "rwkv_a0", "rwkv_a2", "rwkv_g2", "rwkv_k_k", "rwkv_k_a", "rwkv_r_k",
        "rwkv_ln_g", "rwkv_ln_b", "w_rwkv_up", "gla_alpha_up", "gla_alpha_b", "gla_norm_g", "w_gla_up", "w_out",
        "ffn_w_gate", "ffn_w_up", "ffn_w_down"]


def kernel(**inputs):
    import numpy as np
    import concourse.bacc as bacc
    from concourse.bass_utils import run_bass_kernel_spmd

    nc = bacc.Bacc("TRN2", target_bir_lowering=False, num_devices=1)
    arrays, A = {}, {}
    for name in _INS:
        a = np.ascontiguousarray(inputs[name])
        arrays[f"in_{name}"] = a
        A[name] = nc.dram_tensor(f"in_{name}", a.shape, mybir.dt.from_np(a.dtype), kind="ExternalInput").ap()
    for name, a in consts().items():
        arrays[name] = a
        A[name] = nc.dram_tensor(name, a.shape, f32, kind="ExternalInput").ap()
    out = nc.dram_tensor("out_0", (1, SEQ, D), f32, kind="ExternalOutput").ap()
    hybrid_block(nc, A, out)
    r = run_bass_kernel_spmd(nc, [arrays], core_ids=[0])
    return r.results[0]["out_0"]
```

```python
import math
from contextlib import ExitStack

import concourse.bass as bass
from concourse import mybir

D = 2048
SEQ = 256
CTX = 256
GRID_W = 64
GRID_H = SEQ // GRID_W
RH, RD = 16, 64
RW = RH * RD
LORA = 96
GLORA = 64
GH, GK, GV = 4, 128, 256
GQW, GVW = GH * GK, GH * GV
GLR = 16
FF = 5632
P = 128
KT = D // P
TOK = CTX + SEQ
RWKV_IN = 3 * RW + 4 * LORA + GLORA
MIX_IN = RWKV_IN + 2 * GQW + 2 * GVW + 2 * GLR
PAIRS = RW // P
C = 64
NCH = TOK // C
NORM_EPS = 1e-6
GN_EPS = 64e-5
GLA_EPS = 1e-5
GLA_TAU = 16.0
DECAY_TOP = math.exp(-0.5)
REF = DECAY_TOP * C / 2

f32 = mybir.dt.float32
f32r = mybir.dt.float32r
ALU = mybir.AluOpType
ACT = mybir.ActivationFunctionType

PARAM_ROWS = [("norm_pre_mix", KT), ("norm_post_mix", KT), ("norm_pre_ffn", KT), ("norm_post_ffn", KT),
              ("ada_b", 6 * KT), ("c", KT), ("c_ctx", KT), ("mu", 3 * PAIRS), ("mu_lora", 5),
              ("rwkv_w0", 2 * PAIRS), ("rwkv_a0", 2 * PAIRS), ("rwkv_k_k", PAIRS), ("rwkv_k_a", PAIRS),
              ("rwkv_r_k", PAIRS), ("rwkv_ln_g", PAIRS), ("rwkv_ln_b", PAIRS), ("gla_alpha_b", 2 * GH),
              ("gla_norm_g", 2 * GH)]
COL, _n = {}, 0
for _name, _rows in PARAM_ROWS:
    COL[_name] = _n
    _n += _rows
PROWS = -(-_n // P)

T_R, T_K, T_V, T_GQ, T_GK, T_GV, T_GG, T_GATE = 0, 8, 16, 24, 28, 32, 40, 48
T_LORA = 80
N_PX = 86
LORA_COLS = [3 * RW + LORA * n for n in range(5)] + [RWKV_IN + 2 * GQW + 2 * GVW]

RAW = 4
TILE = 2048
KH = 8


LATE_GLA, LATE_PRE = 5, 8
LATE = 2 * KT


def b32(ap):
    return ap.bitcast(f32)


def hybrid_block(nc, A, out):
    top = ExitStack()

    def dram(name, shape):
        return nc.dram_tensor(name, shape, f32, kind="Internal").ap()

    live = []

    def sem(name):
        live.append(nc.alloc_semaphore(name=name))
        return live[-1]

    def end_phase():
        nums = sorted(s.num for s in live)
        with nc.Block() as block:
            @block.sync
            def _(sp):
                at = 0
                while at < len(nums):
                    n = at
                    while n + 1 < len(nums) and nums[n + 1] == nums[n] + 1:
                        n += 1
                    sp.sem_clear(range(nums[at], nums[n] + 1))
                    at = n + 1
        for s in live:
            nc.release_semaphore(s)
        live.clear()

    px = dram("px_scratch", (N_PX, P, TOK))
    xfm_d = dram("xfm_scratch", (P, KT, SEQ))
    shared_d = dram("rwkv_kk_v_scratch", (P, 2 * PAIRS, TOK))
    r_d = dram("rwkv_r_scratch", (P, PAIRS, SEQ))
    dir_d = dram("rwkv_dir_scratch", (2, P, 3 * PAIRS, TOK))
    y_d = dram("rwkv_y_scratch", (P, PAIRS, SEQ))
    yb_d = dram("gla_y_scratch", (P, GVW // P, SEQ))
    x1_d = dram("x1_scratch", (P, KT, SEQ))
    yo_d = dram("ffn_y_scratch", (P, KT, SEQ))
    mod_d = dram("modulation_scratch", (1, 6 * D - LATE * P))
    post_d = dram("rwkv_post_scratch", (P, 2 * PAIRS, SEQ))

    def alloc(stack, name, shape, dt=f32):
        return stack.enter_context(nc.sbuf_tensor(name, shape, dt))

    def psum(stack, name, cols):
        cols = -(-cols // 512) * 512
        return stack.enter_context(nc.psum_tensor(name, [P, cols], f32))

    with top:
        ident = alloc(top, "ident", [P, P])
        ones = alloc(top, "ones", [P, P])
        head_ones = alloc(top, "head_ones", [P, P])
        prm = alloc(top, "prm", [P, PROWS * P])
        modv = alloc(top, "modv", [P, 6 * KT, 2])
        siluc = alloc(top, "siluc", [P, 2, KT])
        one_minus_mu = alloc(top, "one_minus_mu", [P, 29])
        half_mu = alloc(top, "half_mu", [P, 29])
        one_minus_ka = alloc(top, "one_minus_ka", [P, PAIRS])

        def col(name, n=0, w=1):
            return prm[:, COL[name] + n:COL[name] + n + w]

        class Raw:
            def __init__(self, stack, tag):
                self.slots = alloc(stack, f"{tag}_w_raw", [P, RAW, TILE])
                self.landed = [nc.alloc_semaphore(name=f"{tag}_w_landed{n}") for n in range(RAW)]

            def prefetch(self, eng, sources, shape):
                for n, src in enumerate(sources):
                    eng.dma_start(self.slots[:, n].rearrange("p (k n) -> p k n", k=shape[0]), src)\
                       .then_inc(self.landed[n], 16)

            def close(self):
                live.extend(self.landed)

        class Ring:
            def __init__(self, stack, tag, raw, before=0, prefetched=True, split=RAW, parts=(None, None)):
                self.R, self.S = RAW, split
                self.owner, self.raw, self.landed = raw, raw.slots, raw.landed
                self.landed_before, self.prefetched = 16 * before // RAW, prefetched
                self.hi, self.lo = [given if given is not None else
                                    alloc(stack, f"{tag}_w_{n}", [P, split, TILE], f32r)
                                    for n, given in zip(("hi", "lo"), parts)]
                self.hi_done = sem(f"{tag}_w_hi_done")
                self.lo_even = sem(f"{tag}_w_lo_even_done")
                self.lo_odd = sem(f"{tag}_w_lo_odd_done")
                self.used = sem(f"{tag}_w_used")

            def load(self, eng, src, m, t, shape):
                s = m % self.R
                if self.prefetched and isinstance(t, int) and t < self.R:
                    return
                if not (isinstance(t, int) and t < self.R):
                    lo = self.lo_odd if m % 2 else self.lo_even
                    eng.wait_ge(lo, halves(t, 1 - self.R // 2))
                w = shape[0] * shape[1]
                eng.dma_start(self.raw[:, s, 0:w].rearrange("p (k n) -> p k n", k=shape[0]), src)\
                   .then_inc(self.landed[s], 16)

            def prefetch(self, eng, tiles, sources, shape):
                eng.wait_ge(self.lo_even, (tiles + 1) // 2)
                eng.wait_ge(self.lo_odd, tiles // 2)
                self.owner.prefetch(eng, sources, shape)

            def split_hi(self, act, m, t, w=TILE):
                s = m % self.R
                act.wait_ge(self.landed[s], landings(t, self.landed_before))
                if not (isinstance(t, int) and t < self.S):
                    act.wait_ge(self.used, t - self.S + 1)
                act.activation(self.hi[:, m % self.S, 0:w], self.raw[:, s, 0:w], ACT.Copy)\
                   .then_inc(self.hi_done, 1)

            def split_lo(self, eng, m, t, w=TILE):
                s = m % self.R
                eng.wait_ge(self.hi_done, t + 1)
                eng.tensor_tensor(self.lo[:, m % self.S, 0:w], self.raw[:, s, 0:w],
                                  b32(self.hi[:, m % self.S, 0:w]), ALU.subtract)\
                   .then_inc(self.lo_odd if m % 2 else self.lo_even, 1)

            def wait_split(self, pe, m, t):
                pe.wait_ge(self.lo_odd if m % 2 else self.lo_even, halves(t, 1))

        class Tile:
            def __init__(self, i, per, const):
                self.i, self.per, self.const = i, per, const

            def __sub__(self, n):
                return self.i * self.per + (self.const - n)

            def __add__(self, n):
                return self.i * self.per + (self.const + n)

        def halves(t, n):
            return t // 2 + n if isinstance(t, int) else t.i * (t.per // 2) + (t.const // 2 + n)

        def landings(t, before):
            if isinstance(t, int):
                return before + 16 * (t // RAW + 1)
            return t.i * (16 * t.per // RAW) + (before + 16 * (t.const // RAW + 1))

        def tile_no(i, per, const):
            return i * per + const if isinstance(i, int) else Tile(i, per, const)

        def bodies(eng, n, body, peel):
            first = 1 if peel else 0
            if peel:
                body(0)
            if n - first == 1:
                body(first)
            elif n > first:
                with eng.Fori(first, n) as i:
                    body(i)

        def mm3(pe, o, wh, wl, xh, xl, first, last):
            pe.matmul(o, wh, xh, start=first, stop=False)
            pe.matmul(o, wh, xl, start=False, stop=False)
            return pe.matmul(o, wl, xh, start=False, stop=last)

        with ExitStack() as ph_h:
            h_hi = alloc(ph_h, "h_hi", [P, KT, TOK], f32r)
            h_lo = alloc(ph_h, "h_lo", [P, KT, TOK], f32r)
            raw = Raw(ph_h, "h")
            phase_inputs(nc, A, locals())
            end_phase()
            phase_w_in(nc, A, locals())
            raw.close()
            end_phase()
        for phase in (phase_gla, phase_rwkv_pre, phase_rwkv_scan, phase_tail):
            phase(nc, A, out, locals())
            end_phase()


def phase_inputs(nc, A, env):
    alloc, psum, sem, Ring, col = (env[k] for k in ("alloc", "psum", "sem", "Ring", "col"))
    ident, ones, head_ones, prm, modv = (env[k] for k in ("ident", "ones", "head_ones", "prm", "modv"))
    h_hi, h_lo, xfm_d = env["h_hi"], env["h_lo"], env["xfm_d"]
    one_minus_mu, half_mu, one_minus_ka = env["one_minus_mu"], env["half_mu"], env["one_minus_ka"]
    tile_no, bodies = env["tile_no"], env["bodies"]

    vectors = {n: A[n].rearrange("a (r p) -> (a r) p", p=P) for n in
               ("norm_pre_mix", "norm_post_mix", "norm_pre_ffn", "norm_post_ffn", "ada_b", "c",
                "rwkv_k_k", "rwkv_k_a", "rwkv_ln_g", "rwkv_ln_b", "gla_norm_g")}
    vectors["c_ctx"] = A["c_ctx"].rearrange("(r p) -> r p", p=P)
    vectors["mu"] = A["shift_mu"][:, 0:3 * RW].rearrange("a (r p) -> (a r) p", p=P)
    for n in ("rwkv_w0", "rwkv_a0", "gla_alpha_b"):
        vectors[n] = A[n].rearrange("a d (r p) -> (a d r) p", p=P)
    vectors["rwkv_r_k"] = A["rwkv_r_k"].rearrange("a (r h) k -> (a r) (h k)", h=2)
    pieces = []
    for name, rows in PARAM_ROWS:
        if name == "mu_lora":
            for n in range(5):
                w = LORA if n < 4 else GLORA
                q = COL[name] + n
                pieces.append((q // P, q % P, 1, w, A["shift_mu"][:, LORA_COLS[n]:LORA_COLS[n] + w]))
            continue
        q, at = COL[name], 0
        while at < rows:
            take = min(rows - at, P - (q + at) % P)
            pieces.append(((q + at) // P, (q + at) % P, take, P, vectors[name][at:at + take, :]))
            at += take

    s_const = sem("i_constants_made")
    s_prow = sem("i_param_rows_landed")
    s_prmT = sem("i_params_transposed")
    s_prm = sem("i_params_ready")
    s_xt = [sem(f"i_tokens_landed{n}") for n in range(2)]
    s_xT = sem("i_tokens_transposed")
    s_fm = sem("i_tokens_evacuated")
    s_sq = sem("i_squares_ready")
    s_ss = sem("i_square_sums_added")
    s_ssall = sem("i_square_sums_ready")
    s_std = sem("i_std_ready")
    s_nrm = sem("i_normalised")
    s_xst = sem("i_x_stored")
    s_sig = sem("i_c_sigmoid")
    s_sc = sem("i_c_silu")
    s_chi = sem("i_c_hi")
    s_clo = sem("i_c_split")
    s_rowc = sem("i_ada_row_copied")
    s_modp = sem("i_ada_columns_made")
    s_modc = sem("i_ada_columns_copied")
    s_v = sem("i_vector_step")
    s_h = sem("i_h_ready")
    s_hh = sem("i_h_hi_ready")
    s_hl, s_hlo = sem("i_h_lo_even_ready"), sem("i_h_lo_odd_ready")
    s_gain = sem("i_gain_ready")
    ada = A["ada_w"].rearrange("a (k p) n -> p (a k) n", p=P)
    CW = 512
    siluc = env["siluc"]
    NB = LATE * P // CW // 2

    with ExitStack() as st:
        ring = Ring(st, "i", env["raw"], prefetched=False,
                    parts=[h[:].rearrange("p k t -> p (k t)").rearrange("p (s n) -> p s n", s=RAW)
                           for h in (h_hi, h_lo)])
        prow = alloc(st, "prow", [P, PROWS, P])
        xt = alloc(st, "xt", [P, 2, D])
        fm = alloc(st, "fm", [P, KT, TOK])
        c_split = alloc(st, "c_split", [P, KT, P], f32r)
        sigc = alloc(st, "sigc", [P, 2 * KT])
        sel = alloc(st, "sel", [4, 2])
        sq = alloc(st, "sq", [P, KT, TOK])
        rstd = alloc(st, "rstd", [P, TOK])
        hbuf = alloc(st, "hbuf", [P, 2, TOK])
        rows = alloc(st, "ada_rows", [4, 2, CW])
        gain = alloc(st, "gain", [P, KT, 2])
        p_row = [psum(st, f"p_row{n}", CW) for n in range(2)]
        p_col = psum(st, "p_col", 512)
        p_xT = [psum(st, f"p_xT{n}", TOK) for n in range(2)]
        p_ss = psum(st, "p_ss", TOK)

        def low(eng, k, done_sem):
            eng.wait_ge(s_h, k + 1)
            eng.wait_ge(s_hh, k + 1)
            eng.tensor_tensor(h_lo[:, k, :], hbuf[:, k % 2, :], b32(h_hi[:, k, :]), ALU.subtract)\
               .then_inc(done_sem, 1)
        tokens = [A["ctx"][0, 0:P, :], A["ctx"][0, P:2 * P, :], A["x"][0, 0:P, :], A["x"][0, P:2 * P, :]]

        with nc.Block() as block:

            @block.gpsimd
            def _(pool):
                made = [0]

                def make(ins):
                    made[0] += 1
                    ins.then_inc(s_const, 1)
                    pool.wait_ge(s_const, made[0])
                make(pool.memset(prow[:], 0.0))
                make(pool.memset(ident[:], 0.0))
                make(pool.affine_select(out=ident[:], in_=ident[:], compare_op=ALU.not_equal, fill=1.0, base=0,
                                        pattern=[[-1, P]], channel_multiplier=1))
                make(pool.memset(ones[:], 1.0))
                make(pool.memset(head_ones[:], 0.0))
                for b in (0, 64):
                    make(pool.memset(head_ones[b:b + 64, b:b + 64], 1.0))
                make(pool.memset(b32(c_split[:]), 0.0))
                make(pool.memset(sel[:], 0.0))
                for base in (0, -2):
                    make(pool.affine_select(out=sel[:], in_=sel[:], compare_op=ALU.not_equal, fill=1.0, base=base,
                                            pattern=[[-1, 2]], channel_multiplier=1))

                def body(i):
                    for m in range(1, 8, 2):
                        ring.split_lo(pool, m, tile_no(i, 8, m))
                bodies(pool, NB, body, False)
                pool.wait_ge(ring.used, 8 * NB)
                for k in range(1, KT, 2):
                    low(pool, k, s_hlo)

            @block.sync
            def _(sp):
                for n in range(2):
                    sp.dma_start(xt[:, n, :], tokens[n]).then_inc(s_xt[n], 16)
                sp.wait_ge(s_const, 1)
                for tile, row, n, w, src in pieces:
                    sp.dma_start(prow[row:row + n, tile, 0:w], src).then_inc(s_prow, 16)

                def body(i):
                    for m in range(8):
                        src = ada[:, 4 * (m % 4):4 * (m % 4) + 4, bass.ds((i * 2 + m // 4) * CW, CW)]
                        ring.load(sp, src, m, tile_no(i, 8, m), (4, CW))
                        if isinstance(i, int) and i == 0 and m == 1:
                            for n in range(2, 4):
                                sp.wait_ge(s_xT, 4 * (n - 1))
                                sp.dma_start(xt[:, n % 2, :], tokens[n]).then_inc(s_xt[n % 2], 16)
                bodies(sp, NB, body, True)
                ring.prefetch(sp, 8 * NB, *first_w_in(A))
                sp.wait_ge(s_xst, 16)

            @block.tensor
            def _(pe):
                pe.wait_ge(s_const, 11)

                def turn(n):
                    pe.wait_ge(s_xt[n % 2], 16 * (n // 2 + 1))
                    for g in range(4):
                        b = 4 * n + g
                        if b >= 2:
                            pe.wait_ge(s_fm, b - 1)
                        for f in range(4):
                            last = pe.transpose(p_xT[b % 2][:, f * P:(f + 1) * P],
                                                xt[:, n % 2, (4 * g + f) * P:(4 * g + f + 1) * P], ident[:])
                        last.then_inc(s_xT, 1)

                def square_sums(q):
                    pe.wait_ge(s_sq, q + 1)
                    for k in range(4 * q, 4 * q + 4):
                        last = pe.matmul(p_ss[:], ones[:], sq[:, k, :], start=k == 0, stop=k == KT - 1)
                    last.then_inc(s_ss, 1)
                turn(0)
                turn(1)
                pe.wait_ge(s_prow, 16 * len(pieces))
                for r in range(PROWS):
                    last = pe.transpose(p_col[:, r * P:(r + 1) * P], prow[:, r, :], ident[:])
                last.then_inc(s_prmT, 1)
                pe.wait_ge(s_clo, 1)

                def columns(r, h):
                    pe.wait_ge(s_rowc, r + 1)
                    if isinstance(r, int) and r == 0:
                        pe.wait_ge(s_prm, 1)
                    else:
                        pe.wait_ge(s_modc, r)
                    for f in range(4):
                        last = pe.matmul(p_col[:, 2 * f:2 * f + 2], rows[:, h, f * P:(f + 1) * P], sel[:],
                                         start=True, stop=True)
                    last.then_inc(s_modp, 1)

                def body(i):
                    for h in range(2):
                        for q in range(4):
                            m = 4 * h + q
                            if q == 2 and not (isinstance(i, int) and i == 0 and h == 0):
                                columns(i * 2 + (h - 1), 1 - h)
                            ring.wait_split(pe, m, tile_no(i, 8, m))
                            for part in (ring.hi, ring.lo):
                                for k in range(4):
                                    last = pe.matmul(p_row[h][:], c_split[:, 4 * q + k, :],
                                                     part[:, m % ring.S, k * CW:(k + 1) * CW],
                                                     start=q == 0 and k == 0 and part is ring.hi,
                                                     stop=q == 3 and k == 3 and part is ring.lo)
                            last.then_inc(ring.used, 1)
                            if isinstance(i, int) and i == 0:
                                if m == 1:
                                    turn(2)
                                    turn(3)
                                if 3 <= m < 7:
                                    square_sums(m - 3)
                bodies(pe, NB, body, True)
                columns(2 * NB - 1, 1)

            @block.scalar
            def _(act):
                act.wait_ge(s_prm, 1)
                act.activation(sigc[:], prm[:, COL["c"]:COL["c"] + 2 * KT], ACT.Sigmoid).then_inc(s_sig, 1)
                act.wait_ge(s_sc, 1)
                act.activation(c_split[:, :, 0:2].rearrange("p k v -> p v k"), siluc[:], ACT.Copy)\
                   .then_inc(s_chi, 1)

                def body(i):
                    for m in range(8):
                        ring.split_hi(act, m, tile_no(i, 8, m))
                        if isinstance(i, int) and i == 0:
                            if m == 1:
                                act.wait_ge(s_fm, 16)
                                act.dma_start(xfm_d, fm[:, :, CTX:]).then_inc(s_xst, 16)
                            if 2 <= m < 6:
                                q = m - 2
                                act.activation(sq[:, 4 * q:4 * q + 4, :], fm[:, 4 * q:4 * q + 4, :], ACT.Square)\
                                   .then_inc(s_sq, 1)
                    if isinstance(i, int) and i == 0:
                        act.wait_ge(s_ssall, 1)
                        act.activation(rstd[:], rstd[:], ACT.Sqrt).then_inc(s_std, 1)
                bodies(act, NB, body, True)
                act.wait_ge(s_gain, 1)
                act.wait_ge(s_nrm, 4)
                for k in range(KT):
                    for v, lo in ((1, 0), (0, CTX)):
                        last = act.activation(h_hi[:, k, lo:lo + CTX], fm[:, k, lo:lo + CTX], ACT.Identity,
                                              bias=modv[:, k, v:v + 1], scale=gain[:, k, v:v + 1])
                    last.then_inc(s_hh, 1)

            @block.vector
            def _(dve):
                step = [0]

                def done(ins):
                    step[0] += 1
                    ins.then_inc(s_v, 1)
                    dve.wait_ge(s_v, step[0])

                def evac(b):
                    dve.wait_ge(s_xT, b + 1)
                    dve.tensor_copy(fm[:, 4 * (b % 4):4 * (b % 4) + 4, (b // 4) * P:(b // 4 + 1) * P],
                                    p_xT[b % 2][:].rearrange("p (f t) -> p f t", f=4)).then_inc(s_fm, 1)
                for b in range(8):
                    evac(b)
                dve.wait_ge(s_prmT, 1)
                dve.tensor_copy(prm[:], p_col[:, 0:PROWS * P]).then_inc(s_prm, 1)
                dve.wait_ge(s_prm, 1)
                mu = prm[:, COL["mu"]:COL["mu"] + 29]
                dve.tensor_scalar(one_minus_mu[:], mu, -1.0, 1.0, ALU.mult, ALU.add)
                dve.tensor_scalar(half_mu[:], mu, 0.5, None, ALU.mult)
                dve.tensor_scalar(one_minus_ka[:], col("rwkv_k_a", 0, PAIRS), -1.0, 1.0, ALU.mult, ALU.add)
                dve.wait_ge(s_sig, 1)
                dve.tensor_tensor(siluc[:].rearrange("p v k -> p (v k)"), prm[:, COL["c"]:COL["c"] + 2 * KT],
                                  sigc[:], ALU.mult).then_inc(s_sc, 1)
                dve.wait_ge(s_chi, 1)
                dve.tensor_tensor(c_split[:, :, 2:4].rearrange("p k v -> p v k"), siluc[:],
                                  b32(c_split[:, :, 0:2]).rearrange("p k v -> p v k"), ALU.subtract)\
                   .then_inc(s_clo, 1)
                def inverse_std():
                    dve.wait_ge(s_ss, 4)
                    dve.tensor_scalar(rstd[:], p_ss[:], 1.0 / D, NORM_EPS, ALU.mult, ALU.add).then_inc(s_ssall, 1)
                    dve.wait_ge(s_std, 1)
                    done(dve.reciprocal(rstd[:], rstd[:]))
                    dve.wait_ge(s_xst, 16)

                def normalise_quarter(q):
                    dve.tensor_tensor(fm[:, 4 * q:4 * q + 4, :], fm[:, 4 * q:4 * q + 4, :],
                                      rstd[:].unsqueeze(1).broadcast_to([P, 4, TOK]), ALU.mult).then_inc(s_nrm, 1)

                def row(r, h, used, at):
                    dve.wait_ge(ring.used, used)
                    dve.tensor_copy(rows[:, h, :], p_row[h][0:4, :]).then_inc(s_rowc, 1)
                    dve.wait_ge(s_modp, r + 1)
                    dve.tensor_copy(modv[:, bass.ds(at, 4), :],
                                    p_col[:, 0:8].rearrange("p (f v) -> p f v", v=2)).then_inc(s_modc, 1)

                def body(i):
                    for h in range(2):
                        for m in range(4 * h, 4 * h + 4, 2):
                            ring.split_lo(dve, m, tile_no(i, 8, m))
                            if isinstance(i, int) and i == 0 and m == 0:
                                for b in range(8, 16):
                                    evac(b)
                            if isinstance(i, int) and i == 1:
                                normalise_quarter(m // 2)
                        if not (isinstance(i, int) and i == 0 and h == 0):
                            row(i * 2 + (h - 1), 1 - h, i * 8 + 4 * h, i * 8 + 4 * (h - 1))
                    if isinstance(i, int) and i == 0:
                        inverse_std()
                body(0)
                body(1)
                with dve.Fori(2, NB) as i:
                    body(i)
                row(2 * NB - 1, 1, 8 * NB, 8 * NB - 4)
                dve.wait_ge(s_modc, 2 * NB)
                done(dve.tensor_tensor(modv[:, 0:LATE, :], modv[:, 0:LATE, :], col("ada_b", 0, LATE).unsqueeze(2)
                                       .broadcast_to([P, LATE, 2]), ALU.add))
                done(dve.tensor_scalar(gain[:], modv[:, KT:2 * KT, :], 1.0, None, ALU.add))
                dve.tensor_tensor(gain[:], gain[:], col("norm_pre_mix", 0, KT).unsqueeze(2)
                                  .broadcast_to([P, KT, 2]), ALU.mult).then_inc(s_gain, 1)
                dve.wait_ge(s_gain, 1)
                dve.wait_ge(s_nrm, 4)
                for k in range(KT):
                    if k >= 2:
                        dve.wait_ge(s_hlo if k % 2 else s_hl, k // 2)
                    for v, lo in ((1, 0), (0, CTX)):
                        last = dve.tensor_scalar(hbuf[:, k % 2, lo:lo + CTX], fm[:, k, lo:lo + CTX],
                                                 gain[:, k, v:v + 1], modv[:, k, v:v + 1], ALU.mult, ALU.add)
                    last.then_inc(s_h, 1)
                    if k % 2 == 0:
                        low(dve, k, s_hl)


W_IN_SEGMENTS = [(0, 4, True, T_R), (RW, 8, False, T_K), (RWKV_IN, 2, True, T_GQ),
                 (RWKV_IN + GQW, 6, False, T_GK), (RWKV_IN + 2 * GQW + GVW, 4, True, T_GG),
                 (MIX_IN, 16, True, T_GATE)]


def first_w_in(A):
    w, c0 = A["w_in"].rearrange("a (k p) n -> p (a k) n", p=P), W_IN_SEGMENTS[0][0]
    return [w[:, KH * (m % 2):KH * (m % 2) + KH, c0 + 256 * (m // 2):c0 + 256 * (m // 2 + 1)]
            for m in range(RAW)], (KH, 256)


def phase_w_in(nc, A, env):
    alloc, psum, sem, Ring = (env[k] for k in ("alloc", "psum", "sem", "Ring"))
    h_hi, h_lo, px = env["h_hi"], env["h_lo"], env["px"]
    tile_no, bodies, mm3 = env["tile_no"], env["bodies"], env["mm3"]
    s_evac = sem("w_in_group_copied")
    s_out = [sem(f"w_in_group_stored{g}") for g in range(2)]
    w = A["w_in"].rearrange("a (k p) n -> p (a k) n", p=P)
    n_bodies = sum(s[1] for s in W_IN_SEGMENTS) // 2
    with ExitStack() as st:
        ring = Ring(st, "p", env["raw"], LATE * P // 512 * 4)
        stage = alloc(st, "stage", [P, 2, 2, TOK])
        pp = [psum(st, f"p_in{g}", 2 * TOK) for g in range(2)]

        def segments(eng, body):
            before, prev = 0, None
            for seg in W_IN_SEGMENTS:
                n = seg[1] // 2
                bodies(eng, n, lambda i: body(seg, i, before, prev), True)
                prev = (seg, n - 1, before)
                before += n
            return prev

        def start(i, before):
            return isinstance(i, int) and i + before == 0

        def toks(seg):
            return slice(CTX, TOK) if seg[2] else slice(0, TOK)

        with nc.Block() as block:

            @block.sync
            def _(sp):
                def body(seg, i, before, prev):
                    for m in range(4):
                        src = w[:, KH * (m % 2):KH * (m % 2) + KH, bass.ds(i * 512 + (seg[0] + 256 * (m // 2)), 256)]
                        ring.load(sp, src, m, tile_no(i, 4, m + 4 * before), (KH, 256))
                segments(sp, body)
                for n in range(6):
                    t = 4 * n_bodies + n
                    ring.load(sp, w[:, :, LORA_COLS[n]:LORA_COLS[n] + LORA], t, t, (KT, LORA))

            @block.scalar
            def _(act):
                def store_lora(n):
                    act.wait_ge(s_evac, 2 * n_bodies + n + 1)
                    act.dma_start(px[T_LORA + n, 0:LORA, :], stage[0:LORA, n % 2, 0, :]).then_inc(s_out[n % 2], 16)

                def store(seg, i, before, g, back=0):
                    act.wait_ge(s_evac, i * 2 + (2 * (before - back) + g + 1))
                    act.dma_start(px[bass.ds(i * 4 + (seg[3] + 2 * g - 4 * back), 2), :, toks(seg)]
                                  .rearrange("f p t -> p f t"), stage[:, g, :, toks(seg)]).then_inc(s_out[g], 16)

                def body(seg, i, before, prev):
                    for m in range(4):
                        ring.split_hi(act, m, tile_no(i, 4, m + 4 * before))
                        if m == 1 and not (isinstance(i, int) and i == 0):
                            store(seg, i, before, 1, 1)
                        elif m == 1 and prev:
                            store(*prev, 1)
                    store(seg, i, before, 0)
                store(*segments(act, body), 1)
                for n in range(6):
                    t = 4 * n_bodies + n
                    ring.split_hi(act, t, t, KT * LORA)
                    if n:
                        store_lora(n - 1)
                store_lora(5)
                for g in range(2):
                    act.wait_ge(s_out[g], 16 * (n_bodies + 3))

            @block.gpsimd
            def _(pool):
                def body(seg, i, before, prev):
                    for m in (1, 3):
                        ring.split_lo(pool, m, tile_no(i, 4, m + 4 * before))
                segments(pool, body)
                for n in (1, 3, 5):
                    t = 4 * n_bodies + n
                    ring.split_lo(pool, t, t, KT * LORA)

            @block.vector
            def _(dve):
                def copy(seg, i, before, g, back=0):
                    b = before - back
                    dve.wait_ge(ring.used, i * 4 + (4 * b + 2 * g + 2))
                    if not start(i, b):
                        dve.wait_ge(s_out[g], i * 16 + 16 * b)
                    dve.tensor_copy(stage[:, g, :, toks(seg)], pp[g][:].rearrange("p (f t) -> p f t", f=2)
                                    [:, :, toks(seg)]).then_inc(s_evac, 1)

                def body(seg, i, before, prev):
                    ring.split_lo(dve, 0, tile_no(i, 4, 4 * before))
                    if not (isinstance(i, int) and i == 0):
                        copy(seg, i, before, 1, 1)
                    elif prev:
                        copy(*prev, 1)
                    ring.split_lo(dve, 2, tile_no(i, 4, 2 + 4 * before))
                    copy(seg, i, before, 0)
                copy(*segments(dve, body), 1)
                for n in range(6):
                    t = 4 * n_bodies + n
                    if n % 2 == 0:
                        ring.split_lo(dve, t, t, KT * LORA)
                    dve.wait_ge(ring.used, t + 1)
                    dve.wait_ge(s_out[n % 2], 16 * (n_bodies + n // 2))
                    dve.tensor_copy(stage[0:LORA, n % 2, 0, :], pp[n % 2][0:LORA, 0:TOK]).then_inc(s_evac, 1)

            @block.tensor
            def _(pe):
                def body(seg, i, before, prev):
                    ts = toks(seg)
                    for g in range(2):
                        if not start(i, before):
                            pe.wait_ge(s_evac, i * 2 + (2 * before + g - 1))
                        for q in range(2):
                            m = 2 * g + q
                            ring.wait_split(pe, m, tile_no(i, 4, m + 4 * before))
                            s = m % ring.S
                            for f in range(2):
                                o = pp[g][:, f * TOK + ts.start:(f + 1) * TOK]
                                for k in range(KH):
                                    at = slice(k * 256 + f * P, k * 256 + (f + 1) * P)
                                    kk = KH * q + k
                                    last = mm3(pe, o, ring.hi[:, s, at], ring.lo[:, s, at], h_hi[:, kk, ts],
                                               h_lo[:, kk, ts], kk == 0, kk == KT - 1)
                            last.then_inc(ring.used, 1)
                segments(pe, body)
                for n in range(6):
                    t = 4 * n_bodies + n
                    pe.wait_ge(s_evac, 2 * n_bodies + n - 1)
                    ring.wait_split(pe, t, t)
                    for k in range(KT):
                        at = slice(k * LORA, (k + 1) * LORA)
                        last = mm3(pe, pp[n % 2][0:LORA, 0:TOK], ring.hi[:, t % ring.S, at],
                                   ring.lo[:, t % ring.S, at], h_hi[:, k, :], h_lo[:, k, :], k == 0, k == KT - 1)
                    last.then_inc(ring.used, 1)


class LateModulation:
    CW, KS, SLOTS = 512, 2, 4
    PER = KT // KS

    def __init__(self, st, env, A, tag, first, bank):
        alloc, sem = env["alloc"], env["sem"]
        self.w = A["ada_w"].rearrange("a (k p) n -> p (a k) n", p=P)
        self.c, self.mod_d, self.first, self.bank = env["siluc"], env["mod_d"], first, bank
        self.raw = alloc(st, f"{tag}_ada", [P, self.SLOTS, self.KS, self.CW])
        self.row = alloc(st, f"{tag}_ada_row", [1, 2, self.CW])
        self.landed = [sem(f"{tag}_ada_landed{n}") for n in range(self.SLOTS)]
        self.used, self.copied = sem(f"{tag}_ada_used"), sem(f"{tag}_ada_row_copied")
        self.stored = [sem(f"{tag}_ada_row_stored{n}") for n in range(2)]

    def load(self, eng, t0, n):
        for t in range(t0, t0 + n):
            r, q, s = t // self.PER, t % self.PER, t % self.SLOTS
            if t >= self.SLOTS:
                eng.wait_ge(self.used, t - self.SLOTS + 1)
            at = LATE * P + (self.first + r) * self.CW
            eng.dma_start(self.raw[:, s], self.w[:, self.KS * q:self.KS * (q + 1), at:at + self.CW])\
               .then_inc(self.landed[s], 16)

    def multiply(self, pe, t0, n):
        for t in range(t0, t0 + n):
            r, q, s = t // self.PER, t % self.PER, t % self.SLOTS
            if q == 0 and r:
                pe.wait_ge(self.copied, r)
            pe.wait_ge(self.landed[s], 16 * (t // self.SLOTS + 1))
            for k in range(self.KS):
                kk = self.KS * q + k
                last = pe.matmul(self.bank[0:1, :], self.c[:, 0, kk:kk + 1], self.raw[:, s, k], start=kk == 0,
                                 stop=kk == KT - 1)
            last.then_inc(self.used, 1)

    def wait_row(self, eng, r):
        eng.wait_ge(self.used, self.PER * (r + 1))
        if r >= 2:
            eng.wait_ge(self.stored[r % 2], 16 * (r // 2))

    def copy_act(self, act, r):
        self.wait_row(act, r)
        act.activation(self.row[:, r % 2], self.bank[0:1, :], ACT.Copy).then_inc(self.copied, 1)

    def copy_dve(self, dve, r):
        self.wait_row(dve, r)
        dve.tensor_copy(self.row[:, r % 2], self.bank[0:1, :]).then_inc(self.copied, 1)

    def store(self, eng, r):
        eng.wait_ge(self.copied, r + 1)
        at = (self.first + r) * self.CW
        eng.dma_start(self.mod_d[:, at:at + self.CW], self.row[:, r % 2]).then_inc(self.stored[r % 2], 16)

    def finish(self, eng, rows):
        for n in range(2):
            eng.wait_ge(self.stored[n], 16 * ((rows + 1 - n) // 2))


def phase_rwkv_pre(nc, A, out, env):
    alloc, psum, sem, col, px = (env[k] for k in ("alloc", "psum", "sem", "col", "px"))
    shared_d, r_d, dir_d, post_d = (env[k] for k in ("shared_d", "r_d", "dir_d", "post_d"))
    head_ones, one_minus_mu, half_mu, one_minus_ka = (env[k] for k in
                                                      ("head_ones", "one_minus_mu", "half_mu", "one_minus_ka"))
    s_zero = sem("r_edges_zero")
    s_w = sem("r_lora_weights_landed")
    s_lx = sem("r_lora_inputs_landed")
    s_in = [sem(f"r_pair_landed{n}") for n in range(2)]
    s_nb = sem("r_lora_neighbours_added")
    s_mid = sem("r_lora_middle_scaled")
    s_lmix = sem("r_lora_shifted")
    s_lact = sem("r_lora_activated")
    s_nk, s_mk, s_mix = sem("r_neighbours_added"), sem("r_middle_scaled"), sem("r_shifted")
    s_nr = sem("r_r_neighbours_added")
    s_kx, s_sq, s_ss, s_mx, s_nrm = (sem(f"r_{n}") for n in
                                     ("k_scaled", "k_squared", "k_square_sums", "norm_floored", "norm_ready"))
    s_inv = sem("r_norm_inverted")
    s_kk = sem("r_kk_ready")
    s_z, s_sg = sem("r_lora_products"), sem("r_sigmoids")
    s_lw, s_u, s_nak, s_kd, s_ks = (sem(f"r_{n}") for n in
                                    ("log_decay_ready", "k_factor_ready", "rate_ready", "kd_ready", "kd_summed"))
    s_rk, s_bp, s_post = (sem(f"r_{n}") for n in
                               ("bonus_terms", "bonus_and_gate_products", "bonus_and_gate_ready"))
    s_st = [sem(f"r_pair_stored{n}") for n in range(2)]
    N_ST = 5

    with ExitStack() as st:
        w2 = alloc(st, "w2", [LORA, 2, RW])
        a2 = alloc(st, "a2", [LORA, 2, RW])
        g2 = alloc(st, "g2", [GLORA, RW])
        lpad = alloc(st, "lora_pad", [LORA, 5, 2, SEQ + 2])
        lnb = alloc(st, "lora_nb", [LORA, 5, 2, SEQ])
        lmid = alloc(st, "lora_mid", [LORA, 5, 2, SEQ])
        lx = alloc(st, "lora_x", [LORA, 5, TOK])
        pad = alloc(st, "pad", [P, 2, 2, 2, SEQ + 2])
        rpad = alloc(st, "rpad", [P, 2, SEQ + 2])
        nb = alloc(st, "nb", [P, 2, 2, 2, SEQ])
        mid = alloc(st, "mid", [P, 2, 2, 2, SEQ])
        rnb = alloc(st, "rnb", [P, 2, SEQ])
        rmid = alloc(st, "rmid", [P, 2, SEQ])
        kmix = alloc(st, "kmix", [P, 2, TOK])
        kx = alloc(st, "kx", [P, 2, TOK])
        ksq = alloc(st, "ksq", [P, 2, TOK])
        nrm = alloc(st, "nrm", [P, 2, TOK])
        sh = alloc(st, "sh", [P, 2, 2, TOK])
        rr = alloc(st, "rr", [P, 2, SEQ])
        sg = alloc(st, "sg", [P, 2, 2, 2, TOK])
        dr = alloc(st, "dr", [P, 2, 2, 3, TOK])
        u = alloc(st, "u", [P, 2, 2, TOK])
        ks = alloc(st, "ks", [P, 2, SEQ])
        post = alloc(st, "post", [P, 2, 2, SEQ])
        pz = [psum(st, f"pz{n}", TOK) for n in range(4)]
        pss = psum(st, "pss", TOK)
        pbonus = psum(st, "pbonus", SEQ)
        pgate = psum(st, "pgate", SEQ)
        late = LateModulation(st, env, A, "r", LATE_GLA, psum(st, "p_ada", 512))

        with nc.Block() as block:

            @block.sync
            def _(sp):
                for n in range(5):
                    sp.dma_start(lpad[:, n, :, 1:SEQ + 1], px[T_LORA + n, 0:LORA, :]
                                 .rearrange("p (s t) -> p s t", s=2)).then_inc(s_lx, 16)
                late.load(sp, 0, 4)
                sp.dma_start(w2[:], A["rwkv_w2"][0].rearrange("d k n -> k d n")).then_inc(s_w, 16)
                sp.dma_start(a2[:], A["rwkv_a2"][0].rearrange("d k n -> k d n")).then_inc(s_w, 16)
                sp.dma_start(g2[:], A["rwkv_g2"][0]).then_inc(s_w, 16)

                def load(j):
                    if j >= 2:
                        sp.wait_ge(s_mk, j - 1)
                        sp.wait_ge(s_nk, j - 1)
                        sp.wait_ge(s_nr, j - 1)
                    for n, t in enumerate((T_K, T_V)):
                        sp.dma_start(pad[:, j % 2, n, :, 1:SEQ + 1], px[t + j].rearrange("p (s t) -> p s t", s=2))\
                          .then_inc(s_in[j % 2], 16)
                    sp.dma_start(rpad[:, j % 2, 1:SEQ + 1], px[T_R + j, :, CTX:]).then_inc(s_in[j % 2], 16)

                def store(j):
                    b = j % 2
                    sp.wait_ge(s_kk, j + 1)
                    sp.wait_ge(s_mix, 3 * (j + 1))
                    sp.dma_start(shared_d.rearrange("p (a j) t -> p a j t", a=2)[:, :, j, :], sh[:, b])\
                      .then_inc(s_st[b], 16)
                    sp.dma_start(r_d[:, j, :], rr[:, b, :]).then_inc(s_st[b], 16)
                    sp.wait_ge(s_nak, 2 * (j + 1))
                    sp.wait_ge(s_kd, 2 * (j + 1))
                    sp.wait_ge(s_lw, 2 * (j + 1))
                    for d in range(2):
                        sp.dma_start(dir_d[d].rearrange("p (a j) t -> p a j t", a=3)[:, :, j, :], dr[:, b, d])\
                          .then_inc(s_st[b], 16)
                    sp.wait_ge(s_post, 2 * (j + 1))
                    sp.dma_start(post_d.rearrange("p (a j) t -> p a j t", a=2)[:, :, j, :], post[:, b])\
                      .then_inc(s_st[b], 16)
                load(0)
                load(1)
                for j in range(PAIRS):
                    if j + 2 < PAIRS:
                        load(j + 2)
                    late.load(sp, 8 * j + 4, 8 if j + 1 < PAIRS else 4)
                    store(j)
                    late.store(sp, j)
                late.finish(sp, PAIRS)
                for b in range(2):
                    sp.wait_ge(s_st[b], 16 * N_ST * PAIRS // 2)

            @block.gpsimd
            def _(pool):
                pool.wait_ge(s_zero, 2)
                pool.wait_ge(s_lx, 80)
                for n in range(5):
                    pool.tensor_tensor(lnb[:, n], lpad[:, n, :, 0:SEQ], lpad[:, n, :, 2:SEQ + 2], ALU.add)\
                        .then_inc(s_nb, 1)

                def neighbours(j):
                    b = j % 2
                    pool.wait_ge(s_in[b], 48 * (j // 2 + 1))
                    if j >= 2:
                        pool.wait_ge(s_mix, 3 * (j - 1))
                    for n in range(2):
                        last = pool.tensor_tensor(nb[:, b, n], pad[:, b, n, :, 0:SEQ], pad[:, b, n, :, 2:SEQ + 2],
                                                  ALU.add)
                    last.then_inc(s_nk, 1)
                neighbours(0)
                for j in range(PAIRS):
                    b = j % 2
                    if j >= 2:
                        pool.wait_ge(s_st[b], 16 * N_ST * (j // 2))
                    for d in range(2):
                        pool.wait_ge(s_sg, 4 * j + 2 * d + 1)
                        pool.tensor_scalar(dr[:, b, d, 0, :], sg[:, b, 0, d, :], -DECAY_TOP, None, ALU.mult)\
                            .then_inc(s_lw, 1)
                        pool.wait_ge(s_sg, 4 * j + 2 * d + 2)
                        if j >= 2:
                            pool.wait_ge(s_kd, 2 * (j - 1))
                        pool.tensor_scalar(u[:, b, d, :], sg[:, b, 1, d, :], col("rwkv_k_a", j), one_minus_ka[:, j:j + 1],
                                           ALU.mult, ALU.add).then_inc(s_u, 1)
                    if j + 1 < PAIRS:
                        neighbours(j + 1)

            @block.scalar
            def _(act):
                act.wait_ge(s_lx, 80)
                for n in range(5):
                    act.activation(lmid[:, n], lpad[:, n, :, 1:SEQ + 1], ACT.Copy,
                                   scale=one_minus_mu[0:LORA, 24 + n:25 + n]).then_inc(s_mid, 1)
                act.wait_ge(s_lmix, 5)
                act.activation(lx[:, 0:2, :], lx[:, 0:2, :], ACT.Tanh).then_inc(s_lact, 1)
                act.activation(lx[0:GLORA, 4, :], lx[0:GLORA, 4, :], ACT.Sigmoid).then_inc(s_lact, 1)

                def middle(j):
                    b = j % 2
                    act.wait_ge(s_in[b], 48 * (j // 2 + 1))
                    if j >= 2:
                        act.wait_ge(s_mix, 3 * (j - 1))
                    for n, m in enumerate((PAIRS + j, 2 * PAIRS + j)):
                        act.activation(mid[:, b, n], pad[:, b, n, :, 1:SEQ + 1], ACT.Copy,
                                       scale=one_minus_mu[:, m:m + 1])
                    act.activation(rmid[:, b, :], rpad[:, b, 1:SEQ + 1], ACT.Copy, scale=one_minus_mu[:, j:j + 1])\
                       .then_inc(s_mk, 1)
                middle(0)
                for j in range(PAIRS):
                    b = j % 2
                    act.wait_ge(s_kx, j + 1)
                    if j >= 2:
                        act.wait_ge(s_ss, j - 1)
                    act.activation(ksq[:, b, :], kx[:, b, :], ACT.Square).then_inc(s_sq, 1)
                    if j >= 2:
                        act.wait_ge(s_lw, 2 * (j - 1))
                        act.wait_ge(s_u, 2 * (j - 1))
                        act.wait_ge(s_nak, 2 * (j - 1))
                    for d in range(2):
                        for w, name in enumerate(("rwkv_w0", "rwkv_a0")):
                            act.wait_ge(s_z, 4 * j + 2 * d + w + 1)
                            act.activation(sg[:, b, w, d, :], pz[2 * w + d][:], ACT.Sigmoid,
                                           bias=col(name, d * PAIRS + j)).then_inc(s_sg, 1)
                    act.wait_ge(s_mx, j + 1)
                    act.activation(nrm[:, b, :], nrm[:, b, :], ACT.Sqrt).then_inc(s_nrm, 1)
                    act.wait_ge(s_bp, j + 1)
                    if j >= 2:
                        act.wait_ge(s_st[b], 16 * N_ST * (j // 2))
                    act.activation(post[:, b, 1, :], pgate[:, 0:SEQ], ACT.Copy).then_inc(s_post, 1)
                    late.copy_act(act, j)
                    if j + 1 < PAIRS:
                        middle(j + 1)

            @block.tensor
            def _(pe):
                late.multiply(pe, 0, 4)
                pe.wait_ge(s_w, 48)
                pe.wait_ge(s_lact, 2)
                for j in range(PAIRS):
                    b = j % 2
                    at = slice(j * P, (j + 1) * P)
                    for d in range(2):
                        for w, wt in enumerate((w2, a2)):
                            if j:
                                pe.wait_ge(s_sg, 4 * (j - 1) + 2 * d + w + 1)
                            pe.matmul(pz[2 * w + d][:], wt[:, d, at], lx[:, 2 * w + d, :], start=True, stop=True)\
                              .then_inc(s_z, 1)
                    if j:
                        late.multiply(pe, 8 * j, 4)
                    pe.wait_ge(s_sq, j + 1)
                    if j:
                        pe.wait_ge(s_mx, j)
                    pe.matmul(pss[:], head_ones[:], ksq[:, b, :], start=True, stop=True).then_inc(s_ss, 1)
                    late.multiply(pe, 8 * j + 4, 4)
                    pe.wait_ge(s_rk, j + 1)
                    if j:
                        pe.wait_ge(s_post, 2 * j)
                    pe.matmul(pbonus[:, 0:SEQ], head_ones[:], ks[:, b, :], start=True, stop=True)
                    pe.matmul(pgate[:, 0:SEQ], g2[:, at], lx[0:GLORA, 4, CTX:], start=True, stop=True).then_inc(s_bp, 1)

            @block.vector
            def _(dve):
                for n in range(2):
                    dve.memset(lpad[:, :, :, n * (SEQ + 1):n * (SEQ + 1) + 1], 0.0)
                    dve.memset(pad[:, :, :, :, n * (SEQ + 1):n * (SEQ + 1) + 1], 0.0)
                    dve.memset(rpad[:, :, n * (SEQ + 1):n * (SEQ + 1) + 1], 0.0).then_inc(s_zero, 1)
                dve.wait_ge(s_zero, 2)
                for n in range(5):
                    dve.wait_ge(s_nb, n + 1)
                    dve.wait_ge(s_mid, n + 1)
                    dve.scalar_tensor_tensor(out=lx[:, n, :], in0=lnb[:, n].rearrange("p s t -> p (s t)"),
                                             scalar=half_mu[0:LORA, 24 + n:25 + n],
                                             in1=lmid[:, n].rearrange("p s t -> p (s t)"),
                                             op0=ALU.mult, op1=ALU.add).then_inc(s_lmix, 1)
                for j in range(PAIRS):
                    b = j % 2
                    dve.wait_ge(s_nk, j + 1)
                    dve.tensor_tensor(rnb[:, b, :], rpad[:, b, 0:SEQ], rpad[:, b, 2:SEQ + 2], ALU.add).then_inc(s_nr, 1)
                    dve.wait_ge(s_mk, j + 1)
                    if j >= 2:
                        dve.wait_ge(s_st[b], 16 * N_ST * (j // 2))
                    for n, (o, m) in enumerate(((kmix[:, b, :], PAIRS + j), (sh[:, b, 1, :], 2 * PAIRS + j))):
                        dve.scalar_tensor_tensor(out=o, in0=nb[:, b, n].rearrange("p s t -> p (s t)"),
                                                 scalar=half_mu[:, m:m + 1],
                                                 in1=mid[:, b, n].rearrange("p s t -> p (s t)"),
                                                 op0=ALU.mult, op1=ALU.add).then_inc(s_mix, 1)
                    dve.wait_ge(s_nr, j + 1)
                    dve.scalar_tensor_tensor(out=rr[:, b, :], in0=rnb[:, b, :], scalar=half_mu[:, j:j + 1],
                                             in1=rmid[:, b, :], op0=ALU.mult, op1=ALU.add).then_inc(s_mix, 1)
                    dve.wait_ge(s_mix, 3 * j + 1)
                    dve.tensor_scalar(kx[:, b, :], kmix[:, b, :], col("rwkv_k_k", j), None, ALU.mult).then_inc(s_kx, 1)
                    dve.wait_ge(s_ss, j + 1)
                    dve.tensor_scalar(nrm[:, b, :], pss[:], 1e-24, None, ALU.max).then_inc(s_mx, 1)
                    for d in range(2):
                        dve.wait_ge(s_u, 2 * j + d + 1)
                        dve.tensor_tensor(dr[:, b, d, 2, :], u[:, b, d, :], kmix[:, b, :], ALU.mult).then_inc(s_kd, 1)
                    dve.wait_ge(s_kd, 2 * (j + 1))
                    dve.wait_ge(s_mix, 3 * (j + 1))
                    if j >= 2:
                        dve.wait_ge(s_bp, j - 1)
                    dve.tensor_tensor(ks[:, b, :], dr[:, b, 0, 2, CTX:], dr[:, b, 1, 2, CTX:], ALU.add).then_inc(s_ks, 1)
                    dve.wait_ge(s_ks, j + 1)
                    dve.scalar_tensor_tensor(out=ks[:, b, :], in0=ks[:, b, :], scalar=col("rwkv_r_k", j),
                                             in1=rr[:, b, :], op0=ALU.mult, op1=ALU.mult).then_inc(s_rk, 1)
                    dve.wait_ge(s_nrm, j + 1)
                    dve.reciprocal(nrm[:, b, :], nrm[:, b, :]).then_inc(s_inv, 1)
                    dve.wait_ge(s_inv, j + 1)
                    dve.tensor_tensor(sh[:, b, 0, :], kx[:, b, :], nrm[:, b, :], ALU.mult).then_inc(s_kk, 1)
                    dve.wait_ge(s_kk, j + 1)
                    for d in range(2):
                        dve.scalar_tensor_tensor(out=dr[:, b, d, 1, :], in0=sg[:, b, 1, d, :], scalar=-1.0,
                                                 in1=sh[:, b, 0, :], op0=ALU.mult, op1=ALU.mult).then_inc(s_nak, 1)
                    dve.wait_ge(s_bp, j + 1)
                    dve.tensor_tensor(post[:, b, 0, :], pbonus[:, 0:SEQ], sh[:, b, 1, CTX:], ALU.mult).then_inc(s_post, 1)


def phase_rwkv_scan(nc, A, out, env):
    alloc, psum, sem = (env[k] for k in ("alloc", "psum", "sem"))
    shared_d, r_d, dir_d, y_d = (env[k] for k in ("shared_d", "r_d", "dir_d", "y_d"))
    U8 = PAIRS
    LV = 5
    names = {}

    def sm(name, d):
        if (name, d) not in names:
            names[name, d] = sem(f"s_{name}_{'fb'[d]}")
        return names[name, d]

    with ExitStack() as st:
        masks = alloc(st, "masks", [P, 2, 2, C])
        y_sum = alloc(st, "y_sum", [P, U8, SEQ])
        masks_bd = alloc(st, "masks_bd", [P, 2, 8, 2, C])
        eye = env["ident"]

        def pair_of(name, shape, dt=f32):
            return [alloc(st, f"{name}_{x}", [P] + shape, dt) for x in "fb"]

        kkv = pair_of("kkv", [2, U8, C])
        rc = pair_of("rc", [U8, C])
        ldr = pair_of("ldr", [3, U8, C])
        b = pair_of("b", [U8, C])
        bm = pair_of("bm", [U8, C])
        es = pair_of("es", [U8, C])
        q12 = pair_of("q12", [U8, 2, C])
        q1_bd = pair_of("q1_bd", [U8, 2, C])
        s1_bd = pair_of("s1_bd", [U8, 2, C])
        s2_bd = pair_of("s2_bd", [U8, 2, C])
        w_bd = pair_of("w_bd", [U8, 2, C])
        t1_bd = pair_of("t1_bd", [U8, 2, C])
        n_bd = [pair_of(f"n_bd{n}", [U8, 2, C]) for n in range(2)]
        t2_bd = pair_of("t2_bd", [U8, 2, C])
        r1 = pair_of("r1", [U8, C])
        r2 = pair_of("r2", [U8, C])
        x_bd = pair_of("x_bd", [U8, 2, C])
        xt_bd = pair_of("xt_bd", [U8, 2, C])
        rhs = pair_of("rhs", [U8, C])
        vt = pair_of("vt", [U8, C])
        vt_bd = pair_of("vt_bd", [U8, P])
        s1t_bd = pair_of("s1t_bd", [U8, P])
        s2t_bd = pair_of("s2t_bd", [U8, P])
        u = pair_of("u", [U8, C])
        S = pair_of("S", [U8, C])
        s_bd = pair_of("s_bd", [U8, 2, C])
        e_end = pair_of("e_end", [U8])
        keep = alloc(st, "keep", [P, U8 * C])
        refs = alloc(st, "refs", [P, 2])
        pa = [psum(st, f"pa{d}", 2 * U8 * C) for d in range(2)]
        pb = [psum(st, f"pb{d}", 2 * U8 * C) for d in range(2)]
        W = U8 * C

        def halves(bd, h):
            return bd[64 * h:64 * h + 64, :, h, :]

        def flat(t):
            return t[:].rearrange("p u c -> p (u c)")

        def mask(n, d):
            return masks[:, d, n, :].unsqueeze(1).broadcast_to([P, U8, C])

        def mask_bd(n, d):
            return masks_bd[:, d, n].unsqueeze(1).broadcast_to([P, U8, 2, C])

        def twice(t):
            return t.unsqueeze(2).broadcast_to([P, U8, 2, C])

        def mask_half(n, d, h):
            return masks[64 * h:64 * h + 64, d, n, :].unsqueeze(1).broadcast_to([64, U8, C])
        STRICT, INCL = range(2)
        HEADS, LEVEL0_T, LEVEL0 = 5, 6, 7
        EYE_BD = eye[:].unsqueeze(1).broadcast_to([P, U8, P])

        def wide(t):
            return t[:].rearrange("p u h c -> p u (h c)")

        def level_banks(d, l):
            return (pa[d], pb[d]) if l % 2 else (pb[d], pa[d])

        def bank(p, n):
            return p[:, n * W:(n + 1) * W].rearrange("p (u c) -> p u c", u=U8)

        def both(p):
            return p[:].rearrange("p (u c) -> p u c", u=U8)

        def whole(c, n):
            return isinstance(c, int) and c == n

        def later(c):
            return not whole(c, 0)

        def later_x(c, x):
            return x and not whole(c, 4)

        def needs_bd(c, x):
            return whole(c, 3) or (x and not whole(c, 7))

        def half(step, d, last, c, lev):
            def go(name, at, *which):
                if at and name in step:
                    step[name](*at, *which)
            go("prepare", c, d)
            for l, after_a, after_b in ((1, "rhs", "u"), (2, "state", "output"), (3, "scores1", "scores2"),
                                        (4, "tokens", "flip1"), (5, "flip2", None)):
                if l == 3:
                    go("prepare2", c, d)
                go("grow_a", lev, 1 - d, l)
                go(after_a, last if l < 3 else c, d)
                go("grow_b", lev, 1 - d, l)
                go(after_b, last if l < 3 else c, d)

        def run(step):
            def body(c, before, x, bx):
                last = None if before is None else (before, bx)
                half(step, 0, last, (c, x), last)
                half(step, 1, last, (c, x), (c, x))
            eng = step["engine"]
            body(0, None, False, False)
            body(1, 0, False, False)
            with eng.Fori(2, 4) as i:
                body(i, i - 1, False, False)
            body(4, 3, True, False)
            body(5, 4, True, True)
            with eng.Fori(6, 8) as i:
                body(i, i - 1, True, True)
            half(step, 0, (7, True), None, (7, True))
            half(step, 1, (7, True), None, None)

        def clear(eng, d):
            for t in (s1_bd, q1_bd, w_bd, t1_bd, t2_bd, S, s_bd):
                eng.memset(t[d][:], 0.0).then_inc(sm("init", 1), 1)

        with nc.Block() as block:

            @block.sync
            def _(sp):
                sp.dma_start(masks[:], A["scan_masks"]).then_inc(sm("masks", 0), 16)
                sp.dma_start(masks_bd[:], A["scan_masks_bd"]).then_inc(sm("masks", 0), 16)

                def body(c, x):
                    for d in range(2):
                        at = c * C if d == 0 else (c * -C) + (11 if x else 3) * C
                        if x:
                            rat = (c * C) - 4 * C if d == 0 else (c * -C) + 7 * C
                        if later(c):
                            for n, count in (("v_bd", c * 2), ("s1_bd", c * 2), ("q1", c), ("s2_bd", c), ("bm", c)):
                                sp.wait_ge(sm(n, d), count)
                        sp.dma_start(kkv[d][:].rearrange("p a u t -> p (a u) t"), shared_d[:, :, bass.ds(at, C)])\
                          .then_inc(sm("in", d), 16)
                        sp.dma_start(ldr[d][:].rearrange("p a u t -> p (a u) t"), dir_d[d, :, :, bass.ds(at, C)])\
                          .then_inc(sm("in", d), 16)
                        if x:
                            if later_x(c, x):
                                sp.wait_ge(sm("q2", d), c - 4)
                            sp.dma_start(rc[d][:], r_d[:, :, bass.ds(rat, C)]).then_inc(sm("rin", d), 16)
                body(0, False)
                with sp.Fori(1, 4) as i:
                    body(i, False)
                body(4, True)
                with sp.Fori(5, 8) as i:
                    body(i, True)
                sp.wait_ge(sm("ysum", 0), 8)
                sp.dma_start(y_d, y_sum[:]).then_inc(sm("stored", 0), 16)
                sp.wait_ge(sm("stored", 0), 16)

            @block.vector
            def _(dve):
                dve.memset(keep[:], 1.0).then_inc(sm("init", 0), 1)
                dve.wait_ge(sm("init", 0), 1)
                dve.memset(keep[:].rearrange("p (u c) -> p u c", u=U8)[:, :, 0:1], 0.0).then_inc(sm("init", 0), 1)
                for n, v in ((0, REF), (1, -REF)):
                    dve.memset(refs[:, n:n + 1], v)
                clear(dve, 0)
                dve.wait_ge(sm("init", 0), 2)
                dve.wait_ge(sm("init", 1), 2 * 7 + 1)

                def prepare(c, x, d):
                    rev = slice(None, None, -1 if d else 1)
                    dve.wait_ge(sm("in", d), c * 32 + 32)
                    if later(c):
                        dve.wait_ge(sm("e2", d), c)
                    dve.tensor_tensor_scan(out=flat(b[d])[:, rev], data0=keep[:],
                                           data1=ldr[d][:, 0].rearrange("p u c -> p (u c)")[:, rev], initial=0.0,
                                           op0=ALU.mult, op1=ALU.add).then_inc(sm("b", d), 1)
                    dve.wait_ge(sm("b", d), c + 1)
                    dve.tensor_tensor(bm[d][:], b[d][:], ldr[d][:, 0], ALU.subtract).then_inc(sm("bm", d), 1)
                    dve.wait_ge(sm("es", d), c + 1)
                    if later(c):
                        dve.wait_ge(sm("t2r2", d), c)
                        dve.wait_ge(sm("q1_bd", d), c * 2)
                    dve.tensor_tensor(ldr[d][:, 1], ldr[d][:, 1], es[d][:], ALU.mult).then_inc(sm("s1", d), 1)
                    dve.wait_ge(sm("e1", d), c + 1)
                    dve.tensor_tensor(q12[d][:, :, 0, :], kkv[d][:, 0], bm[d][:], ALU.mult).then_inc(sm("q1", d), 1)

                def prepare2(c, x, d):
                    if x:
                        if later_x(c, x):
                            dve.wait_ge(sm("y", d), c - 4)
                        dve.wait_ge(sm("rin", d), c * 16 - 48)
                        dve.wait_ge(sm("e2", d), c + 1)
                        dve.tensor_tensor(q12[d][:, :, 1, :], rc[d][:], b[d][:], ALU.mult).then_inc(sm("q2", d), 1)

                def scores1(c, x, d):
                    p1 = pa[d][:].rearrange("p (u q c) -> p u q c", u=U8, q=2)
                    if whole(c, 0):
                        dve.wait_ge(sm("masks", 0), 32)
                    dve.wait_ge(sm("t1r1", d), c + 1)
                    if later(c):
                        dve.wait_ge(sm("n_bd", d), c * LV)
                    for h in range(2):
                        dve.tensor_tensor(halves(t1_bd[d], h), p1[64 * h:64 * h + 64, :, 0, :],
                                          mask_half(STRICT, d, h), ALU.mult).then_inc(sm("t1", d), 1)
                    if x:
                        dve.tensor_tensor(r1[d][:], p1[:, :, 1, :], mask(INCL, d), ALU.mult).then_inc(sm("r1", d), 1)

                def scores2(c, x, d):
                    p2 = pb[d][:].rearrange("p (u q c) -> p u q c", u=U8, q=2)
                    dve.wait_ge(sm("t2r2", d), c + 1)
                    for h in range(2):
                        dve.tensor_tensor(halves(t2_bd[d], h), p2[64 * h:64 * h + 64, :, 0, :],
                                          mask_half(STRICT, d, h), ALU.mult).then_inc(sm("t2", d), 1)
                    if x:
                        dve.tensor_tensor(r2[d][:], p2[:, :, 1, :], mask(INCL, d), ALU.mult).then_inc(sm("r2", d), 1)

                def flip1(c, x, d):
                    dve.wait_ge(sm("ntr", d), c + 1)
                    dve.tensor_tensor(wide(x_bd[d]), both(pb[d]), mask_bd(LEVEL0, d).rearrange("p u h c -> p u (h c)"),
                                      ALU.mult).then_inc(sm("xm", d), 1)
                    dve.wait_ge(sm("xm", d), c + 1)
                    dve.tensor_tensor(wide(x_bd[d]), wide(x_bd[d]), EYE_BD, ALU.add).then_inc(sm("x", d), 1)
                    dve.wait_ge(sm("xtm", d), c + 1)
                    dve.tensor_tensor(wide(xt_bd[d]), wide(xt_bd[d]), EYE_BD, ALU.add).then_inc(sm("xt", d), 1)

                def grow_a(c, x, d, l):
                    if l > 1:
                        dve.wait_ge(sm("xtr", d), c * (LV - 1) + (l - 1))
                        dve.tensor_copy(wide(xt_bd[d]), both(level_banks(d, l - 1)[0])).then_inc(sm("xtc", d), 1)

                def grow_b(c, x, d, l):
                    p_xt, p_x = level_banks(d, l)
                    if l < LV:
                        dve.wait_ge(sm("dx", d), c * (LV - 1) + l)
                        dve.tensor_tensor(wide(x_bd[d]), wide(x_bd[d]), both(p_x), ALU.add).then_inc(sm("x", d), 1)
                    else:
                        dve.wait_ge(sm("dxt", d), c + 1)
                        dve.tensor_tensor(wide(xt_bd[d]), wide(xt_bd[d]), both(p_xt), ALU.add)\
                            .then_inc(sm("inverse", d), 1)

                def state(c, x, d):
                    if whole(c, 7):
                        return
                    dve.wait_ge(sm("st", d), c + 1)
                    dve.tensor_tensor(S[d][:], S[d][:], bank(pa[d], 1), ALU.add).then_inc(sm("sadd", d), 1)
                    dve.wait_ge(sm("sadd", d), c + 1)
                    dve.wait_ge(sm("e_end", d), c + 1)
                    dve.tensor_tensor(S[d][:], S[d][:], e_end[d][:].unsqueeze(2).broadcast_to([P, U8, C]), ALU.mult)\
                       .then_inc(sm("S", d), 1)

                def output(c, x, d):
                    if x:
                        yat = y_sum[:, :, bass.ds((c * C) - 4 * C if d == 0 else (c * -C) + 7 * C, C)]
                        dve.wait_ge(sm("y", d), c - 3)
                        if d or later_x(c, x):
                            dve.wait_ge(sm("ysum", 0), c * 2 - 8 + d)
                        dve.tensor_tensor(yat, yat, bank(pb[d], 0), ALU.add).then_inc(sm("ysum", 0), 1)
                    if needs_bd(c, x):
                        dve.wait_ge(sm("S", d), c + 1)
                        for h in range(2):
                            dve.tensor_copy(halves(s_bd[d], h), S[d][64 * h:64 * h + 64]).then_inc(sm("s_bd", d), 1)
                run(dict(engine=dve, prepare=prepare, prepare2=prepare2, scores1=scores1, scores2=scores2,
                         flip1=flip1, grow_a=grow_a, grow_b=grow_b,
                         state=state, output=output))

            @block.scalar
            def _(act):
                act.wait_ge(sm("init", 1), 2 * 7 + 1)

                def prepare(c, x, d):
                    act.wait_ge(sm("b", d), c + 1)
                    if later(c):
                        act.wait_ge(sm("s1", d), c)
                        act.wait_ge(sm("s2_bd", d), c)
                    act.activation(es[d][:], b[d][:], ACT.Exp, bias=refs[:, 1:2], scale=-1.0).then_inc(sm("es", d), 1)
                    act.wait_ge(sm("bm", d), c + 1)
                    act.activation(bm[d][:], bm[d][:], ACT.Exp, bias=refs[:, 0:1]).then_inc(sm("e1", d), 1)
                    act.wait_ge(sm("s1", d), c + 1)
                    if later(c):
                        act.wait_ge(sm("s1tr", d), c)
                    for h in range(2):
                        act.activation(halves(s1_bd[d], h), ldr[d][64 * h:64 * h + 64, 1], ACT.Copy)\
                           .then_inc(sm("s1_bd", d), 1)

                def prepare2(c, x, d):
                    last = 0 if d else C - 1
                    if later(c):
                        act.wait_ge(sm("S", d), c)
                    act.activation(e_end[d][:].unsqueeze(2), b[d][:, :, last:last + 1], ACT.Exp)\
                       .then_inc(sm("e_end", d), 1)
                    act.wait_ge(sm("es", d), c + 1)
                    act.wait_ge(sm("e_end", d), c + 1)
                    act.activation(b[d][:], b[d][:], ACT.Exp, bias=refs[:, 0:1]).then_inc(sm("e2", d), 1)
                    act.wait_ge(sm("q1", d), c + 1)
                    if later(c):
                        act.wait_ge(sm("rhs", d), c)
                    for h in range(2):
                        act.activation(halves(q1_bd[d], h), q12[d][64 * h:64 * h + 64, :, 0, :], ACT.Copy)\
                           .then_inc(sm("q1_bd", d), 1)
                    if later_x(c, x):
                        act.wait_ge(sm("y", d), c - 4)
                    for h in range(2):
                        act.activation(halves(w_bd[d], h), kkv[d][64 * h:64 * h + 64, 1], ACT.Copy)\
                           .then_inc(sm("v_bd", d), 1)

                def tokens(c, x, d):
                    act.wait_ge(sm("vtr", d), c + 1)
                    act.activation(vt_bd[d][:], both(pa[d]), ACT.Copy).then_inc(sm("vt_bd", d), 1)
                    for h in range(2):
                        act.activation(vt[d][64 * h:64 * h + 64], both(pa[d])[64 * h:64 * h + 64, :, 64 * h:64 * h + 64],
                                       ACT.Copy).then_inc(sm("vt", d), 1)

                def flip1(c, x, d):
                    act.wait_ge(sm("s1tr", d), c + 1)
                    act.activation(s1t_bd[d][:], both(pa[d]), ACT.Copy).then_inc(sm("s1t", d), 1)

                def flip2(c, x, d):
                    act.wait_ge(sm("s2tr", d), c + 1)
                    act.activation(s2t_bd[d][:], both(pb[d]), ACT.Copy).then_inc(sm("s2t", d), 1)

                def grow_a(c, x, d, l):
                    act.wait_ge(sm("nx", d), c * LV + l)
                    act.activation(wide(w_bd[d]), both(level_banks(d, l)[0]), ACT.Copy).then_inc(sm("y_bd", d), 1)

                def rhs_copy(c, x, d):
                    act.wait_ge(sm("rhs", d), c + 1)
                    act.activation(rhs[d][:], bank(pb[d], 1), ACT.Copy).then_inc(sm("rhsc", d), 1)

                def u_step(c, x, d):
                    act.wait_ge(sm("u", d), c + 1)
                    act.activation(u[d][:], bank(pa[d], 0), ACT.Copy).then_inc(sm("uc", d), 1)
                    if x:
                        for h in range(2):
                            act.activation(halves(w_bd[d], h), bank(pa[d], 0)[64 * h:64 * h + 64], ACT.Copy)\
                               .then_inc(sm("u_bd", d), 1)
                run(dict(engine=act, prepare=prepare, prepare2=prepare2, tokens=tokens, flip1=flip1,
                         flip2=flip2, grow_a=grow_a,                         rhs=rhs_copy, u=u_step))

            @block.gpsimd
            def _(pool):
                clear(pool, 1)
                pool.memset(y_sum[:], 0.0).then_inc(sm("init", 1), 1)
                pool.wait_ge(sm("masks", 0), 32)

                def prepare(c, x, d):
                    pool.wait_ge(sm("es", d), c + 1)
                    pool.tensor_tensor(ldr[d][:, 2], ldr[d][:, 2], es[d][:], ALU.mult).then_inc(sm("s2", d), 1)
                    pool.wait_ge(sm("s2", d), c + 1)
                    if later(c):
                        pool.wait_ge(sm("s2tr", d), c)
                    pool.tensor_tensor(s2_bd[d][:], twice(ldr[d][:, 2]), mask_bd(HEADS, d), ALU.mult).then_inc(sm("s2_bd", d), 1)

                def block_of(c, d, l):
                    pool.tensor_tensor(n_bd[l % 2][d][:], t1_bd[d][:], mask_bd(l - 1, d), ALU.mult)\
                        .then_inc(sm("n_bd", d), 1)

                def tokens(c, x, d):
                    pool.wait_ge(sm("t1", d), c * 2 + 2)
                    if later(c):
                        pool.wait_ge(sm("u", d), c)
                    pool.tensor_tensor(xt_bd[d][:], t1_bd[d][:], mask_bd(LEVEL0_T, d), ALU.mult)\
                        .then_inc(sm("xtm", d), 1)
                    if later(c):
                        pool.wait_ge(sm("nx", d), c * LV)
                    for l in (1, 2):
                        block_of(c, d, l)

                def grow_a(c, x, d, l):
                    if l + 2 <= LV:
                        pool.wait_ge(sm("nx", d), c * LV + l)
                        block_of(c, d, l + 2)
                run(dict(engine=pool, prepare=prepare, tokens=tokens, grow_a=grow_a))

            @block.tensor
            def _(pe):
                pe.wait_ge(sm("init", 1), 2 * 7 + 1)

                def unit(t, d, j):
                    return t[d][:, j].rearrange("p h c -> p (h c)")

                def scores1(c, x, d):
                    n = 2 if x else 1
                    pe.wait_ge(sm("s1_bd", d), c * 2 + 2)
                    pe.wait_ge(sm("q1", d), c + 1)
                    if x:
                        pe.wait_ge(sm("q2", d), c - 3)
                    if later(c):
                        pe.wait_ge(sm("sadd", d), c)
                        pe.wait_ge(sm("uc", d), c)
                    if later_x(c, x):
                        pe.wait_ge(sm("u_bd", d), c * 2 - 8)
                    for j in range(U8):
                        last = pe.matmul(pa[d][:, j * P:j * P + n * C], unit(s1_bd, d, j),
                                         q12[d][:, j, 0:n, :].rearrange("p q c -> p (q c)"), start=True, stop=True)
                    last.then_inc(sm("t1r1", d), 1)

                def scores2(c, x, d):
                    n = 2 if x else 1
                    pe.wait_ge(sm("s2_bd", d), c + 1)
                    if later(c):
                        pe.wait_ge(sm("rhsc", d), c)
                    if later_x(c, x):
                        pe.wait_ge(sm("ysum", 0), c * 2 - 9 + d)
                    for j in range(U8):
                        last = pe.matmul(pb[d][:, j * P:j * P + n * C], unit(s2_bd, d, j),
                                         q12[d][:, j, 0:n, :].rearrange("p q c -> p (q c)"), start=True, stop=True)
                    last.then_inc(sm("t2r2", d), 1)

                def tokens(c, x, d):
                    pe.wait_ge(sm("v_bd", d), c * 2 + 2)
                    pe.wait_ge(sm("t1", d), c * 2 + 2)
                    if x:
                        pe.wait_ge(sm("r1", d), c - 3)
                    for j in range(U8):
                        last = pe.transpose(pa[d][:, j * P:(j + 1) * P], unit(w_bd, d, j), env["ident"][:])
                    last.then_inc(sm("vtr", d), 1)
                    pe.wait_ge(sm("t2", d), c * 2 + 2)
                    if x:
                        pe.wait_ge(sm("r2", d), c - 3)
                    for j in range(U8):
                        last = pe.transpose(pb[d][:, j * P:(j + 1) * P], unit(t1_bd, d, j), eye[:])
                    last.then_inc(sm("ntr", d), 1)

                def flip1(c, x, d):
                    pe.wait_ge(sm("vt_bd", d), c + 1)
                    pe.wait_ge(sm("vt", d), c * 2 + 2)
                    for j in range(U8):
                        last = pe.transpose(pa[d][:, j * P:(j + 1) * P], unit(s1_bd, d, j), env["ident"][:])
                    last.then_inc(sm("s1tr", d), 1)

                def flip2(c, x, d):
                    pe.wait_ge(sm("xm", d), c + 1)
                    for j in range(U8):
                        last = pe.transpose(pb[d][:, j * P:(j + 1) * P], unit(s2_bd, d, j), env["ident"][:])
                    last.then_inc(sm("s2tr", d), 1)

                def grow_a(c, x, d, l):
                    pe.wait_ge(sm("x", d), c * LV + l)
                    if l > 1:
                        for j in range(U8):
                            last = pe.transpose(level_banks(d, l - 1)[0][:, j * P:(j + 1) * P], unit(x_bd, d, j), eye[:])
                        last.then_inc(sm("xtr", d), 1)
                    pe.wait_ge(sm("n_bd", d), c * LV + l)
                    if l == 1:
                        pe.wait_ge(sm("s1t", d), c + 1)
                        pe.wait_ge(sm("s2t", d), c + 1)
                    for j in range(U8):
                        last = pe.matmul(level_banks(d, l)[0][:, j * P:(j + 1) * P], unit(n_bd[l % 2], d, j),
                                         unit(x_bd, d, j), start=True, stop=True)
                    last.then_inc(sm("nx", d), 1)

                def grow_b(c, x, d, l):
                    p_xt, p_x = level_banks(d, l)
                    if l == 1:
                        pe.wait_ge(sm("xt", d), c + 1)
                    else:
                        pe.wait_ge(sm("xtc", d), c * (LV - 1) + (l - 1))
                    pe.wait_ge(sm("y_bd", d), c * LV + l)
                    if l < LV:
                        for j in range(U8):
                            last = pe.matmul(p_x[:, j * P:(j + 1) * P], unit(xt_bd, d, j), unit(w_bd, d, j),
                                             start=True, stop=True)
                        last.then_inc(sm("dx", d), 1)
                    else:
                        for j in range(U8):
                            last = pe.matmul(p_xt[:, j * P:(j + 1) * P], unit(w_bd, d, j), unit(xt_bd, d, j),
                                             start=True, stop=True)
                        last.then_inc(sm("dxt", d), 1)

                def rhs_sum(c, x, d):
                    pe.wait_ge(sm("q1_bd", d), c * 2 + 2)
                    if later(c):
                        pe.wait_ge(sm("S", d), c)
                    for j in range(U8):
                        o = pb[d][:, W + j * C:W + (j + 1) * C]
                        pe.matmul(o, unit(q1_bd, d, j), S[d][:, j, :], start=True, stop=False)
                        last = pe.matmul(o, unit(t2_bd, d, j), vt[d][:, j, :], start=False, stop=True)
                    last.then_inc(sm("rhs", d), 1)

                def u_step(c, x, d):
                    pe.wait_ge(sm("inverse", d), c + 1)
                    pe.wait_ge(sm("rhsc", d), c + 1)
                    for j in range(U8):
                        last = pe.matmul(pa[d][:, j * C:(j + 1) * C], unit(xt_bd, d, j), rhs[d][:, j, :],
                                         start=True, stop=True)
                    last.then_inc(sm("u", d), 1)

                def state(c, x, d):
                    if whole(c, 7):
                        return
                    pe.wait_ge(sm("uc", d), c + 1)
                    for j in range(U8):
                        o = pa[d][:, W + j * C:W + (j + 1) * C]
                        pe.matmul(o, s2t_bd[d][:, j, :], vt[d][:, j, :], start=True, stop=False)
                        last = pe.matmul(o, s1t_bd[d][:, j, :], u[d][:, j, :], start=False, stop=True)
                    last.then_inc(sm("st", d), 1)

                def output(c, x, d):
                    if not x:
                        return
                    pe.wait_ge(sm("uc", d), c + 1)
                    pe.wait_ge(sm("u_bd", d), c * 2 - 6)
                    pe.wait_ge(sm("s_bd", d), c * 2 - 6)
                    for j in range(U8):
                        o = pb[d][:, j * C:(j + 1) * C]
                        pe.matmul(o, unit(s_bd, d, j), q12[d][:, j, 1, :], start=True, stop=False)
                        pe.matmul(o, vt_bd[d][:, j, :], r2[d][:, j, :], start=False, stop=False)
                        last = pe.matmul(o, unit(w_bd, d, j), r1[d][:, j, :], start=False, stop=True)
                    last.then_inc(sm("y", d), 1)
                run(dict(engine=pe, scores1=scores1, scores2=scores2, tokens=tokens, flip1=flip1, flip2=flip2,
                         grow_a=grow_a, grow_b=grow_b, rhs=rhs_sum,
                         u=u_step, state=state, output=output))


def phase_gla(nc, A, out, env):
    alloc, psum, sem, col, px = (env[k] for k in ("alloc", "psum", "sem", "col", "px"))
    ident, ones, yb_d = (env[k] for k in ("ident", "ones", "yb_d"))
    BT = SEQ // P
    LEVELS = 8
    VT = GVW // P
    ORDER = [(l, d) for l in range(LEVELS) for d in range(2)]
    (s_w, s_lx, s_q, s_k, s_v, s_g, s_zero, s_z, s_zc, s_abs, s_exp, s_ln, s_la, s_b, s_qp, s_kp, s_vp, s_vt, s_vtc,
     s_be, s_bx, s_kc, s_kt, s_ktc, s_S, s_Sc, s_qb, s_qbm, s_diff, s_e, s_Q, s_K, s_att, s_sel, s_sel2, s_o, s_oc,
     s_osq, s_oss, s_std, s_sqrt, s_rec, s_sig, s_silu, s_yb1, s_yb, s_st, s_v2, s_mask) = \
        [sem(f"g_{n}") for n in
         ("weights_landed", "lora_landed", "q_landed", "k_landed", "v_landed", "g_landed", "zeroed", "gate_products",
          "gates_copied", "abs", "exp", "ln", "log_decay", "cumulative", "q_ready", "k_ready", "v_permuted",
          "v_transposed", "v_tokens_ready", "to_end", "to_end_exp", "k_decayed", "k_transposed", "k_tokens_ready",
          "state_done", "state_ready", "from_start_exp", "q_decayed", "level_diff", "level_exp", "level_q", "level_k",
          "level_products", "level_selected", "cross_copied", "o_done", "o_copied", "o_squared", "o_square_sums",
          "o_meaned", "o_std", "o_rstd", "g_sigmoid", "g_silu", "y_scaled", "y_ready", "y_stored", "vector_step",
          "masks_landed")]

    def raster(t):
        return t.rearrange("p f (c r) -> p f r c", r=GRID_H)

    def colmajor(t):
        return t.rearrange("p f (r c) -> p f c r", c=GRID_W)

    with ExitStack() as st:
        up = alloc(st, "up", [2 * GLR, 2, GQW])
        lx = alloc(st, "g_lx", [2 * GLR, TOK])
        qr = alloc(st, "qr", [P, GH, SEQ])
        kr = alloc(st, "kr", [P, GH, TOK])
        vr = alloc(st, "vr", [P, VT, TOK])
        gr = alloc(st, "gr", [P, VT, SEQ])
        q = alloc(st, "q", [P, GH, SEQ])
        q_twice = alloc(st, "q_twice", [P, GH, SEQ])
        k = alloc(st, "k", [P, GH, SEQ])
        vp = alloc(st, "vp", [P, VT, SEQ])
        vt = alloc(st, "g_vt", [P, 2 * BT, GVW])
        zb = [alloc(st, f"zb{d}", [P, GH, TOK]) for d in range(2)]
        ez = alloc(st, "ez", [P, GH, TOK])
        keep = alloc(st, "g_keep", [P, GH, TOK])
        B = [alloc(st, f"B{d}", [P, GH, TOK]) for d in range(2)]
        kc = alloc(st, "kc", [P, GH, CTX])
        kct = alloc(st, "kct", [P, GH, BT, P])
        S = [alloc(st, f"g_S{d}", [P, GH, GV]) for d in range(2)]
        qb = [alloc(st, f"qb{d}", [P, GH, SEQ]) for d in range(2)]
        E = alloc(st, "E", [P, 2, GH, SEQ])
        Q = alloc(st, "Q", [P, 2, GH, SEQ])
        K = alloc(st, "K", [P, 2, GH, SEQ])
        att = ez[:].rearrange("p h (s t n) -> p h s t n", s=BT, t=BT)
        gm = alloc(st, "gm", [P, 2, 7, P])
        one = alloc(st, "one", [P, 1])
        o, osq, rec = vr[:, :, 0:SEQ], vr[:, :, SEQ:], kr[:, :, 0:SEQ]
        pl = [psum(st, f"pl{n}", 512) for n in range(4)]
        po = [psum(st, f"po{n}", 512) for n in range(4)]
        late = LateModulation(st, env, A, "g", 0, po[3])

        with nc.Block() as block:

            @block.sync
            def _(sp):
                sp.wait_ge(s_zero, 1)
                for d in range(2):
                    sp.dma_start(up[GLR * d:GLR * d + GLR, d, :], A["gla_alpha_up"][0, d]).then_inc(s_w, 16)
                sp.dma_start(lx[:], px[T_LORA + 5, 0:2 * GLR, :]).then_inc(s_lx, 16)

                def rows(t0, n, lo):
                    return px[t0:t0 + n, :, lo:].rearrange("f p t -> p f t")
                sp.dma_start(kr[:], rows(T_GK, GH, 0)).then_inc(s_k, 16)
                sp.dma_start(vr[:], rows(T_GV, VT, 0)).then_inc(s_v, 16)
                sp.dma_start(qr[:], rows(T_GQ, GH, CTX)).then_inc(s_q, 16)
                late.load(sp, 0, 4)
                sp.dma_start(gm[:], A["gla_masks"]).then_inc(s_mask, 16)
                sp.dma_start(gr[:], rows(T_GG, VT, CTX)).then_inc(s_g, 16)
                for n in range(LATE_GLA):
                    late.load(sp, 8 * n if n else 4, 8 if n else 4)
                    if n:
                        late.store(sp, n - 1)
                late.store(sp, LATE_GLA - 1)
                late.finish(sp, LATE_GLA)
                sp.wait_ge(s_yb, VT)
                sp.dma_start(yb_d, vp[:]).then_inc(s_st, 16)
                sp.wait_ge(s_st, 16)

            @block.gpsimd
            def _(pool):
                pool.wait_ge(s_k, 16)
                pool.tensor_copy(k[:].rearrange("p f (c r) -> p f c r", r=GRID_H), colmajor(kr[:, :, CTX:])).then_inc(s_kp, 1)
                pool.wait_ge(s_v, 16)
                pool.tensor_copy(vp[:].rearrange("p f (c r) -> p f c r", r=GRID_H), colmajor(vr[:, :, CTX:])).then_inc(s_vp, 1)
                for n, (l, d) in enumerate(ORDER):
                    pool.wait_ge(s_e, n + 1)
                    if n >= 2:
                        pool.wait_ge(s_att, n - 1)
                    pool.tensor_tensor(K[:, n % 2], k[:], E[:, n % 2], ALU.mult).then_inc(s_K, 1)

            @block.scalar
            def _(act):
                for n in range(2 * GH):
                    d, h = n // GH, n % GH
                    act.wait_ge(s_z, n + 1)
                    bias = col("gla_alpha_b", n)
                    act.activation(zb[d][:, h, 0:CTX], pl[n % 4][:, 0:CTX], ACT.Identity, bias=bias)
                    act.activation(zb[d][:, h, CTX:].rearrange("p (c r) -> p c r", r=GRID_H),
                                   pl[n % 4][:, CTX:].rearrange("p (r c) -> p c r", c=GRID_W), ACT.Identity,
                                   bias=bias).then_inc(s_zc, 1)
                act.wait_ge(s_v2, 3)
                for d in range(2):
                    act.wait_ge(s_zc, GH * (d + 1))
                    if d:
                        act.wait_ge(s_la, 1)
                    act.activation(ez[:], zb[d][:], ACT.Abs).then_inc(s_abs, 1)
                    act.wait_ge(s_abs, d + 1)
                    act.activation(ez[:], ez[:], ACT.Exp, scale=-1.0).then_inc(s_exp, 1)
                    act.wait_ge(s_exp, d + 1)
                    act.activation(ez[:], ez[:], ACT.Ln, bias=one[:]).then_inc(s_ln, 1)
                act.wait_ge(s_q, 16)
                for f in range(GH):
                    act.activation(q[:, f].rearrange("p (c r) -> p c r", r=GRID_H),
                                   qr[:, f].rearrange("p (r c) -> p c r", c=GRID_W), ACT.Copy, scale=float(GK) ** -0.5)
                    act.activation(q_twice[:, f].rearrange("p (c r) -> p c r", r=GRID_H),
                                   qr[:, f].rearrange("p (r c) -> p c r", c=GRID_W), ACT.Copy,
                                   scale=2 * float(GK) ** -0.5).then_inc(s_qp, 1)
                late.copy_act(act, 0)
                for n in range(2 * VT * BT // 4):
                    act.wait_ge(s_vt, n + 1)
                    blk, f = n // 2, 4 * (n % 2)
                    act.activation(vt[:, blk, f * P:(f + 4) * P], pl[n % 4][:], ACT.Copy).then_inc(s_vtc, 1)
                late.copy_act(act, 1)
                for d in range(2):
                    act.wait_ge(s_be, d + 1)
                    act.activation(kc[:], kc[:], ACT.Exp, scale=1 / GLA_TAU).then_inc(s_bx, 1)
                    act.activation(qb[d][:], B[d][:, :, CTX:], ACT.Exp, scale=1 / GLA_TAU).then_inc(s_qb, 1)
                    for n in range(2):
                        act.wait_ge(s_kt, 2 * d + n + 1)
                        act.activation(kct[:, 2 * n:2 * n + 2].rearrange("p f b s -> p (f b s)"), pl[n][:], ACT.Copy)\
                           .then_inc(s_ktc, 1)
                    for n in range(2):
                        act.wait_ge(s_S, 2 * d + n + 1)
                        act.activation(S[d][:, 2 * n:2 * n + 2, :].rearrange("p f v -> p (f v)"), pl[2 + n][:], ACT.Copy)\
                           .then_inc(s_Sc, 1)
                late.copy_act(act, 2)
                for n, (l, d) in enumerate(ORDER):
                    act.wait_ge(s_diff, n + 1)
                    act.activation(E[:, n % 2], E[:, n % 2], ACT.Exp, scale=1 / GLA_TAU).then_inc(s_e, 1)
                    if l == LEVELS - 1:
                        act.wait_ge(s_att, n + 1)
                        src, dst = (0, 1) if d == 0 else (1, 0)
                        act.activation(att[:, :, src, dst, :], pl[2 * (n % 2)][:].rearrange("p (h t) -> p h t", h=GH),
                                       ACT.Copy).then_inc(s_sel2, 1)
                for n in range(VT // 2):
                    act.wait_ge(s_o, n + 1)
                    act.activation(o[:, 2 * n:2 * n + 2, :], po[n][:].rearrange("p (f t) -> p f t", f=2), ACT.Copy)\
                       .then_inc(s_oc, 1)
                    act.wait_ge(s_oc, n + 1)
                    act.activation(osq[:, 2 * n:2 * n + 2, :], o[:, 2 * n:2 * n + 2, :], ACT.Square).then_inc(s_osq, 1)
                act.wait_ge(s_std, GH)
                act.activation(rec, rec, ACT.Sqrt).then_inc(s_sqrt, 1)
                act.wait_ge(s_g, 16)
                act.activation(vp[:], gr[:], ACT.Sigmoid).then_inc(s_sig, 1)

            @block.vector
            def _(dve):
                step = [0]

                def done(ins):
                    step[0] += 1
                    ins.then_inc(s_v2, 1)
                    dve.wait_ge(s_v2, step[0])
                dve.memset(up[:], 0.0).then_inc(s_zero, 1)
                done(dve.memset(keep[:], 1.0))
                done(dve.memset(keep[:].rearrange("p h (s t) -> p (h s) t", s=2)[:, :, 0:1], 0.0))
                done(dve.memset(one[:], 1.0))
                for d in range(2):
                    dve.wait_ge(s_ln, d + 1)
                    dve.scalar_tensor_tensor(out=zb[d][:].rearrange("p h t -> p (h t)"),
                                             in0=zb[d][:].rearrange("p h t -> p (h t)"), scalar=0.0,
                                             in1=ez[:].rearrange("p h t -> p (h t)"), op0=ALU.min, op1=ALU.subtract)\
                       .then_inc(s_la, 1)
                    dve.wait_ge(s_la, d + 1)
                    rev = slice(None, None, -1 if d else 1)
                    dve.tensor_tensor_scan(out=B[d][:].rearrange("p h t -> p (h t)")[:, rev],
                                           data0=keep[:].rearrange("p h t -> p (h t)"),
                                           data1=zb[d][:].rearrange("p h t -> p (h t)")[:, rev], initial=0.0,
                                           op0=ALU.mult, op1=ALU.add).then_inc(s_b, 1)
                for d in range(2):
                    end = 0 if d else CTX - 1
                    dve.wait_ge(s_b, d + 1)
                    if d:
                        dve.wait_ge(s_kt, 2)
                    dve.tensor_tensor(kc[:], B[d][:, :, end:end + 1].broadcast_to([P, GH, CTX]), B[d][:, :, 0:CTX],
                                      ALU.subtract).then_inc(s_be, 1)
                    dve.wait_ge(s_bx, d + 1)
                    dve.wait_ge(s_k, 16)
                    dve.tensor_tensor(kc[:], kc[:], kr[:, :, 0:CTX], ALU.mult).then_inc(s_kc, 1)
                    dve.wait_ge(s_qb, d + 1)
                    dve.wait_ge(s_qp, GH)
                    dve.tensor_tensor(qb[d][:], qb[d][:], q[:], ALU.mult).then_inc(s_qbm, 1)

                def diff(n):
                    l, d = ORDER[n]
                    m = 1 << l
                    if n >= 2:
                        dve.wait_ge(s_K, n - 1)
                        dve.wait_ge(s_Q, n - 1)
                    x = B[d][:, :, CTX:].rearrange("p h (n two m) -> p h n two m", two=2, m=m)
                    e = E[:, n % 2].rearrange("p h (n two m) -> p h n two m", two=2, m=m)
                    earlier, later = (1, 0) if d else (0, 1)
                    ref = x[:, :, :, 1, 0:1] if d else x[:, :, :, 0, m - 1:m]
                    ref = ref.broadcast_to([P, GH, SEQ // (2 * m), m])
                    dve.tensor_tensor(e[:, :, :, later, :], x[:, :, :, later, :], ref, ALU.subtract)
                    dve.tensor_tensor(e[:, :, :, earlier, :], ref, x[:, :, :, earlier, :], ALU.subtract).then_inc(s_diff, 1)

                def select(n, mask):
                    dve.wait_ge(s_att, n + 1)
                    if n:
                        dve.wait_ge(s_sel, 2 * min(n, 2 * (LEVELS - 1)))
                    for blk in range(BT):
                        dve.copy_predicated(att[:, :, blk, blk, :], mask, pl[2 * (n % 2) + blk][:]
                                            .rearrange("p (h t) -> p h t", h=GH)).then_inc(s_sel, 1)
                dve.memset(ez[:], 0.0).then_inc(s_zero, 1)
                diff(0)
                dve.wait_ge(s_mask, 16)
                dve.wait_ge(s_zero, 2)
                for n, (l, d) in enumerate(ORDER):
                    if n + 1 < len(ORDER):
                        diff(n + 1)
                    dve.wait_ge(s_e, n + 1)
                    if n >= 2:
                        dve.wait_ge(s_att, n - 1)
                    dve.tensor_tensor(Q[:, n % 2], q[:], E[:, n % 2], ALU.mult).then_inc(s_Q, 1)
                    if n and n % 8 == 0:
                        late.copy_dve(dve, n // 8 + 2)
                    if n >= 1 and n - 1 < 2 * (LEVELS - 1):
                        pl_, pd = ORDER[n - 1]
                        select(n - 1, gm[:, pd, pl_, :].bitcast(mybir.dt.uint32).unsqueeze(1).broadcast_to([P, GH, P]))
                late.copy_dve(dve, LATE_GLA - 1)
                select(len(ORDER), ident[:].bitcast(mybir.dt.uint32).unsqueeze(1).broadcast_to([P, GH, P]))
                for h in range(GH):
                    dve.wait_ge(s_oss, h + 1)
                    dve.tensor_scalar(rec[:, h, :], pl[h][:, 0:SEQ], 1.0 / GV, GLA_EPS, ALU.mult, ALU.add).then_inc(s_std, 1)
                dve.wait_ge(s_sqrt, 1)
                dve.reciprocal(rec, rec).then_inc(s_rec, 1)
                dve.wait_ge(s_sig, 1)
                dve.tensor_tensor(gr[:], gr[:], vp[:], ALU.mult).then_inc(s_silu, 1)
                dve.wait_ge(s_rec, 1)
                for f in range(VT):
                    dve.scalar_tensor_tensor(out=o[:, f, :], in0=o[:, f, :], scalar=col("gla_norm_g", f),
                                             in1=rec[:, f // 2, :], op0=ALU.mult, op1=ALU.mult).then_inc(s_yb1, 1)
                dve.wait_ge(s_silu, 1)
                for f in range(VT):
                    dve.wait_ge(s_yb1, f + 1)
                    dve.tensor_tensor(vp[:, f, :].rearrange("p (r c) -> p r c", c=GRID_W),
                                      o[:, f, :].rearrange("p (c r) -> p r c", r=GRID_H),
                                      gr[:, f, :].rearrange("p (r c) -> p r c", c=GRID_W), ALU.mult).then_inc(s_yb, 1)

            @block.tensor
            def _(pe):
                pe.wait_ge(s_w, 32)
                pe.wait_ge(s_lx, 16)
                for n in range(2 * GH):
                    if n >= 4:
                        pe.wait_ge(s_zc, n - 3)
                    pe.matmul(pl[n % 4][:], up[:, n // GH, (n % GH) * P:(n % GH + 1) * P], lx[:], start=True, stop=True)\
                      .then_inc(s_z, 1)
                late.multiply(pe, 0, 8)
                pe.wait_ge(s_v, 16)
                for n in range(2 * VT * BT // 4):
                    pe.wait_ge(s_zc, 2 * GH)
                    if n >= 4:
                        pe.wait_ge(s_vtc, n - 3)
                    if n == 4:
                        pe.wait_ge(s_vp, 1)
                    blk, f0 = n // 2, 4 * (n % 2)
                    for f in range(4):
                        src = vr[:, f0 + f, blk * P:(blk + 1) * P] if blk < BT else vp[:, f0 + f, (blk - BT) * P:(blk - BT + 1) * P]
                        last = pe.transpose(pl[n % 4][:, f * P:(f + 1) * P], src, ident[:])
                    last.then_inc(s_vt, 1)
                    late.multiply(pe, 8 + n, 1)
                pe.wait_ge(s_vtc, 2 * VT * BT // 4)
                for d in range(2):
                    pe.wait_ge(s_kc, d + 1)
                    if d:
                        pe.wait_ge(s_ktc, 2)
                    for n in range(2):
                        for i in range(4):
                            h, b = 2 * n + i // 2, i % 2
                            last = pe.transpose(pl[n][:, i * P:(i + 1) * P], kc[:, h, b * P:(b + 1) * P], ident[:])
                        last.then_inc(s_kt, 1)
                    late.multiply(pe, 16 + 4 * d, 2)
                    pe.wait_ge(s_ktc, 2 * d + 2)
                    if d:
                        pe.wait_ge(s_Sc, 2)
                    for n in range(2):
                        for i in range(2):
                            h = 2 * n + i
                            for b in range(BT):
                                last = pe.matmul(pl[2 + n][:, i * GV:(i + 1) * GV], kct[:, h, b, :],
                                                 vt[:, b, h * GV:(h + 1) * GV], start=b == 0, stop=b == BT - 1)
                        last.then_inc(s_S, 1)
                    late.multiply(pe, 18 + 4 * d, 2)
                pe.wait_ge(s_Sc, 4)

                def level(n, kk, qq, cross):
                    if n >= 2:
                        pe.wait_ge(s_sel, 2 * min(n - 1, 2 * (LEVELS - 1)))
                    if n >= 2 * (LEVELS - 1) + 2:
                        pe.wait_ge(s_sel2, 1)
                    blocks = ([(0, 1), (1, 0)][cross[1]],) if cross else ((0, 0), (1, 1))
                    for i, (sb, tb) in enumerate(blocks):
                        for h in range(GH):
                            last = pe.matmul(pl[2 * (n % 2) + i][:, h * P:(h + 1) * P], kk[:, h, sb * P:(sb + 1) * P],
                                             qq[:, h, tb * P:(tb + 1) * P], start=True, stop=True)
                    last.then_inc(s_att, 1)
                for n, (l, d) in enumerate(ORDER):
                    late.multiply(pe, 24 + n, 1)
                    pe.wait_ge(s_Q, n + 1)
                    pe.wait_ge(s_K, n + 1)
                    level(n, K[:, n % 2], Q[:, n % 2], (True, d) if l == LEVELS - 1 else None)
                pe.wait_ge(s_qp, GH)
                level(len(ORDER), k[:], q_twice[:], None)
                pe.wait_ge(s_sel, 2 * (2 * (LEVELS - 1) + 1))
                pe.wait_ge(s_sel2, 2)
                pe.wait_ge(s_qbm, 2)
                for f in range(VT):
                    h, at = f // 2, slice(f * P, (f + 1) * P)
                    dst = po[f // 2][:, (f % 2) * SEQ:(f % 2 + 1) * SEQ]
                    for b in range(BT):
                        pe.matmul(dst, vt[:, BT + b, at], att[:, h, b].rearrange("p b t -> p (b t)"),
                                  start=b == 0, stop=False)
                    for d in range(2):
                        last = pe.matmul(dst, S[d][:, h, (f % 2) * P:(f % 2 + 1) * P], qb[d][:, h, :],
                                         start=False, stop=d == 1)
                    if f % 2:
                        last.then_inc(s_o, 1)
                for h in range(GH):
                    pe.wait_ge(s_osq, h + 1)
                    for f in range(2):
                        last = pe.matmul(pl[h][:, 0:SEQ], ones[:], osq[:, 2 * h + f, :], start=f == 0, stop=f == 1)
                    last.then_inc(s_oss, 1)


def phase_branches(nc, A, out, env, ya, yb, raw):
    alloc, psum, sem, col = (env[k] for k in ("alloc", "psum", "sem", "col"))
    y_d, yb_d, post_d, head_ones = (env[k] for k in ("y_d", "yb_d", "post_d", "head_ones"))
    s_in, s_mean, s_cen, s_sq, s_var, s_ve, s_sqrt, s_rec, s_gn, s_aff, s_b, s_y, s_hi, s_lo, s_bin, s_pin = \
        [sem(f"b_{n}") for n in ("y_landed", "means", "centred", "squared", "variances", "variances_copied", "std",
                                 "rstd", "normed", "affine", "bonus_added", "y_ready", "hi", "lo", "gla_landed",
                                 "post_landed")]
    with ExitStack() as st:
        y = alloc(st, "b_y", [P, PAIRS, SEQ])
        sq = alloc(st, "b_sq", [P, PAIRS, SEQ])
        v = alloc(st, "b_var", [P, PAIRS, SEQ])
        post = alloc(st, "b_post", [P, 2 * PAIRS, SEQ])
        g = alloc(st, "b_gla", [P, PAIRS, SEQ])
        pm = [psum(st, f"pm{n}", 512) for n in range(4)]
        pv = pm
        late = LateModulation(st, env, A, "b", LATE_GLA + LATE_PRE, psum(st, "p_ada_b", 512))
        LATE_B = (6 * KT - LATE) * P // 512 - LATE_GLA - LATE_PRE

        def two(t, n):
            return t[:, 2 * n:2 * n + 2, :].rearrange("p f t -> p (f t)")

        with nc.Block() as block:

            @block.sync
            def _(sp):
                sp.dma_start(y[:], y_d).then_inc(s_in, 16)
                sp.dma_start(g[:], yb_d).then_inc(s_bin, 16)
                sp.dma_start(post[:], post_d).then_inc(s_pin, 16)
                for n in range(LATE_B):
                    late.load(sp, 8 * n, 8)
                    if n:
                        late.store(sp, n - 1)
                late.store(sp, LATE_B - 1)
                raw.prefetch(sp, *first_merge(A))
                late.finish(sp, LATE_B)

            @block.tensor
            def _(pe):
                pe.wait_ge(s_in, 16)
                for n in range(4):
                    pe.matmul(pm[n][:], head_ones[:], two(y, n), start=True, stop=True).then_inc(s_mean, 1)
                for n in range(4):
                    pe.wait_ge(s_sq, n + 1)
                    pe.matmul(pv[n][:], head_ones[:], two(sq, n), start=True, stop=True).then_inc(s_var, 1)
                late.multiply(pe, 0, 8 * LATE_B)

            @block.scalar
            def _(act):
                act.wait_ge(s_bin, 16)
                act.activation(yb[0][:], g[:], ACT.Copy).then_inc(s_hi, 1)
                for n in range(4):
                    act.wait_ge(s_cen, n + 1)
                    act.activation(two(sq, n), two(y, n), ACT.Square).then_inc(s_sq, 1)
                act.wait_ge(s_ve, 4)
                act.activation(v[:], v[:], ACT.Sqrt).then_inc(s_sqrt, 1)
                for n in range(LATE_B - 1):
                    late.copy_act(act, n)
                act.wait_ge(s_y, 1)
                act.activation(ya[0][:], y[:], ACT.Copy).then_inc(s_hi, 1)
                late.copy_act(act, LATE_B - 1)

            @block.vector
            def _(dve):
                for n in range(4):
                    dve.wait_ge(s_mean, n + 1)
                    dve.scalar_tensor_tensor(out=two(y, n), in0=pm[n][:], scalar=-1.0 / RD, in1=two(y, n),
                                             op0=ALU.mult, op1=ALU.add).then_inc(s_cen, 1)
                for n in range(4):
                    dve.wait_ge(s_var, n + 1)
                    dve.tensor_scalar(two(v, n), pv[n][:], 1.0 / RD, GN_EPS, ALU.mult, ALU.add).then_inc(s_ve, 1)
                dve.wait_ge(s_hi, 1)
                dve.tensor_tensor(yb[1][:], g[:], b32(yb[0][:]), ALU.subtract).then_inc(s_lo, 1)
                dve.wait_ge(s_sqrt, 1)
                dve.reciprocal(v[:], v[:]).then_inc(s_rec, 1)
                dve.wait_ge(s_rec, 1)
                dve.tensor_tensor(y[:], y[:], v[:], ALU.mult).then_inc(s_gn, 1)
                dve.wait_ge(s_gn, 1)
                for f in range(PAIRS):
                    dve.tensor_scalar(y[:, f, :], y[:, f, :], col("rwkv_ln_g", f), col("rwkv_ln_b", f), ALU.mult,
                                      ALU.add).then_inc(s_aff, 1)
                dve.wait_ge(s_pin, 16)
                dve.wait_ge(s_aff, PAIRS)
                dve.tensor_tensor(y[:], y[:], post[:, 0:PAIRS, :], ALU.add).then_inc(s_b, 1)
                dve.wait_ge(s_b, 1)
                dve.tensor_tensor(y[:], y[:], post[:, PAIRS:, :], ALU.mult).then_inc(s_y, 1)
                dve.wait_ge(s_hi, 2)
                dve.tensor_tensor(ya[1][:], y[:], b32(ya[0][:]), ALU.subtract).then_inc(s_lo, 1)


def weights(t):
    return t[0, :, :].rearrange("(k p) n -> p k n", p=P)


def two_banks(p):
    return p[:].rearrange("p (f t) -> p f t", f=2)[:, :, 0:SEQ]


T_MERGE, T_OUT, T_UP = 2 * D * RW // (P * TILE), D * D // (P * TILE), 2 * D * FF // (P * TILE)


def first_merge(A):
    return [weights(A[n])[:, :, 256 * g:256 * g + 256] for g in range(2) for n in ("w_rwkv_up", "w_gla_up")], (KH, 256)


def first_w_out(A):
    w = weights(A["w_out"])
    return [w[:, KH * (n % 2):KH * (n % 2 + 1), 256 * (n // 2):256 * (n // 2) + 256] for n in range(RAW)], (KH, 256)


def first_ffn_up(A):
    w = [weights(A[n]) for n in ("ffn_w_gate", "ffn_w_up")]
    return [w[n // 2][:, KH * (n % 2):KH * (n % 2 + 1), 0:256] for n in range(RAW)], (KH, 256)


def first_ffn_down(A):
    w = weights(A["ffn_w_down"])
    return [w[:, 4 * n:4 * n + 4, 0:512] for n in range(RAW)], (4, 512)


def phase_merge(nc, A, out, env, ya, yb, m, slots, raw):
    alloc, psum, sem, Ring, px = (env[k] for k in ("alloc", "psum", "sem", "Ring", "px"))
    tile_no, bodies, mm3 = env["tile_no"], env["bodies"], env["mm3"]
    s_g = [sem(f"m_gates_landed{g}") for g in range(2)]
    s_sig, s_m1, s_m, s_hi, s_lo = (sem(f"m_{n}") for n in ("sigmoid", "gated", "merged", "hi", "lo"))
    wa, wb = weights(A["w_rwkv_up"]), weights(A["w_gla_up"])
    NB = D // 512
    with ExitStack() as st:
        ring = Ring(st, "m", raw, 0, parts=(slots, None))
        gates = alloc(st, "m_gates", [P, 2, 2, 2, SEQ])
        gated = alloc(st, "m_gated", [P, 2, 2, 2, SEQ])
        stage = alloc(st, "m_stage", [P, 2, 2, SEQ])
        pp = [[psum(st, f"pm_{g}{b}", 1024) for b in range(2)] for g in range(2)]

        with nc.Block() as block:

            @block.sync
            def _(sp):
                def body(i):
                    for g in range(2):
                        for b, w in enumerate((wa, wb)):
                            ring.load(sp, w[:, :, bass.ds(i * 512 + 256 * g, 256)], 2 * g + b,
                                      tile_no(i, 4, 2 * g + b), (KH, 256))
                        if not (isinstance(i, int) and i == 0):
                            sp.wait_ge(s_m1, i * 4 + (2 * g - 2))
                        for b in range(2):
                            sp.dma_start(gates[:, g, b], px[bass.ds(i * 4 + (T_GATE + KT * b + 2 * g), 2), :, CTX:]
                                         .rearrange("f p t -> p f t")).then_inc(s_g[g], 16)
                bodies(sp, NB, body, True)
                ring.prefetch(sp, T_MERGE, *first_w_out(A))

            @block.scalar
            def _(act):
                def body(i):
                    for g in range(2):
                        for b in range(2):
                            ring.split_hi(act, 2 * g + b, tile_no(i, 4, 2 * g + b))
                        act.wait_ge(s_g[g], i * 32 + 32)
                        act.activation(gates[:, g], gates[:, g], ACT.Sigmoid).then_inc(s_sig, 1)
                        if not (isinstance(i, int) and i == 0 and g == 0):
                            hi(i * 2 + g, i * 4 + (2 * g - 2), 1 - g)

                def hi(count, at, g):
                    act.wait_ge(s_m, count)
                    act.activation(m[0][:, bass.ds(at, 2), :], stage[:, g], ACT.Copy).then_inc(s_hi, 1)
                bodies(act, NB, body, True)
                hi(2 * NB, 4 * NB - 2, 1)

            @block.gpsimd
            def _(pool):
                def body(i):
                    for n in (1, 3):
                        ring.split_lo(pool, n, tile_no(i, 4, n))
                bodies(pool, NB, body, False)

            @block.vector
            def _(dve):
                def finish(used, n, at, g):
                    dve.wait_ge(ring.used, used)
                    dve.wait_ge(s_sig, n + 1)
                    for b in range(2):
                        dve.tensor_tensor(gated[:, g, b], two_banks(pp[g][b]), gates[:, g, b], ALU.mult)\
                           .then_inc(s_m1, 1)
                    dve.wait_ge(s_m1, n * 2 + 2)
                    dve.tensor_tensor(stage[:, g], gated[:, g, 0], gated[:, g, 1], ALU.add).then_inc(s_m, 1)
                    dve.wait_ge(s_hi, n + 1)
                    dve.tensor_tensor(m[1][:, bass.ds(at, 2), :], stage[:, g], b32(m[0][:, bass.ds(at, 2), :]),
                                      ALU.subtract).then_inc(s_lo, 1)

                def body(i):
                    for g in range(2):
                        ring.split_lo(dve, 2 * g, tile_no(i, 4, 2 * g))
                        if not (isinstance(i, int) and i == 0 and g == 0):
                            finish(i * 4 + (2 * g), i * 2 + (g - 1), i * 4 + (2 * g - 2), 1 - g)
                bodies(dve, NB, body, True)
                finish(4 * NB, 2 * NB - 1, 4 * NB - 2, 1)

            @block.tensor
            def _(pe):
                def body(i):
                    for g in range(2):
                        if not (isinstance(i, int) and i == 0):
                            pe.wait_ge(s_m1, i * 4 + (2 * g - 2))
                        for b, x in enumerate((ya, yb)):
                            n = 2 * g + b
                            ring.wait_split(pe, n, tile_no(i, 4, n))
                            for f in range(2):
                                for k in range(KH):
                                    at = slice(k * 256 + f * P, k * 256 + (f + 1) * P)
                                    last = mm3(pe, pp[g][b][:, 512 * f:512 * f + SEQ], ring.hi[:, n % ring.S, at],
                                               ring.lo[:, n % ring.S, at], x[0][:, k, :], x[1][:, k, :], k == 0,
                                               k == KH - 1)
                            last.then_inc(ring.used, 1)
                bodies(pe, NB, body, True)


class Norm:
    Q = 4

    def __init__(self, st, env, tag):
        alloc, psum, sem = (env[k] for k in ("alloc", "psum", "sem"))
        self.ones = env["ones"]
        self.sq = alloc(st, f"{tag}_sq", [P, self.Q, SEQ])
        self.acc = alloc(st, f"{tag}_acc", [P, self.Q, SEQ])
        self.rstd = alloc(st, f"{tag}_rstd", [P, SEQ])
        self.ps = psum(st, f"{tag}_ps", 512)
        self.s_sq, self.s_acc, self.s_ss, self.s_ms, self.s_std, self.s_rstd = \
            [sem(f"{tag}_{n}") for n in ("squared", "added_up", "square_sums", "mean", "std", "rstd")]

    def square(self, act, x, q):
        act.wait_ge(self.s_acc, q + 1)
        act.activation(self.sq[:], x, ACT.Square).then_inc(self.s_sq, 1)

    def start(self, eng):
        eng.memset(self.acc[:], 0.0).then_inc(self.s_acc, 1)

    def add(self, eng, q):
        eng.wait_ge(self.s_sq, q + 1)
        eng.wait_ge(self.s_acc, q + 1)
        eng.tensor_tensor(self.acc[:], self.acc[:], self.sq[:], ALU.add).then_inc(self.s_acc, 1)

    def pe(self, pe):
        pe.wait_ge(self.s_acc, KT // self.Q + 1)
        for k in range(self.Q):
            last = pe.matmul(self.ps[:, 0:SEQ], self.ones[:], self.acc[:, k, :], start=k == 0, stop=k == self.Q - 1)
        last.then_inc(self.s_ss, 1)

    def std(self, act):
        act.wait_ge(self.s_ms, 1)
        act.activation(self.rstd[:], self.rstd[:], ACT.Sqrt).then_inc(self.s_std, 1)

    def dve(self, dve):
        dve.wait_ge(self.s_ss, 1)
        dve.tensor_scalar(self.rstd[:], self.ps[:, 0:SEQ], 1.0 / D, NORM_EPS, ALU.mult, ALU.add).then_inc(self.s_ms, 1)
        dve.wait_ge(self.s_std, 1)
        dve.reciprocal(self.rstd[:], self.rstd[:]).then_inc(self.s_rstd, 1)
        dve.wait_ge(self.s_rstd, 1)


def phase_w_out(nc, A, out, env, m, h2, slots, raw):
    alloc, psum, sem, Ring, col = (env[k] for k in ("alloc", "psum", "sem", "Ring", "col"))
    tile_no, bodies, mm3, modv, xfm_d, x1_d = (env[k] for k in ("tile_no", "bodies", "mm3", "modv", "xfm_d", "x1_d"))
    s_late, s_late_t, s_x, s_evac, s_v, s_mo, s_x1, s_h, s_hi, s_lo, s_st = (sem(f"o_{n}") for n in (
        "modulation_landed", "modulation_transposed", "x_landed", "copied", "vector_step", "normed", "x1_ready", "h_ready",
        "h_hi", "h_lo", "x1_stored"))
    w = weights(A["w_out"])
    NB = D // 512
    NQ = KT // Norm.Q
    with ExitStack() as st:
        ring = Ring(st, "o", raw, T_MERGE, parts=(slots, None))
        x = alloc(st, "o_x", [P, KT, SEQ])
        mo = alloc(st, "mo", [P, KT, SEQ])
        gain = alloc(st, "o_gain", [P, KT])
        n1, n2 = Norm(st, env, "on1"), Norm(st, env, "on2")
        pp = [psum(st, f"po_{g}", 1024) for g in range(2)]
        n_late = 6 * KT - LATE
        late_rows = alloc(st, "late_rows", [n_late, P])
        p_late = psum(st, "p_late", 512)

        with nc.Block() as block:

            @block.sync
            def _(sp):
                def body(i):
                    for n in range(4):
                        ring.load(sp, w[:, KH * (n % 2):KH * (n % 2 + 1), bass.ds(i * 512 + 256 * (n // 2), 256)], n,
                                  tile_no(i, 4, n), (KH, 256))
                bodies(sp, NB, body, True)
                sp.dma_start(late_rows[:], env["mod_d"].rearrange("a (r p) -> (a r) p", p=P)).then_inc(s_late, 16)
                sp.dma_start(x[:], xfm_d).then_inc(s_x, 16)
                ring.prefetch(sp, T_OUT, *first_ffn_up(A))
                sp.wait_ge(s_x1, NQ)
                sp.dma_start(x1_d, x[:]).then_inc(s_st, 16)
                sp.wait_ge(s_st, 16)

            @block.scalar
            def _(act):
                def body(i):
                    for n in range(4):
                        ring.split_hi(act, n, tile_no(i, 4, n))
                        if n == 2 and not (isinstance(i, int) and i == 0):
                            act.wait_ge(s_evac, i * 2)
                            n1.square(act, mo[:, bass.ds(i * 4 - 4, 4), :], i - 1)
                bodies(act, NB, body, True)
                act.wait_ge(s_evac, 2 * NB)
                n1.square(act, mo[:, KT - 4:, :], NB - 1)
                n1.std(act)
                for q in range(NQ):
                    act.wait_ge(s_x1, q + 1)
                    n2.square(act, x[:, 4 * q:4 * q + 4, :], q)
                n2.std(act)
                for k in range(KT):
                    act.wait_ge(s_h, k + 1)
                    act.activation(h2[0][:, k, :], mo[:, k, :], ACT.Identity, bias=modv[:, 3 * KT + k, 0:1])\
                       .then_inc(s_hi, 1)

            @block.gpsimd
            def _(pool):
                n1.start(pool)
                n2.start(pool)

                def body(i):
                    for n in (1, 3):
                        ring.split_lo(pool, n, tile_no(i, 4, n))
                    if not (isinstance(i, int) and i == 0):
                        n1.add(pool, i - 1)
                bodies(pool, NB, body, True)
                n1.add(pool, NB - 1)
                for q in range(NQ):
                    n2.add(pool, q)

            @block.vector
            def _(dve):
                step = [0]

                def done(ins):
                    step[0] += 1
                    ins.then_inc(s_v, 1)
                    dve.wait_ge(s_v, step[0])

                def copy(used, at, g):
                    dve.wait_ge(ring.used, used)
                    dve.tensor_copy(mo[:, bass.ds(at, 2), :], two_banks(pp[g])).then_inc(s_evac, 1)

                def body(i):
                    for g in range(2):
                        ring.split_lo(dve, 2 * g, tile_no(i, 4, 2 * g))
                        if not (isinstance(i, int) and i == 0 and g == 0):
                            copy(i * 4 + 2 * g, i * 4 + (2 * g - 2), 1 - g)
                bodies(dve, NB, body, True)
                copy(4 * NB, 4 * NB - 2, 1)
                dve.wait_ge(s_late_t, 1)
                done(dve.tensor_tensor(modv[:, LATE:, 0], p_late[:, 0:n_late], col("ada_b", LATE, n_late), ALU.add))
                done(dve.tensor_tensor(gain[:], modv[:, 2 * KT:3 * KT, 0], col("norm_post_mix", 0, KT), ALU.mult))
                n1.dve(dve)
                dve.wait_ge(s_evac, 2 * NB)
                dve.wait_ge(s_x, 16)
                for q in range(NQ):
                    for k in range(4 * q, 4 * q + 4):
                        dve.scalar_tensor_tensor(out=mo[:, k, :], in0=mo[:, k, :], scalar=gain[:, k:k + 1],
                                                 in1=n1.rstd[:], op0=ALU.mult, op1=ALU.mult).then_inc(s_mo, 1)
                    dve.wait_ge(s_mo, 4 * q + 4)
                    at = slice(4 * q, 4 * q + 4)
                    dve.tensor_tensor(x[:, at, :], x[:, at, :], mo[:, at, :], ALU.add).then_inc(s_x1, 1)
                done(dve.tensor_scalar(gain[:], modv[:, 4 * KT:5 * KT, 0], 1.0, None, ALU.add))
                done(dve.tensor_tensor(gain[:], gain[:], col("norm_pre_ffn", 0, KT), ALU.mult))
                dve.wait_ge(s_x1, NQ)
                n2.dve(dve)

                def low(k):
                    dve.wait_ge(s_hi, k + 1)
                    dve.scalar_tensor_tensor(out=h2[1][:, k, :], in0=mo[:, k, :], scalar=modv[:, 3 * KT + k, 0:1],
                                             in1=b32(h2[0][:, k, :]), op0=ALU.add, op1=ALU.subtract).then_inc(s_lo, 1)
                for k in range(KT):
                    dve.scalar_tensor_tensor(out=mo[:, k, :], in0=x[:, k, :], scalar=gain[:, k:k + 1],
                                             in1=n2.rstd[:], op0=ALU.mult, op1=ALU.mult).then_inc(s_h, 1)
                    if k >= 2:
                        low(k - 2)
                low(KT - 2)
                low(KT - 1)

            @block.tensor
            def _(pe):
                def body(i):
                    for g in range(2):
                        if not (isinstance(i, int) and i == 0):
                            pe.wait_ge(s_evac, i * 2 + (g - 1))
                        for q in range(2):
                            n = 2 * g + q
                            ring.wait_split(pe, n, tile_no(i, 4, n))
                            for f in range(2):
                                for k in range(KH):
                                    at = slice(k * 256 + f * P, k * 256 + (f + 1) * P)
                                    kk = KH * q + k
                                    last = mm3(pe, pp[g][:, 512 * f:512 * f + SEQ], ring.hi[:, n % ring.S, at],
                                               ring.lo[:, n % ring.S, at], m[0][:, kk, :], m[1][:, kk, :], kk == 0,
                                               kk == KT - 1)
                            last.then_inc(ring.used, 1)
                bodies(pe, NB, body, True)
                pe.wait_ge(s_late, 16)
                pe.transpose(p_late[:, 0:n_late], late_rows[:], env["ident"][0:n_late, 0:n_late]).then_inc(s_late_t, 1)
                n1.pe(pe)
                n2.pe(pe)


def phase_ffn_up(nc, A, out, env, h2, hid, raw):
    alloc, psum, sem, Ring = (env[k] for k in ("alloc", "psum", "sem", "Ring"))
    tile_no, bodies, mm3 = env["tile_no"], env["bodies"], env["mm3"]
    s_sig, s_a, s_b, s_hi, s_lo = (sem(f"f_{n}") for n in ("sigmoid", "silu", "hidden", "hi", "lo"))
    wg, wu = weights(A["ffn_w_gate"]), weights(A["ffn_w_up"])
    NB = FF // 512
    with ExitStack() as st:
        ring = Ring(st, "f", raw, T_MERGE + T_OUT, split=2)
        sig = alloc(st, "f_sig", [P, 2, SEQ])
        stage = alloc(st, "f_stage", [P, 2, SEQ])
        pp = [[psum(st, f"pf_{g}{b}", 1024) for b in range(2)] for g in range(2)]

        with nc.Block() as block:

            @block.sync
            def _(sp):
                def body(i):
                    for n in range(8):
                        w = (wg, wu)[n // 2 % 2]
                        ring.load(sp, w[:, KH * (n % 2):KH * (n % 2 + 1), bass.ds(i * 512 + 256 * (n // 4), 256)], n,
                                  tile_no(i, 8, n), (KH, 256))
                bodies(sp, NB, body, True)
                ring.prefetch(sp, T_UP, *first_ffn_down(A))

            @block.scalar
            def _(act):
                def gate(n, g):
                    act.wait_ge(ring.used, n * 4 + 2)
                    if not isinstance(n, int) or n:
                        act.wait_ge(s_a, n)
                    act.activation(sig[:], two_banks(pp[g][0]), ACT.Sigmoid).then_inc(s_sig, 1)

                def hi(n, at):
                    act.wait_ge(s_b, n + 1)
                    act.activation(hid[0][:, bass.ds(at, 2), :], stage[:], ACT.Copy).then_inc(s_hi, 1)

                def body(i):
                    for g in range(2):
                        first = isinstance(i, int) and i == 0 and g == 0
                        for n in range(4 * g, 4 * g + 4):
                            ring.split_hi(act, n, tile_no(i, 8, n))
                            if n % 4 == 1 and not first:
                                hi(i * 2 + (g - 1), i * 4 + (2 * g - 2))
                        gate(i * 2 + g, g)
                bodies(act, NB, body, True)
                hi(2 * NB - 1, 4 * NB - 2)

            @block.vector
            def _(dve):
                def finish(n, at, g):
                    dve.wait_ge(s_sig, n + 1)
                    if not isinstance(n, int) or n:
                        dve.wait_ge(s_lo, n)
                    dve.tensor_tensor(stage[:], two_banks(pp[g][0]), sig[:], ALU.mult).then_inc(s_a, 1)
                    dve.wait_ge(s_a, n + 1)
                    dve.wait_ge(ring.used, n * 4 + 4)
                    dve.tensor_tensor(stage[:], stage[:], two_banks(pp[g][1]), ALU.mult).then_inc(s_b, 1)

                def low(n, at):
                    dve.wait_ge(s_hi, n + 1)
                    dve.tensor_tensor(hid[1][:, bass.ds(at, 2), :], stage[:], b32(hid[0][:, bass.ds(at, 2), :]),
                                      ALU.subtract).then_inc(s_lo, 1)

                def body(i):
                    for g in range(2):
                        first = isinstance(i, int) and i == 0 and g == 0
                        for n in range(4 * g, 4 * g + 4):
                            ring.split_lo(dve, n, tile_no(i, 8, n))
                            if n % 4 == 0 and not first:
                                finish(i * 2 + (g - 1), i * 4 + (2 * g - 2), 1 - g)
                            if n % 4 == 2 and not first:
                                low(i * 2 + (g - 1), i * 4 + (2 * g - 2))
                bodies(dve, NB, body, True)
                finish(2 * NB - 1, 4 * NB - 2, 1)
                low(2 * NB - 1, 4 * NB - 2)

            @block.tensor
            def _(pe):
                def body(i):
                    for g in range(2):
                        if not (isinstance(i, int) and i == 0):
                            pe.wait_ge(s_b, i * 2 + (g - 1))
                        for b in range(2):
                            for q in range(2):
                                n = 4 * g + 2 * b + q
                                ring.wait_split(pe, n, tile_no(i, 8, n))
                                for f in range(2):
                                    for k in range(KH):
                                        at = slice(k * 256 + f * P, k * 256 + (f + 1) * P)
                                        kk = KH * q + k
                                        last = mm3(pe, pp[g][b][:, 512 * f:512 * f + SEQ], ring.hi[:, n % ring.S, at],
                                                   ring.lo[:, n % ring.S, at], h2[0][:, kk, :], h2[1][:, kk, :],
                                                   kk == 0, kk == KT - 1)
                                last.then_inc(ring.used, 1)
                bodies(pe, NB, body, True)


def phase_ffn_down(nc, A, out, env, hid, slots, raw):
    alloc, psum, sem, Ring = (env[k] for k in ("alloc", "psum", "sem", "Ring"))
    mm3, yo_d = env["mm3"], env["yo_d"]
    s_evac, s_st = sem("d_copied"), sem("d_stored")
    w = weights(A["ffn_w_down"])
    KQ, CW = 4, 512
    PER = FF // P // KQ
    N = D // CW * PER
    with ExitStack() as st:
        ring = Ring(st, "d", raw, T_MERGE + T_OUT + T_UP, parts=(slots, None))
        yo = alloc(st, "yo", [P, KT, SEQ])
        pp = [[psum(st, f"pd_{g}{f}", 512) for f in range(4)] for g in range(2)]

        with nc.Block() as block:

            @block.sync
            def _(sp):
                def store(g):
                    sp.wait_ge(s_evac, g + 1)
                    sp.dma_start(yo_d[:, 4 * g:4 * g + 4, :], yo[:, 4 * g:4 * g + 4, :]).then_inc(s_st, 16)
                for t in range(N):
                    g, q = t // PER, t % PER
                    ring.load(sp, w[:, KQ * q:KQ * q + KQ, g * CW:(g + 1) * CW], t, t, (KQ, CW))
                    if g and q == 7:
                        store(g - 1)
                store(D // CW - 1)
                sp.wait_ge(s_st, 16 * D // CW)

            @block.scalar
            def _(act):
                for t in range(N):
                    ring.split_hi(act, t, t)

            @block.vector
            def _(dve):
                def copy(g):
                    dve.wait_ge(ring.used, PER * (g + 1))
                    for f in range(4):
                        last = dve.tensor_copy(yo[:, 4 * g + f, :], pp[g % 2][f][:, 0:SEQ])
                    last.then_inc(s_evac, 1)
                copied = 0
                for t in range(N):
                    ring.split_lo(dve, t, t)
                    if t > PER * (copied + 1):
                        copy(copied)
                        copied += 1
                copy(copied)

            @block.tensor
            def _(pe):
                for t in range(N):
                    g, q = t // PER, t % PER
                    if q == 0 and g >= 2:
                        pe.wait_ge(s_evac, g - 1)
                    ring.wait_split(pe, t, t)
                    for f in range(4):
                        for k in range(KQ):
                            at = slice(k * CW + f * P, k * CW + (f + 1) * P)
                            kk = KQ * q + k
                            last = mm3(pe, pp[g % 2][f][:, 0:SEQ], ring.hi[:, t % ring.S, at],
                                       ring.lo[:, t % ring.S, at], hid[0][:, kk, :], hid[1][:, kk, :], kk == 0,
                                       kk == FF // P - 1)
                    last.then_inc(ring.used, 1)


def phase_final(nc, A, out, env):
    alloc, psum, sem, col = (env[k] for k in ("alloc", "psum", "sem", "col"))
    modv, x1_d, yo_d, ident = (env[k] for k in ("modv", "x1_d", "yo_d", "ident"))
    s_x, s_v, s_n, s_x2, s_t, s_tc, s_st = (sem(f"e_{n}") for n in (
        "x1_landed", "vector_step", "normed", "x2_ready", "transposed", "tokens_copied", "stored"))
    NQ = KT // Norm.Q
    s_y = [sem(f"e_y_landed{q}") for q in range(NQ)]
    with ExitStack() as st:
        yo = alloc(st, "e_yo", [P, KT, SEQ])
        x = alloc(st, "e_x", [P, KT, SEQ])
        gain = alloc(st, "e_gain", [P, KT])
        tok = alloc(st, "tok", [P, 2, D])
        n3 = Norm(st, env, "en")
        pt = [psum(st, f"pt{n}", 512) for n in range(2)]

        def quarter(q):
            return slice(4 * q, 4 * q + 4)

        with nc.Block() as block:

            @block.sync
            def _(sp):
                for q in range(NQ):
                    sp.dma_start(yo[:, quarter(q), :], yo_d[:, quarter(q), :]).then_inc(s_y[q], 16)
                sp.dma_start(x[:], x1_d).then_inc(s_x, 16)
                for n in range(2 * NQ):
                    q, b = n // 2, n % 2
                    sp.wait_ge(s_tc, n + 1)
                    sp.dma_start(out[0, b * P:(b + 1) * P, q * 512:(q + 1) * 512], tok[:, b, q * 512:(q + 1) * 512])\
                      .then_inc(s_st, 16)
                sp.wait_ge(s_st, 16 * 2 * NQ)

            @block.scalar
            def _(act):
                for q in range(NQ):
                    act.wait_ge(s_y[q], 16)
                    n3.square(act, yo[:, quarter(q), :], q)
                n3.std(act)
                for n in range(2 * NQ):
                    q, b = n // 2, n % 2
                    act.wait_ge(s_t, n + 1)
                    act.activation(tok[:, b, q * 512:(q + 1) * 512], pt[n % 2][:], ACT.Copy).then_inc(s_tc, 1)

            @block.vector
            def _(dve):
                n3.start(dve)
                dve.tensor_tensor(gain[:], modv[:, 5 * KT:6 * KT, 0], col("norm_post_ffn", 0, KT), ALU.mult)\
                   .then_inc(s_v, 1)
                for q in range(NQ):
                    n3.add(dve, q)
                dve.wait_ge(s_v, 1)
                n3.dve(dve)
                dve.wait_ge(s_x, 16)
                for q in range(NQ):
                    dve.wait_ge(s_y[q], 16)
                    for k in range(4 * q, 4 * q + 4):
                        dve.scalar_tensor_tensor(out=yo[:, k, :], in0=yo[:, k, :], scalar=gain[:, k:k + 1],
                                                 in1=n3.rstd[:], op0=ALU.mult, op1=ALU.mult).then_inc(s_n, 1)
                    dve.wait_ge(s_n, 4 * q + 4)
                    dve.tensor_tensor(x[:, quarter(q), :], x[:, quarter(q), :], yo[:, quarter(q), :], ALU.add)\
                       .then_inc(s_x2, 1)

            @block.tensor
            def _(pe):
                n3.pe(pe)
                for n in range(2 * NQ):
                    q, b = n // 2, n % 2
                    pe.wait_ge(s_x2, q + 1)
                    if n >= 2:
                        pe.wait_ge(s_tc, n - 1)
                    for f in range(4):
                        last = pe.transpose(pt[n % 2][:, f * P:(f + 1) * P], x[:, 4 * q + f, b * P:(b + 1) * P],
                                            ident[:])
                    last.then_inc(s_t, 1)


def phase_tail(nc, A, out, env):
    alloc, end_phase = env["alloc"], env["end_phase"]

    def parts(stack, name, k):
        return [alloc(stack, f"{name}_{n}", [P, k, SEQ], f32r) for n in ("hi", "lo")]
    with ExitStack() as st_h2:
        h2_pair = alloc(st_h2, "h2", [P, 2, KT, SEQ], f32r)
        h2 = [h2_pair[:, 0], h2_pair[:, 1]]
        raw = env["Raw"](st_h2, "t")
        slots = h2_pair[:].rearrange("p a k t -> p (a k t)").rearrange("p (s n) -> p s n", s=RAW)
        with ExitStack() as st_m:
            m = parts(st_m, "m", KT)
            with ExitStack() as st_y:
                ya, yb = parts(st_y, "ya", PAIRS), parts(st_y, "yb", PAIRS)
                phase_branches(nc, A, out, env, ya, yb, raw)
                end_phase()
                phase_merge(nc, A, out, env, ya, yb, m, slots, raw)
                end_phase()
            phase_w_out(nc, A, out, env, m, h2, slots, raw)
            end_phase()
        with ExitStack() as st_f:
            hid = parts(st_f, "hid", FF // P)
            phase_ffn_up(nc, A, out, env, h2, hid, raw)
            end_phase()
            phase_ffn_down(nc, A, out, env, hid, slots, raw)
            raw.close()
            end_phase()
    phase_final(nc, A, out, env)


def scan_masks():
    import numpy as np
    i, t = np.arange(P)[:, None] % C, np.arange(C)[None, :]
    m = np.zeros((P, 2, 9, C), np.float32)

    def joins(src, dst, l, back):
        src_half, dst_half = (1, 0) if back else (0, 1)
        return (src >> l + 1 == dst >> l + 1) & (src >> l & 1 == src_half) & (dst >> l & 1 == dst_half)
    for d in range(2):
        m[:, d, 0] = i > t if d else i < t
        m[:, d, 1] = i >= t if d else i <= t
        for l in range(6):
            m[:, d, 2 + l] = joins(i, t, l, d)
        m[:, d, 8] = joins(t, i, 0, d)
    bd = np.zeros((P, 2, 8, 2, C), np.float32)
    for h in range(2):
        rows = slice(64 * h, 64 * h + 64)
        bd[rows, :, 0:5, h] = m[rows, :, 3:8]
        bd[rows, :, 5, h] = 1.0
        bd[rows, :, 6, h] = m[rows, :, 2]
        bd[rows, :, 7, h] = m[rows, :, 8]
    return {"scan_masks": np.ascontiguousarray(m[:, :, 0:2]), "scan_masks_bd": bd}


def gla_masks():
    import numpy as np
    s, t = np.arange(P)[:, None], np.arange(P)[None, :]
    m = np.zeros((P, 2, 7, P), np.float32)
    for d in range(2):
        for l in range(7):
            m[:, d, l] = (s >> l + 1 == t >> l + 1) & (s >> l & 1 == d) & (t >> l & 1 == 1 - d)
    return m


def consts():
    return {**scan_masks(), "gla_masks": gla_masks()}


_INS = ["x", "c", "ctx", "c_ctx", "ada_w", "ada_b", "norm_pre_mix", "norm_post_mix", "norm_pre_ffn", "norm_post_ffn",
        "w_in", "shift_mu", "rwkv_w0", "rwkv_w2", "rwkv_a0", "rwkv_a2", "rwkv_g2", "rwkv_k_k", "rwkv_k_a", "rwkv_r_k",
        "rwkv_ln_g", "rwkv_ln_b", "w_rwkv_up", "gla_alpha_up", "gla_alpha_b", "gla_norm_g", "w_gla_up", "w_out",
        "ffn_w_gate", "ffn_w_up", "ffn_w_down"]


def kernel(**inputs):
    import numpy as np
    import concourse.bacc as bacc
    from concourse.bass_utils import run_bass_kernel_spmd

    nc = bacc.Bacc("TRN2", target_bir_lowering=False, num_devices=1)
    arrays, A = {}, {}
    for name in _INS:
        a = np.ascontiguousarray(inputs[name])
        arrays[f"in_{name}"] = a
        A[name] = nc.dram_tensor(f"in_{name}", a.shape, mybir.dt.from_np(a.dtype), kind="ExternalInput").ap()
    for name, a in consts().items():
        arrays[name] = a
        A[name] = nc.dram_tensor(name, a.shape, f32, kind="ExternalInput").ap()
    out = nc.dram_tensor("out_0", (1, SEQ, D), f32, kind="ExternalOutput").ap()
    hybrid_block(nc, A, out)
    r = run_bass_kernel_spmd(nc, [arrays], core_ids=[0])
    return r.results[0]["out_0"]
```
